# Optimizing a Trainium2 kernel written in Bass

```python
import jax, jax.numpy as jnp
from jax import lax
import numpy as np
import math

D_MODEL = 2048
BATCH = 1
SEQ = 256
DEPTH = 1

D_MIX = D_MODEL
HEAD_DIM = 128
ATT_HEADS = (D_MIX // 2) // HEAD_DIM
D_ATT = ATT_HEADS * HEAD_DIM
D_RNN = D_MIX - D_ATT
RNN_BLOCKS = 8
RNN_BLOCK = D_RNN // RNN_BLOCKS
CONV_WIDTH = 4
LRU_C = 8.0
Q_BLOCK = 128
COL_Q = 0
COL_K = COL_Q + D_ATT
COL_V = COL_K + D_ATT
COL_F = COL_V + D_ATT
COL_RX = COL_F + ATT_HEADS
COL_RG = COL_RX + D_RNN
D_IN_PROJ = COL_RG + D_RNN
N_GROUPS = 4
EXPERTS_PER_GROUP = 8
N_EXPERTS = N_GROUPS * EXPERTS_PER_GROUP
TOP_K_INNER = 2
D_EXPERT = D_MODEL // 8
D_PLE = 256
FORGET_BIAS_INIT = 2.0
EPS = 1e-6


def rms_norm(x, gain):
    x32 = x.astype(jnp.float32)
    y = x32 * lax.rsqrt(jnp.mean(x32 * x32, axis=-1, keepdims=True) + EPS)
    return (y * gain.astype(jnp.float32)).astype(x.dtype)

def forgetting_attention(q, k, v, log_f):
    b, s, h, dh = q.shape
    nb = s // Q_BLOCK
    scale = dh ** -0.5
    c = jnp.cumsum(log_f, axis=1).transpose(0, 2, 1)
    kh = k.transpose(0, 2, 1, 3)
    vh = v.transpose(0, 2, 1, 3)
    q_blocks = q.transpose(0, 2, 1, 3).reshape(b, h, nb, Q_BLOCK, dh).transpose(2, 0, 1, 3, 4)
    c_blocks = c.reshape(b, h, nb, Q_BLOCK).transpose(2, 0, 1, 3)
    k_pos = jnp.arange(s, dtype=jnp.int32)
    starts = jnp.arange(nb, dtype=jnp.int32) * Q_BLOCK

    def one_block(args):
        qb, cb, start = args
        logits = jnp.einsum('bhqd,bhkd->bhqk', qb, kh,
                            preferred_element_type=jnp.float32) * scale
        logits = logits + cb[..., :, None] - c[:, :, None, :]
        q_pos = start + jnp.arange(Q_BLOCK, dtype=jnp.int32)
        causal = k_pos[None, :] <= q_pos[:, None]
        logits = jnp.where(causal, logits, -jnp.inf)
        probs = jax.nn.softmax(logits, axis=-1)
        return jnp.einsum('bhqk,bhkd->bhqd', probs.astype(vh.dtype), vh)

    out = lax.map(one_block, (q_blocks, c_blocks, starts))
    return out.transpose(1, 0, 3, 2, 4).reshape(b, s, h * dh)

def causal_depthwise_conv(x, w, bias):
    y = lax.conv_general_dilated(
        x, w[:, None, :].astype(x.dtype), window_strides=(1,),
        padding=[(CONV_WIDTH - 1, 0)],
        dimension_numbers=('NWC', 'WIO', 'NWC'),
        feature_group_count=x.shape[-1])
    return y + bias

def rg_lru(x, w_a, b_a, w_i, b_i, lam):
    b, s, d = x.shape
    xb = x.reshape(b, s, RNN_BLOCKS, RNN_BLOCK)
    r = jax.nn.sigmoid(jnp.einsum('bsni,nij->bsnj', xb, w_a).reshape(b, s, d) + b_a)
    i = jax.nn.sigmoid(jnp.einsum('bsni,nij->bsnj', xb, w_i).reshape(b, s, d) + b_i)
    log_a = -LRU_C * r.astype(jnp.float32) * jax.nn.softplus(-lam.astype(jnp.float32))
    a = jnp.exp(log_a)
    u = jnp.sqrt(-jnp.expm1(2.0 * log_a)) * (i * x).astype(jnp.float32)

    def combine(left, right):
        a1, b1 = left
        a2, b2 = right
        return a1 * a2, a2 * b1 + b2

    _, h = lax.associative_scan(combine, (a, u), axis=1)
    return h.astype(x.dtype)

def hierarchical_moe(hn, w_router_group, w_router_expert, w_gate, w_up, w_down):
    b, s, d = hn.shape
    t = hn.reshape(b * s, d)
    g_probs = jax.nn.softmax(jnp.dot(t, w_router_group, preferred_element_type=jnp.float32), axis=-1)
    g_w, g_idx = lax.top_k(g_probs, 1)
    e_logits = jnp.dot(t, w_router_expert, preferred_element_type=jnp.float32)
    e_logits = e_logits.reshape(-1, N_GROUPS, EXPERTS_PER_GROUP)
    e_in_group = jnp.take_along_axis(e_logits, g_idx[:, :, None], axis=1)[:, 0]
    top_l, top_i = lax.top_k(e_in_group, TOP_K_INNER)
    weights = jax.nn.softmax(top_l, axis=-1) * g_w
    ids = g_idx * EXPERTS_PER_GROUP + top_i
    comb = jnp.sum(jax.nn.one_hot(ids, N_EXPERTS, dtype=jnp.float32) * weights[..., None], axis=1)
    out = jnp.zeros((b * s, d), jnp.float32)
    for e in range(N_EXPERTS):
        hid = jax.nn.silu(t @ w_gate[e]) * (t @ w_up[e])
        out = out + (hid @ w_down[e]).astype(jnp.float32) * comb[:, e:e + 1]
    return out.astype(hn.dtype).reshape(b, s, d)

def first_inputs(seed: int = 0) -> dict:
    key = jax.random.key(seed)
    ks = jax.random.split(key, 32)
    f32 = jnp.float32

    def nrm(k, shape, scale):
        return jax.random.normal(k, shape, f32) * scale

    def gain(k, shape):
        return 1.0 + 0.02 * jax.random.normal(k, shape, f32)

    u = jax.random.uniform(ks[12], (DEPTH, D_RNN), f32, 0.9, 0.999)
    s_lam = u ** (1.0 / LRU_C)
    lru_lambda = jnp.log(s_lam) - jnp.log1p(-s_lam)
    return {
        "x": nrm(ks[0], (BATCH, SEQ, D_MODEL), 1.0),
        "p": nrm(ks[1], (DEPTH, BATCH, SEQ, D_PLE), 1.0),
        "mix_norm": gain(ks[2], (DEPTH, D_MODEL)),
        "w_in": nrm(ks[3], (DEPTH, D_MODEL, D_IN_PROJ), D_MODEL ** -0.5),
        "b_forget": FORGET_BIAS_INIT + 0.1 * jax.random.normal(ks[4], (DEPTH, ATT_HEADS), f32),
        "q_norm": gain(ks[5], (DEPTH, HEAD_DIM)),
        "k_norm": gain(ks[6], (DEPTH, HEAD_DIM)),
        "conv_w": nrm(ks[7], (DEPTH, CONV_WIDTH, D_RNN), CONV_WIDTH ** -0.5),
        "conv_b": nrm(ks[8], (DEPTH, D_RNN), 0.02),
        "w_rec_gate": nrm(ks[9], (DEPTH, RNN_BLOCKS, RNN_BLOCK, RNN_BLOCK), RNN_BLOCK ** -0.5),
        "b_rec_gate": nrm(ks[10], (DEPTH, D_RNN), 0.02),
        "w_in_gate": nrm(ks[11], (DEPTH, RNN_BLOCKS, RNN_BLOCK, RNN_BLOCK), RNN_BLOCK ** -0.5),
        "b_in_gate": nrm(ks[13], (DEPTH, D_RNN), 0.02),
        "lru_lambda": lru_lambda,
        "w_out": nrm(ks[14], (DEPTH, D_MIX, D_MODEL), D_MIX ** -0.5),
        "ffn_norm": gain(ks[15], (DEPTH, D_MODEL)),
        "w_router_group": nrm(ks[16], (DEPTH, D_MODEL, N_GROUPS), D_MODEL ** -0.5),
        "w_router_expert": nrm(ks[17], (DEPTH, D_MODEL, N_EXPERTS), D_MODEL ** -0.5),
        "w_expert_gate": nrm(ks[18], (DEPTH, N_EXPERTS, D_MODEL, D_EXPERT), D_MODEL ** -0.5),
        "w_expert_up": nrm(ks[19], (DEPTH, N_EXPERTS, D_MODEL, D_EXPERT), D_MODEL ** -0.5),
        "w_expert_down": nrm(ks[20], (DEPTH, N_EXPERTS, D_EXPERT, D_MODEL), D_EXPERT ** -0.5),
        "ple_norm": gain(ks[21], (DEPTH, D_MODEL)),
        "w_ple_gate": nrm(ks[22], (DEPTH, D_MODEL, D_MODEL), D_MODEL ** -0.5),
        "w_ple_up": nrm(ks[23], (DEPTH, D_PLE, D_MODEL), D_PLE ** -0.5),
    }

def first_block(x, p, mix_norm, w_in, b_forget, q_norm, k_norm, conv_w, conv_b,
              w_rec_gate, b_rec_gate, w_in_gate, b_in_gate, lru_lambda, w_out,
              ffn_norm, w_router_group, w_router_expert, w_expert_gate,
              w_expert_up, w_expert_down, ple_norm, w_ple_gate, w_ple_up):
    h = x
    b, s, _ = x.shape
    for i in range(DEPTH):
        hn = rms_norm(h, mix_norm[i])
        proj = hn @ w_in[i]
        q = rms_norm(proj[..., COL_Q:COL_K].reshape(b, s, ATT_HEADS, HEAD_DIM), q_norm[i])
        k = rms_norm(proj[..., COL_K:COL_V].reshape(b, s, ATT_HEADS, HEAD_DIM), k_norm[i])
        v = proj[..., COL_V:COL_F].reshape(b, s, ATT_HEADS, HEAD_DIM)
        log_f = jax.nn.log_sigmoid((proj[..., COL_F:COL_RX] + b_forget[i]).astype(jnp.float32))
        att_out = forgetting_attention(q, k, v, log_f)

        rx = causal_depthwise_conv(proj[..., COL_RX:COL_RG], conv_w[i], conv_b[i])
        rnn = rg_lru(rx, w_rec_gate[i], b_rec_gate[i], w_in_gate[i], b_in_gate[i], lru_lambda[i])
        rnn_out = jax.nn.gelu(proj[..., COL_RG:D_IN_PROJ], approximate=True) * rnn

        h = h + jnp.concatenate([att_out, rnn_out], axis=-1) @ w_out[i]

        hn = rms_norm(h, ffn_norm[i])
        h = h + hierarchical_moe(hn, w_router_group[i], w_router_expert[i],
                                 w_expert_gate[i], w_expert_up[i], w_expert_down[i])

        gate = jax.nn.sigmoid(rms_norm(h, ple_norm[i]) @ w_ple_gate[i])
        h = h + gate * (p[i] @ w_ple_up[i])
    return h


N_HEADS_DIFF = 6
N_HEADS_MOBA = 4
N_HEADS_DIL = 6
N_SELF_HEADS = N_HEADS_DIFF + N_HEADS_MOBA + N_HEADS_DIL
W_DIFF = N_HEADS_DIFF * HEAD_DIM
W_MOBA = N_HEADS_MOBA * HEAD_DIM
W_DIL = N_HEADS_DIL * HEAD_DIM
MIX_WIDTH = W_DIFF + W_MOBA + W_DIL
DIFF_QK_DIM = HEAD_DIM // 2
MOBA_BLOCK = 256
MOBA_TOPK = 3
MOBA_Q_CHUNK = 64
DIL_PAIRS = ((128, 1), (512, 4), (2048, 16))
DIL_BLOCK = 128
N_BUCKETS = 32
REL_MAX_DIST = 2048
N_MEM = 256
N_MEM_HEADS = 4
MEM_WIDTH = N_MEM_HEADS * HEAD_DIM
D_FF = 5632
CONV_WIDTH_2 = 3
NORM_EPS = 1e-6
NEG_INF = -1e30


def rms_norm_2(x, g):
    xf = x.astype(jnp.float32)
    y = xf * lax.rsqrt(jnp.mean(xf * xf, axis=-1, keepdims=True) + NORM_EPS)
    return (y * g.astype(jnp.float32)).astype(x.dtype)

def t5_bucket(dist):
    n = jnp.maximum(dist, 0)
    max_exact = N_BUCKETS // 2
    nf = jnp.maximum(n, 1).astype(jnp.float32)
    log_ratio = jnp.log(nf / max_exact) / math.log(REL_MAX_DIST / max_exact)
    large = max_exact + (log_ratio * (N_BUCKETS - max_exact)).astype(jnp.int32)
    large = jnp.minimum(large, N_BUCKETS - 1)
    return jnp.where(n < max_exact, n, large)

def rel_bias(table, dist):
    return jnp.moveaxis(table.astype(jnp.float32)[t5_bucket(dist)], -1, 0)

def diff_attention(q, k, v, lam, sub_g, lam_init, table):
    B, S, H, _, dqk = q.shape
    nq = S // Q_BLOCK
    scale = dqk ** -0.5
    qb = q.reshape(B, nq, Q_BLOCK, H, 2, dqk).transpose(1, 0, 3, 4, 2, 5)
    kt = k.transpose(0, 2, 3, 1, 4)
    vt = v.transpose(0, 2, 1, 3)
    kpos = jnp.arange(S)

    def block(args):
        i, qi = args
        qpos = i * Q_BLOCK + jnp.arange(Q_BLOCK)
        dist = qpos[:, None] - kpos[None, :]
        s = jnp.einsum('bhcqd,bhckd->bhcqk', qi, kt).astype(jnp.float32) * scale
        s = s + rel_bias(table, dist)[None, :, None]
        s = jnp.where(dist >= 0, s, NEG_INF)
        p = jax.nn.softmax(s, axis=-1)
        a = p[:, :, 0] - lam * p[:, :, 1]
        return jnp.einsum('bhqk,bhkd->bhqd', a.astype(vt.dtype), vt)

    o = lax.map(block, (jnp.arange(nq), qb))
    o = o.transpose(1, 0, 3, 2, 4).reshape(B, S, H, -1)
    return rms_norm_2(o, sub_g) * (1.0 - lam_init)

def moba_attention(q, k, v, table):
    B, S, H, D = q.shape
    Sp = -(-S // MOBA_BLOCK) * MOBA_BLOCK
    nb = Sp // MOBA_BLOCK
    ksel = min(MOBA_TOPK, nb)
    C = MOBA_Q_CHUNK
    nc = Sp // C
    pad = ((0, 0), (0, Sp - S), (0, 0), (0, 0))
    qt = jnp.pad(q, pad).transpose(0, 2, 1, 3)
    kt = jnp.pad(k, pad).transpose(0, 2, 1, 3)
    vt = jnp.pad(v, pad).transpose(0, 2, 1, 3)
    kb = kt.reshape(B, H, nb, MOBA_BLOCK, D)
    vb = vt.reshape(B, H, nb, MOBA_BLOCK, D)
    kmean = jnp.mean(kb.astype(jnp.float32), axis=3)
    gate = jnp.einsum('bhsd,bhnd->bhsn', qt.astype(jnp.float32), kmean)
    qblk = jnp.arange(Sp) // MOBA_BLOCK
    past = jnp.arange(nb)[None, :] < qblk[:, None]
    gate = jnp.where(past, gate, NEG_INF)
    _, sel = lax.top_k(gate, ksel)
    sel_ok = sel < qblk[:, None]
    qc = qt.reshape(B, H, nc, C, D).transpose(2, 0, 1, 3, 4)
    selc = sel.reshape(B, H, nc, C, ksel).transpose(2, 0, 1, 3, 4)
    okc = sel_ok.reshape(B, H, nc, C, ksel).transpose(2, 0, 1, 3, 4)
    scale = D ** -0.5
    tab_t = table.astype(jnp.float32).T
    bidx = jnp.arange(B)[:, None, None]
    hidx = jnp.arange(H)[None, :, None]
    koff = jnp.arange(MOBA_BLOCK)

    def chunk(args):
        i, qi, si, oki = args
        qpos = i * C + jnp.arange(C)
        own = (i * C) // MOBA_BLOCK
        flat = si.reshape(B, H, C * ksel)
        kg = kb[bidx, hidx, flat].reshape(B, H, C, ksel, MOBA_BLOCK, D)
        vg = vb[bidx, hidx, flat].reshape(B, H, C, ksel, MOBA_BLOCK, D)
        s_sel = jnp.einsum('bhqd,bhqjkd->bhqjk', qi, kg).astype(jnp.float32) * scale
        dist_sel = qpos[None, None, :, None, None] - (si[..., None] * MOBA_BLOCK + koff)
        s_sel = s_sel + tab_t[jnp.arange(H)[None, :, None, None, None], t5_bucket(dist_sel)]
        s_sel = jnp.where(oki[..., None], s_sel, NEG_INF)
        ko = lax.dynamic_slice_in_dim(kt, own * MOBA_BLOCK, MOBA_BLOCK, axis=2)
        vo = lax.dynamic_slice_in_dim(vt, own * MOBA_BLOCK, MOBA_BLOCK, axis=2)
        dist_own = qpos[:, None] - (own * MOBA_BLOCK + koff)[None, :]
        s_own = jnp.einsum('bhqd,bhkd->bhqk', qi, ko).astype(jnp.float32) * scale
        s_own = s_own + rel_bias(table, dist_own)[None]
        s_own = jnp.where(dist_own >= 0, s_own, NEG_INF)
        s = jnp.concatenate([s_sel.reshape(B, H, C, ksel * MOBA_BLOCK), s_own], axis=-1)
        p = jax.nn.softmax(s, axis=-1).astype(vt.dtype)
        p_sel = p[..., :ksel * MOBA_BLOCK].reshape(B, H, C, ksel, MOBA_BLOCK)
        p_own = p[..., ksel * MOBA_BLOCK:]
        return (jnp.einsum('bhqjk,bhqjkd->bhqd', p_sel, vg)
                + jnp.einsum('bhqk,bhkd->bhqd', p_own, vo))

    o = lax.map(chunk, (jnp.arange(nc), qc, selc, okc))
    o = o.transpose(1, 0, 3, 2, 4).reshape(B, Sp, H, D)
    return o[:, :S]

def dilated_branch(q, k, v, table, window, dil):
    B, H, S, D = q.shape
    L = S // dil
    steps = window // dil
    nb = -(-L // DIL_BLOCK)
    Lp = nb * DIL_BLOCK

    def sub(t):
        return t.reshape(B, H, L, dil, D).transpose(0, 1, 3, 2, 4)

    def windowed(t):
        tp = jnp.pad(sub(t), ((0, 0), (0, 0), (0, 0), (DIL_BLOCK, Lp - L), (0, 0)))
        tp = tp.reshape(B, H, dil, nb + 1, DIL_BLOCK, D)
        return jnp.concatenate([tp[:, :, :, :-1], tp[:, :, :, 1:]], axis=4)

    qs = jnp.pad(sub(q), ((0, 0), (0, 0), (0, 0), (0, Lp - L), (0, 0))).reshape(B, H, dil, nb, DIL_BLOCK, D)
    kw = windowed(k)
    vw = windowed(v)
    qi = jnp.arange(DIL_BLOCK)
    ki = jnp.arange(2 * DIL_BLOCK) - DIL_BLOCK
    j = qi[:, None] - ki[None, :]
    kidx = jnp.arange(nb)[:, None, None] * DIL_BLOCK + ki[None, None, :]
    valid = (j >= 0) & (j <= steps) & (kidx >= 0)
    s = jnp.einsum('bhrnqd,bhrnkd->bhrnqk', qs, kw).astype(jnp.float32) * D ** -0.5
    s = s + rel_bias(table, j * dil)[None, :, None, None]
    s = jnp.where(valid, s, NEG_INF)
    lse = jax.nn.logsumexp(s, axis=-1)
    p = jnp.exp(s - lse[..., None]).astype(v.dtype)
    o = jnp.einsum('bhrnqk,bhrnkd->bhrnqd', p, vw)
    o = o.reshape(B, H, dil, Lp, D)[:, :, :, :L].transpose(0, 1, 3, 2, 4).reshape(B, H, S, D)
    lse = lse.reshape(B, H, dil, Lp)[:, :, :, :L].transpose(0, 1, 3, 2).reshape(B, H, S)
    return o, lse

def dilated_attention(q, k, v, table):
    qt, kt, vt = (t.transpose(0, 2, 1, 3) for t in (q, k, v))
    outs, lses = [], []
    for window, dil in DIL_PAIRS:
        o, lse = dilated_branch(qt, kt, vt, table, window, dil)
        outs.append(o)
        lses.append(lse)
    wts = jax.nn.softmax(jnp.stack(lses), axis=0)
    o = jnp.sum(wts[..., None] * jnp.stack(outs).astype(jnp.float32), axis=0)
    return o.astype(q.dtype).transpose(0, 2, 1, 3)

def memory_cross_attention(h, mem_n, w_q, w_kv, w_o):
    B, S, _ = h.shape
    q = (h @ w_q).reshape(B, S, N_MEM_HEADS, HEAD_DIM)
    kv = (mem_n @ w_kv).reshape(B, -1, 2, N_MEM_HEADS, HEAD_DIM)
    k, v = kv[:, :, 0], kv[:, :, 1]
    s = jnp.einsum('bshd,bmhd->bhsm', q, k).astype(jnp.float32) * HEAD_DIM ** -0.5
    p = jax.nn.softmax(s, axis=-1).astype(v.dtype)
    o = jnp.einsum('bhsm,bmhd->bshd', p, v).reshape(B, S, MEM_WIDTH)
    return o @ w_o

def conv_glu_ffn(h, w_up, conv_w, conv_b, w_down):
    gu = h @ w_up
    g, u = jnp.split(gu, 2, axis=-1)
    g = lax.conv_general_dilated(
        g, conv_w[:, None, :].astype(g.dtype), window_strides=(1,),
        padding=[(CONV_WIDTH_2 - 1, 0)], dimension_numbers=('NWC', 'WIO', 'NWC'),
        feature_group_count=D_FF) + conv_b
    return (jax.nn.silu(g) * u) @ w_down

def second_inputs(seed: int = 0) -> dict:
    key = jax.random.key(seed)
    ks = jax.random.split(key, 19)
    f32 = jnp.float32

    def w(k, shape, fan_in):
        return jax.random.normal(k, shape, f32) * fan_in ** -0.5

    def gain(k, shape):
        return 1.0 + 0.02 * jax.random.normal(k, shape, f32)

    return {
        'x': jax.random.normal(ks[0], (BATCH, SEQ, D_MODEL), f32),
        'mem': jax.random.normal(ks[1], (BATCH, N_MEM, D_MODEL), f32),
        'w_in': w(ks[2], (DEPTH, D_MODEL, 3 * MIX_WIDTH), D_MODEL),
        'w_out': w(ks[3], (DEPTH, MIX_WIDTH, D_MODEL), MIX_WIDTH),
        'g_mix': gain(ks[4], (DEPTH, D_MODEL)),
        'diff_lambda': 0.1 * jax.random.normal(ks[5], (DEPTH, 4, DIFF_QK_DIM), f32),
        'diff_subln': gain(ks[6], (DEPTH, HEAD_DIM)),
        'rel_bias_table': 0.3 * jax.random.normal(ks[7], (N_BUCKETS, N_SELF_HEADS), f32),
        'g_cross': gain(ks[8], (DEPTH, D_MODEL)),
        'g_mem': gain(ks[9], (DEPTH, D_MODEL)),
        'w_cq': w(ks[10], (DEPTH, D_MODEL, MEM_WIDTH), D_MODEL),
        'w_ckv': w(ks[11], (DEPTH, D_MODEL, 2 * MEM_WIDTH), D_MODEL),
        'w_co': w(ks[12], (DEPTH, MEM_WIDTH, D_MODEL), MEM_WIDTH),
        'g_ffn': gain(ks[13], (DEPTH, D_MODEL)),
        'w_up': w(ks[14], (DEPTH, D_MODEL, 2 * D_FF), D_MODEL),
        'conv_w': w(ks[15], (DEPTH, CONV_WIDTH_2, D_FF), CONV_WIDTH_2),
        'conv_b': 0.01 * jax.random.normal(ks[16], (DEPTH, D_FF), f32),
        'w_down': w(ks[17], (DEPTH, D_FF, D_MODEL), D_FF),
        'g_final': gain(ks[18], (D_MODEL,)),
    }

def second_block(x, mem, w_in, w_out, g_mix, diff_lambda, diff_subln, rel_bias_table,
              g_cross, g_mem, w_cq, w_ckv, w_co, g_ffn, w_up, conv_w, conv_b, w_down, g_final):
    B, S, _ = x.shape
    tab_a = rel_bias_table[:, :N_HEADS_DIFF]
    tab_b = rel_bias_table[:, N_HEADS_DIFF:N_HEADS_DIFF + N_HEADS_MOBA]
    tab_c = rel_bias_table[:, N_HEADS_DIFF + N_HEADS_MOBA:]
    widths = (W_DIFF,) * 3 + (W_MOBA,) * 3 + (W_DIL,) * 3
    cuts = [int(c) for c in np.cumsum(widths)[:-1]]
    for l in range(DEPTH):
        h = rms_norm_2(x, g_mix[l])
        qa, ka, va, qb, kb, vb, qc, kc, vc = jnp.split(h @ w_in[l], cuts, axis=-1)
        lam_init = 0.8 - 0.6 * math.exp(-0.3 * l)
        lp = diff_lambda[l].astype(jnp.float32)
        lam = jnp.exp(jnp.sum(lp[0] * lp[1])) - jnp.exp(jnp.sum(lp[2] * lp[3])) + lam_init
        o_a = diff_attention(qa.reshape(B, S, N_HEADS_DIFF, 2, DIFF_QK_DIM),
                             ka.reshape(B, S, N_HEADS_DIFF, 2, DIFF_QK_DIM),
                             va.reshape(B, S, N_HEADS_DIFF, HEAD_DIM),
                             lam, diff_subln[l], lam_init, tab_a)
        o_b = moba_attention(qb.reshape(B, S, N_HEADS_MOBA, HEAD_DIM),
                             kb.reshape(B, S, N_HEADS_MOBA, HEAD_DIM),
                             vb.reshape(B, S, N_HEADS_MOBA, HEAD_DIM), tab_b)
        o_c = dilated_attention(qc.reshape(B, S, N_HEADS_DIL, HEAD_DIM),
                                kc.reshape(B, S, N_HEADS_DIL, HEAD_DIM),
                                vc.reshape(B, S, N_HEADS_DIL, HEAD_DIM), tab_c)
        mixed = jnp.concatenate([o_a.reshape(B, S, W_DIFF), o_b.reshape(B, S, W_MOBA),
                                 o_c.reshape(B, S, W_DIL)], axis=-1)
        x = x + mixed @ w_out[l]
        x = x + memory_cross_attention(rms_norm_2(x, g_cross[l]), rms_norm_2(mem, g_mem[l]),
                                       w_cq[l], w_ckv[l], w_co[l])
        x = x + conv_glu_ffn(rms_norm_2(x, g_ffn[l]), w_up[l], conv_w[l], conv_b[l], w_down[l])
    return rms_norm_2(x, g_final)


def setup_inputs(seed=0):
    out = dict(first_inputs(seed))
    for name, value in second_inputs(seed + 1).items():
        if name != "x":
            out[name + "_2"] = value
    return out


def reference(
    x, p, mix_norm, w_in, b_forget, q_norm, k_norm, conv_w, conv_b, w_rec_gate, b_rec_gate,
    w_in_gate, b_in_gate, lru_lambda, w_out, ffn_norm, w_router_group, w_router_expert,
    w_expert_gate, w_expert_up, w_expert_down, ple_norm, w_ple_gate, w_ple_up, mem_2, w_in_2,
    w_out_2, g_mix_2, diff_lambda_2, diff_subln_2, rel_bias_table_2, g_cross_2, g_mem_2, w_cq_2,
    w_ckv_2, w_co_2, g_ffn_2, w_up_2, conv_w_2, conv_b_2, w_down_2, g_final_2,
):
    x = first_block(
        x, p, mix_norm, w_in, b_forget, q_norm, k_norm, conv_w, conv_b, w_rec_gate, b_rec_gate,
        w_in_gate, b_in_gate, lru_lambda, w_out, ffn_norm, w_router_group, w_router_expert,
        w_expert_gate, w_expert_up, w_expert_down, ple_norm, w_ple_gate, w_ple_up,
    )
    return second_block(
        x, mem_2, w_in_2, w_out_2, g_mix_2, diff_lambda_2, diff_subln_2, rel_bias_table_2,
        g_cross_2, g_mem_2, w_cq_2, w_ckv_2, w_co_2, g_ffn_2, w_up_2, conv_w_2, conv_b_2,
        w_down_2, g_final_2,
    )


_drawn_inputs = setup_inputs


def setup_inputs(seed=0):
    import zlib

    import numpy as np

    out = dict(_drawn_inputs(seed))
    spreads = {}
    factors = {'mix_norm': 3.053,
     'q_norm': 5.334,
     'k_norm': 5.74,
     'b_rec_gate': 8.0,
     'b_in_gate': 8.0,
     'ple_norm': 8.0,
     'g_mix_2': 3.879,
     'diff_lambda_2': 5.557,
     'diff_subln_2': 6.719,
     'g_cross_2': 8.0,
     'g_mem_2': 8.0,
     'g_ffn_2': 4.649,
     'conv_b_2': 31.081,
     'g_final_2': 7.756}
    for name, (base, spread) in spreads.items():
        noise = np.random.default_rng([zlib.crc32(name.encode()), seed]).standard_normal(out[name].shape)
        drawn = base * np.exp(spread * noise) if base else spread * noise
        out[name] = __import__('jax').numpy.asarray(drawn.astype(out[name].dtype))
    for name, factor in factors.items():
        out[name] = (out[name] * factor).astype(out[name].dtype)
    return out
```

```python
import math
from contextlib import ExitStack

import numpy as np
import concourse.bass as bass
from concourse import mybir

F32 = mybir.dt.float32
F32R = mybir.dt.float32r
ALU = mybir.AluOpType
ACT = mybir.ActivationFunctionType
AX_X = mybir.AxisListType.X

P = 128
S = 256
TT = S // P
D = 2048
KT = D // P
HEADS1 = 8
RNN_T = 8
N_GROUPS, PER_GROUP = 4, 8
N_EXPERTS = N_GROUPS * PER_GROUP
D_EXPERT = 256
D_PLE = 256
N_DIFF, N_MOBA, N_DIL = 6, 4, 6
N_SELF = N_DIFF + N_MOBA + N_DIL
N_MEM_HEADS = 4
D_FF = 5632
FF_T = D_FF // P
EPS = 1e-6
NEG = -1e30
LRU_C = 8.0
COL_F = 3072
COL_RX = 3080
N_ROUTER = N_GROUPS + N_EXPERTS

CHUNK = 1024
RING = 8
AHEAD = 4
N_CHUNKS = 2 * (40 + 16 + 6 * N_EXPERTS + 2 + 16 + 48 + 16 + 8 + 4 + 4 + 88 + 44)

V_GAIN = 0
V_CONV = 7 * KT
V_BREC, V_BIN, V_LAM = V_CONV + 5 * RNN_T, V_CONV + 6 * RNN_T, V_CONV + 7 * RNN_T
V_QN = V_CONV + 8 * RNN_T
V_KN, V_SUB, V_BF = V_QN + 1, V_QN + 2, V_QN + 3
V_CONV2 = V_QN + 4
N_VEC = V_CONV2 + 4 * FF_T

DIFF_SCALE = 64 ** -0.5
HEAD_SCALE = 128 ** -0.5


class Count:

    def __init__(self):
        self.n, self.i, self.per = 0, None, 0

    def enter(self, i, per, start=0):
        self.i, self.per, self.first, self.start = i, per, self.n, start

    def leave(self, turns):
        assert self.n - self.first == self.per, (self.n - self.first, self.per)
        self.n, self.i = self.first + turns * self.per, None

    def at(self, k=0, div=1, mul=1):
        v = (self.n + k) // div * mul
        if self.i is None:
            return v
        assert self.per % div == 0
        turn = self.per // div * mul
        return self.i * turn + (v - self.start * turn)


def program(nc, I, out):
    ctx = ExitStack()
    with ctx:
        def sb(name, shape, dt=F32):
            return ctx.enter_context(nc.sbuf_tensor(name, shape, dt))

        def sem(name):
            return ctx.enter_context(nc.semaphore(name))

        whi = sb("whi", [P, RING, CHUNK], F32R)
        h = sb("h", [P, TT, D])
        xh = sb("xh", [P, KT, S], F32R)
        xl = sb("xl", [P, KT, S], F32R)
        vec = sb("vec", [P, N_VEC])
        ident = sb("ident", [P, P])
        mean = sb("mean", [P, P])
        eps = sb("eps", [P, 1])
        lam = sb("lam", [P, 8])
        ss = sb("ss", [P, TT])
        rstd = sb("rstd", [P, TT])
        inv = sb("inv", [P, TT])
        sp8 = sb("sp8", [P, RNN_T])
        lru_t = sb("lru_t", [P, 6, RNN_T])
        qg = sb("qg", [P, 2])
        stat = sb("stat", [P, 2, 4])
        rsum = sb("rsum", [P, 2, 2])

        base = (nc.sbuf_base + 31) // 32 * 32
        size = (nc.sbuf_usable_end - base) // 32 * 32 - 64

        def at(name, kb, shape, dt=F32):
            off = int(kb * 1024)
            assert off + 4 * int(np.prod(shape[1:])) <= size, (name, off, shape, size)
            return nc.alloc_sbuf_tensor_at(name, shape, dt, offset=base + off)

        raw = at("raw", 0, [P, RING, CHUNK])
        wlo = at("wlo", 0, [P, RING, CHUNK], F32R)
        ring_size = RING * CHUNK * 4
        base, size = base + ring_size, size - ring_size

        hs = at("hs", 0, [P, TT, D])
        qk1 = at("qk1", 0, [P, 16, S])
        sq1 = at("sq1", 16, [P, 16, S])
        v1 = at("v1", 16, [P, TT, 1024])
        rxp = at("rxp", 32, [P, RNN_T, 4 + S])
        a_t = at("a_t", 32, [P, RNN_T, S])
        rxc = at("rxc", 41, [P, RNN_T, S])
        gel = at("gel", 49, [P, RNN_T, S])
        r_t = at("r_t", 57, [P, RNN_T, S])
        i_t = at("i_t", 65, [P, RNN_T, S])
        w_rec = at("w_rec", 73, [P, RNN_T, P])
        w_ing = at("w_ing", 77, [P, RNN_T, P])
        negsel = at("negsel", 81, [P, HEADS1, P])
        causal = at("causal", 85, [P, S])
        c_cum = at("c_cum", 86, [P, S])
        f_raw = at("f_raw", 87, [P, KT * 8 + 120])
        f_hi = at("f_hi", 88, [P, KT * 8 + 120], F32R)
        f_lo = at("f_lo", 89, [P, KT * 8 + 120], F32R)
        rst1 = at("rst1", 65, [P, 2, 512])
        den = at("den", 76, [P, 2, 512])
        z_f = at("z_f", 69, [8, S])
        z_n = at("z_n", 70, [8, S])
        z_y = at("z_y", 71, [8, S])
        z_z = at("z_z", 72, [8, S])
        z_q = at("z_q", 57, [8, S])
        z_s = at("z_s", 58, [8, S])
        z_1 = at("z_1", 59, [8, S])
        t1 = [at("sneg1", 57, [P, 2, 512]), at("e1", 61, [P, 2, 512]), at("pt1", 65, [P, 2, 512])]
        rt_raw = at("rt_raw", 73, [P, KT * N_ROUTER + 92])
        rt_hi = at("rt_hi", 76, [P, KT * N_ROUTER + 92], F32R)
        rt_lo = at("rt_lo", 79, [P, KT * N_ROUTER + 92], F32R)
        lgT = at("lgT", 16, [P, S])
        lg = at("lg", 17, [P, TT, N_ROUTER])
        comb = at("comb", 18, [P, TT, N_EXPERTS])
        oh1 = at("oh1", 18.5, [P, TT, N_EXPERTS])
        oh2 = at("oh2", 19, [P, TT, N_EXPERTS])
        em = at("em", 19.5, [P, TT, N_EXPERTS])
        key = at("key", 20, [P, TT, N_EXPERTS])
        desc = at("desc", 20.5, [P, TT, N_EXPERTS])
        desc4 = at("desc4", 21, [P, TT, N_GROUPS])
        g_sh = at("g_sh", 21.25, [P, TT, N_GROUPS])
        g_e = at("g_e", 21.5, [P, TT, N_GROUPS])
        g_oh = at("g_oh", 21.75, [P, TT, N_GROUPS])
        g_key = at("g_key", 22, [P, TT, N_GROUPS])
        r_s = at("r_s", 22.25, [P, 12, TT])
        sg = at("sg", 24, [P, 2, 512])
        hid = at("hid", 28, [P, 2, 512])
        hid_h = at("hid_h", 32, [P, 2, 512], F32R)
        hid_l = at("hid_l", 36, [P, 2, 512], F32R)
        upb = at("upb", 40, [P, TT, D])
        pT = at("pT", 56, [P, 2, S])
        pT_h = at("pT_h", 58, [P, 2, S], F32R)
        pT_l = at("pT_l", 60, [P, 2, S], F32R)
        gate = at("gate", 62, [P, 2, 1024])
        qk2 = at("qk2", 0, [P, 32, S])
        v2 = at("v2", 32, [P, TT, N_SELF * P])
        bias = at("bias", 48, [P, N_SELF, S])
        hank = at("hank", 64, [P, N_SELF, S])
        flip = at("flip", 88, [P, P])
        mem = at("mem", 64, [P, TT, D])
        t2 = [at("sneg2", 80, [P, 2, 512]), at("e2", 84, [P, 2, 512]), at("pt2", 88, [P, 2, 512])]
        junk_a = at("junk_a", 80, [P, D])
        junk_v = at("junk_v", 48, [P, D])
        rst2 = at("rst2", 80, [P, 2, 512])
        tab = at("tab", 16, [32, N_SELF])
        onehot = at("onehot", 17, [32, 384])
        addend = at("addend", 19, [N_SELF, 384])
        iscale = at("iscale", 21, [N_SELF, 1])
        frev = at("frev", 22, [N_SELF, 384])
        lamv = at("lamv", 24, [P, 4, 64])
        lamj = at("lamj", 25, [P, 2, 64])
        memh = at("memh", 0, [P, KT, S], F32R)
        meml = at("meml", 16, [P, KT, S], F32R)
        km = at("km", 32, [P, N_MEM_HEADS, S])
        vm = at("vm", 36, [P, TT, 512])
        qc = at("qc", 40, [P, N_MEM_HEADS, S])
        zero = at("zero", 44, [P, S])
        hs_c = at("hs_c", 48, [P, TT, D])
        FA = FF_T - 2
        ah = at("ah", 0, [P, FA, S], F32R)
        al = at("al", FA, [P, FA, S], F32R)
        gpad = at("gpad", 2 * FA, [P, 2, 2 + S])
        cv = at("cv", 2 * FA + 2.0625, [P, 2, S])
        af = at("af", 2 * FA + 4.0625, [P, 2, S])
        gfin = at("gfin", 2 * FA, [P, D])

        acc = [ctx.enter_context(nc.psum_tensor(f"acc{b}", [P, 1024], F32)) for b in range(2)]
        tp = [ctx.enter_context(nc.psum_tensor(f"tp{b}", [P, 512], F32)) for b in range(2)]
        ps = [ctx.enter_context(nc.psum_tensor(f"ps{b}", [P, 512], F32)) for b in range(2)]
        score = [acc[b][:, k * 512:(k + 1) * 512] for b in range(2) for k in range(2)]

        frev_d = nc.dram_tensor("frev_d", (N_SELF, 384), F32, kind="Internal").ap()

        raw_in = [sem(f"raw_in{r}") for r in range(RING)]
        hi_ready, lo_ready = sem("hi_ready"), sem("lo_ready")
        chunk_used = sem("chunk_used")
        acc_free = [sem(f"acc_free{b}") for b in range(2)]
        act_step, dve_step = sem("act_step"), sem("dve_step")
        x_in, vec_in, ident_in = sem("x_in"), sem("vec_in"), sem("ident_in")
        small_in, lam_in, gates_in, late_in = sem("small_in"), sem("lam_in"), sem("gates_in"), sem("late_in")
        consts = sem("consts")
        n_ss, n_inv, n_rstd = sem("n_ss"), sem("n_inv"), sem("n_rstd")
        n_hs0, n_hs1 = sem("n_hs0"), sem("n_hs1")
        n_tp, n_hi, n_lo = sem("n_tp"), sem("n_hi"), sem("n_lo")
        lam_y, lam_dot, lam_e = sem("lam_y"), sem("lam_dot"), sem("lam_e")
        f_split, f_done, f_z, f_y, f_abs, c_ready = (sem(n) for n in
                                                     ("f_split", "f_done", "f_z", "f_y", "f_abs", "c_ready"))
        conv_done, gate_mm, gate_read = sem("conv_done"), sem("gate_mm"), sem("gate_read")
        la_ready, a_ready, lru_q, lru_root, gel_ready = (sem(n) for n in
                                                         ("la_ready", "a_ready", "lru_q", "lru_root", "gel_ready"))
        sq_ready, ms_mm, ms_root, qk_ready = sem("sq_ready"), sem("ms_mm"), sem("ms_root"), sem("qk_ready")
        rnn_ready, rnn_hi, rnn_lo = sem("rnn_ready"), sem("rnn_hi"), sem("rnn_lo")
        s_mm, s_max, s_exp, p_ready = sem("s_mm"), sem("s_max"), sem("s_exp"), sem("p_ready")
        pt_mm, pt_copy, o_mm, o_hi, o_lo = sem("pt_mm"), sem("pt_copy"), sem("o_mm"), sem("o_hi"), sem("o_lo")
        o_sq = sem("o_sq")
        rt_in, rt_split, rt_mm, rt_copy, rt_tp, rt_read, rt_e = (sem(n) for n in
                                                                 ("rt_in", "rt_split", "rt_mm", "rt_copy", "rt_tp", "rt_read", "rt_e"))
        silu_ready, hid_ready, hid_hi, hid_lo = sem("silu_ready"), sem("hid_ready"), sem("hid_hi"), sem("hid_lo")
        p_in, pT_ready, gate_ready = sem("p_in"), sem("pT_ready"), sem("gate_ready")
        b_mm, b_f, b_out, b_in, b_flip, b_copy = (sem(n) for n in ("b_mm", "b_f", "b_out", "b_in", "b_flip", "b_copy"))
        mem_in, km_ready, vm_ready, qc_ready = sem("mem_in"), sem("km_ready"), sem("vm_ready"), sem("qc_ready")
        g_ready, cv_ready, sil2, af_ready, a_hi, a_lo = (sem(n) for n in
                                                         ("g_ready", "cv_ready", "sil2", "af_ready", "a_hi", "a_lo"))
        rt_pad = sem("rt_pad")
        ple_prod, conv2 = sem("ple_prod"), sem("conv2")
        gf_in, fin_ready, out_done = sem("gf_in"), sem("fin_ready"), sem("out_done")

        block = ctx.enter_context(nc.Block())

        def col(c, n=1):
            return vec[:, c:c + n]

        def rows4(w):
            return w.rearrange("(ko p) n -> p ko n", p=P)

        @block.sync
        def _(sp):
            n = Count()

            def load(pieces):
                r = n.n % RING
                if n.n >= RING:
                    sp.wait_ge(chunk_used, n.at(1 - RING))
                for dst, src in pieces(r):
                    sp.dma_start(dst, src).then_inc(raw_in[r], 16)
                n.n += 1

            def two_tiles(r):
                return raw[:, r, :].rearrange("p (k n) -> p k n", k=2)

            def k2(w, kt, cols):
                return lambda r: [(two_tiles(r)[:, j:j + 1, :], w[:, one(kt, j), cols]) for j in range(2)]

            def two(wa, ca, wb, cb, kt):
                k = slice(kt, kt + 2) if isinstance(kt, int) else bass.ds(kt, 2)
                return lambda r: [(two_tiles(r)[:, :, 0:256], wa[:, k, ca]), (two_tiles(r)[:, :, 256:512], wb[:, k, cb])]

            def one(kt, j):
                return slice(kt + j, kt + j + 1) if isinstance(kt, int) else bass.ds(kt + j, 1)

            for t in range(TT):
                sp.dma_start(h[:, t, :], I["x"][0, t * P:(t + 1) * P, :]).then_inc(x_in, 16)
            w_in = rows4(I["w_in"][0])
            for c in range(RING):
                load(k2(w_in, 2 * c, slice(COL_RX, COL_RX + 512)))
            for c0, first in ((COL_RX, 1), (0, 0)):
                with sp.Fori(first, 4) as j:
                    n.enter(j, 8, first)
                    for c in range(8):
                        load(k2(w_in, 2 * c, bass.ds(j * 512 + c0, 512)))
                    n.leave(4 - first)
            for c0 in (2048, 2560):
                for c in range(8):
                    load(k2(w_in, 2 * c, slice(c0, c0 + 512)))
            w_out = rows4(I["w_out"][0])
            with sp.Fori(0, 4) as j:
                n.enter(j, 8)
                for c in range(8):
                    load(k2(w_out, 2 * c, bass.ds(j * 512, 512)))
                n.leave(4)
            wg = I["w_expert_gate"][0].rearrange("e (ko p) n -> p (e ko) n", p=P)
            wu = I["w_expert_up"][0].rearrange("e (ko p) n -> p (e ko) n", p=P)
            wd = I["w_expert_down"][0].rearrange("e (ko p) n -> p (e ko) n", p=P)

            def gate_up(e):
                for c in range(8):
                    load(two(wg, slice(0, 256), wu, slice(0, 256), e * KT + 2 * c))

            def down(e):
                for c in range(4):
                    load(k2(wd, e * 2, slice(c * 512, c * 512 + 512)))

            gate_up(0)
            with sp.Fori(0, N_EXPERTS // 2 - 1) as i:
                n.enter(i, 24)
                gate_up(i * 2 + 1)
                down(i * 2)
                gate_up(i * 2 + 2)
                down(i * 2 + 1)
                n.leave(N_EXPERTS // 2 - 1)
            gate_up(N_EXPERTS - 1)
            down(N_EXPERTS - 2)
            down(N_EXPERTS - 1)
            w_pu = rows4(I["w_ple_up"][0])
            for c in range(4):
                load(k2(w_pu, 0, slice(c * 512, c * 512 + 512)))
            w_pg = rows4(I["w_ple_gate"][0])
            with sp.Fori(0, 4) as j:
                n.enter(j, 8)
                for c in range(8):
                    load(k2(w_pg, 2 * c, bass.ds(j * 512, 512)))
                n.leave(4)
            w_in2 = rows4(I["w_in_2"][0])
            for c0, blocks in ((0, 3), (2304, 2), (3840, 3)):
                with sp.Fori(0, blocks) as j:
                    n.enter(j, 8)
                    for c in range(8):
                        load(k2(w_in2, 2 * c, bass.ds(j * 512 + c0, 512)))
                    n.leave(blocks)
            for ca, cb in ((1536, 1792), (2048, 5376), (3328, 3584), (5632, 5888)):
                for c in range(8):
                    load(two(w_in2, slice(ca, ca + 256), w_in2, slice(cb, cb + 256), 2 * c))
            w_out2 = rows4(I["w_out_2"][0])
            with sp.Fori(0, 4) as j:
                n.enter(j, 8)
                for c in range(8):
                    load(k2(w_out2, 2 * c, bass.ds(j * 512, 512)))
                n.leave(4)
            w_ckv = rows4(I["w_ckv_2"][0])
            with sp.Fori(0, 2) as j:
                n.enter(j, 8)
                for c in range(8):
                    load(k2(w_ckv, 2 * c, bass.ds(j * 512, 512)))
                n.leave(2)
            w_cq = rows4(I["w_cq_2"][0])
            for c in range(8):
                load(k2(w_cq, 2 * c, slice(0, 512)))
            w_co = rows4(I["w_co_2"][0])
            for j in range(4):
                for c in range(2):
                    load(k2(w_co, 2 * c, slice(j * 512, j * 512 + 512)))
            w_up = rows4(I["w_up_2"][0])
            with sp.Fori(0, FF_T // 2) as j:
                n.enter(j, 8)
                for c in range(8):
                    load(two(w_up, bass.ds(j * 256, 256), w_up, bass.ds(j * 256 + D_FF, 256), 2 * c))
                n.leave(FF_T // 2)
            w_dn = rows4(I["w_down_2"][0])
            for j in range(4):
                for c in range(FF_T // 2):
                    load(k2(w_dn, 2 * c, slice(j * 512, j * 512 + 512)))
            assert n.n == N_CHUNKS
            for t in range(TT):
                sp.wait_ge(fin_ready, t + 1)
                sp.dma_start(out[0, t * P:(t + 1) * P, :], h[:, t, :]).then_inc(out_done, 16)
            sp.wait_ge(out_done, 32)

        @block.gpsimd
        def _(pool):
            pool.dma_start(vec[:, :], I["vec"]).then_inc(vec_in, 16)
            pool.dma_start(ident[:, :], I["ident"]).then_inc(ident_in, 16)
            pool.dma_start(lamv[:, :, :], I["diff_lambda_2"].broadcast_to((P, 4, 64))).then_inc(lam_in, 16)
            pool.dma_start(tab[:, :], I["rel_bias_table_2"]).then_inc(small_in, 16)
            pool.dma_start(onehot[:, :], I["onehot"]).then_inc(small_in, 16)
            pool.dma_start(addend[:, :], I["addend"]).then_inc(small_in, 16)
            pool.dma_start(iscale[:, :], I["iscale"]).then_inc(small_in, 16)
            pool.dma_start(w_rec[:, :, :], I["w_rec_gate"][0].rearrange("n i j -> i n j")).then_inc(gates_in, 16)
            pool.dma_start(w_ing[:, :, :], I["w_in_gate"][0].rearrange("n i j -> i n j")).then_inc(gates_in, 16)
            pool.wait_ge(consts, 1)
            pool.dma_start(f_raw[:, 0:KT * 8], I["w_f"]).then_inc(late_in, 16)
            pool.dma_start(negsel[:, :, :], I["negsel"]).then_inc(late_in, 16)
            pool.dma_start(causal[:, :], I["causal"]).then_inc(late_in, 16)
            pool.wait_ge(b_f, 1)
            pool.dma_start(frev_d, frev[:, :]).then_inc(b_out, 16)
            pool.wait_ge(gate_mm, RNN_T)
            pool.memset(rt_raw[:, KT * N_ROUTER:], 0.0).then_inc(rt_pad, 1)
            pool.dma_start(rt_raw[:, 0:KT * N_ROUTER], I["w_router"]).then_inc(rt_in, 16)
            pool.wait_ge(o_lo, HEADS1)
            pool.wait_ge(rnn_lo, 1)
            pool.dma_start(pT[:, :, :], I["pT"]).then_inc(p_in, 16)
            pool.dma_start(desc[:, :, :], I["desc"]).then_inc(p_in, 16)
            pool.dma_start(desc4[:, :, :], I["desc4"]).then_inc(p_in, 16)
            pool.wait_ge(b_out, 16)
            pool.wait_ge(acc_free[0], PLE_END[0])
            pool.wait_ge(acc_free[1], PLE_END[1])
            diagonals = bass.AP(tensor=frev_d.tensor, offset=0, ap=[[1, P], [384, N_SELF], [1, S]])
            pool.dma_start(hank[:, :, :], diagonals).then_inc(b_in, 16)
            pool.dma_start(flip[:, :], I["flip"]).then_inc(b_in, 16)
            pool.wait_ge(b_copy, 8)
            for t in range(TT):
                pool.dma_start(mem[:, t, :], I["mem_2"][0, t * P:(t + 1) * P, :]).then_inc(mem_in, 16)
            pool.wait_ge(af_ready, FF_T // 2)
            pool.wait_ge(a_lo, FF_T // 2)
            pool.wait_ge(a_hi, FF_T // 2)
            pool.dma_start(gfin[:, :], I["g_final_2"].rearrange("(a n) -> a n", a=1).broadcast_to((P, D))).then_inc(gf_in, 16)

        V_TILE = [0, 1, 2, 3, 4, 5] + [8, 9, 10, 11] + [6, 7, 12, 13, 14, 15]
        comps2 = [2] * N_DIFF + [1] * (N_MOBA + N_DIL)
        M1 = HEADS1
        M2 = sum(comps2)

        def operands2(u, c):
            if u < N_DIFF:
                part = slice(64 * c, 64 * c + 64)
                return qk2[part, u, :], qk2[part, N_DIFF + u, :]
            if u < N_DIFF + N_MOBA:
                return qk2[:, 12 + u - N_DIFF, :], qk2[:, 16 + u - N_DIFF, :]
            v = u - N_DIFF - N_MOBA
            return qk2[:, 20 + v, :], qk2[:, 26 + v, :]

        AT = [dict(units=HEADS1, comps=[1] * HEADS1, causal=True, m0=0, u0=0, t=t1),
              dict(units=N_SELF, comps=comps2, causal=True, m0=M1, u0=HEADS1, t=t2),
              dict(units=N_MEM_HEADS, comps=[1] * N_MEM_HEADS, causal=False, m0=M1 + M2, u0=HEADS1 + N_SELF, t=t2)]

        def spans(at_):
            if at_["causal"]:
                return [(0, P, P), (P, P + S, 0)]
            return [(0, S, 0), (S, 2 * S, 0)]

        def prob_tiles(A):
            if A["causal"]:
                return [(0, P, 0), (P, 2 * P, 0), (2 * P, 3 * P, 0)]
            return [(0, P, 0), (S, S + P, 0), (P, S, 0), (S + P, 2 * S, 0)]

        @block.tensor
        def _(pe):
            n, bl = Count(), Count()
            norms = Count()

            def three(o, wh, wl, ah_, al_, first, last, weights_stationary):
                pairs = ((wh, ah_), (wh, al_), (wl, ah_))
                if not weights_stationary:
                    pairs = ((wh, ah_), (wl, ah_), (wh, al_))
                for j, (w, a) in enumerate(pairs):
                    lhsT, rhs = (w, a) if weights_stationary else (a, w)
                    mm = pe.matmul(o, lhsT, rhs, start=first and j == 0, stop=last and j == 2, skip_group_check=True)
                return mm

            def take():
                b = bl.n % 2
                if bl.i is not None or bl.n >= 2:
                    pe.wait_ge(acc_free[b], bl.at(0, 2))
                bl.n += 1
                return acc[b]

            def chunk():
                pe.wait_ge(lo_ready, n.at(1))
                s = n.n % RING
                n.n += 1
                return tuple(w[:, s, :].rearrange("p (k n) -> p k n", k=2) for w in (whi, wlo))

            def features(ah_, al_):
                o = take()
                for c in range(KT // 2):
                    wh, wl = chunk()
                    for k in range(2):
                        for ct in range(4):
                            w = slice(ct * P, ct * P + P)
                            mm = three(o[:, ct * S:(ct + 1) * S], wh[:, k, w], wl[:, k, w], ah_[:, 2 * c + k, :],
                                       al_[:, 2 * c + k, :], c == 0 and k == 0 and ct % 2 == 0, c == KT // 2 - 1 and k == 1, True)
                    mm.then_inc(chunk_used, 1)

            def tokens(operand, chunks=KT // 2):
                o = take()
                for c in range(chunks):
                    wh, wl = chunk()
                    for k in range(2):
                        xh_, xl_ = operand(2 * c + k)
                        for t in range(TT):
                            q = slice(t * P, t * P + P)
                            mm = three(o[:, t * 512:(t + 1) * 512], wh[:, k, :], wl[:, k, :], xh_[:, q], xl_[:, q],
                                       c == 0 and k == 0, c == chunks - 1 and k == 1, False)
                    mm.then_inc(chunk_used, 1)

            def current(k):
                return xh[:, k, :], xl[:, k, :]

            def norm(src):
                k = norms.n
                norms.n += 1
                if k == 0:
                    pe.wait_ge(ident_in, 16)
                pe.wait_ge(n_hs0, k + 1)
                pe.wait_ge(n_hs1, k + 1)
                for g in range(KT // 2):
                    if 8 * k + g >= 2:
                        pe.wait_ge(n_lo, 8 * k + g - 1)
                    for j in range(2):
                        for t in range(TT):
                            kt = 2 * g + j
                            mm = pe.transpose(tp[g % 2][:, j * S + t * P:j * S + t * P + P],
                                              src[:, t, kt * P:kt * P + P], ident[:, :])
                    mm.then_inc(n_tp, 1)

            def normed(k):
                pe.wait_ge(n_lo, 8 * (k + 1))

            def attend(a, operands, values, scores_extra=None):
                A = AT[a]
                comps, N = A["comps"], A["units"]
                first = [sum(comps[:u]) for u in range(N)]
                for s in range(N + 2):
                    if s < N:
                        for c in range(comps[s]):
                            m = A["m0"] + first[s] + c
                            if m >= 4:
                                pe.wait_ge(s_max, m - 3)
                            q, k = operands(s, c)
                            o = score[m % 4]
                            for t, (c0, c1, _) in enumerate(spans(A)):
                                w = c1 - c0
                                mm = pe.matmul(o[:, c0:c1], q[:, t * P:t * P + P], k[:, 0:w], start=True,
                                               stop=scores_extra is None, skip_group_check=True)
                                if scores_extra:
                                    mm = scores_extra(s, o[:, c0:c1], w)
                            mm.then_inc(s_mm, 1)
                    if 1 <= s <= N:
                        u = s - 1
                        pe.wait_ge(p_ready, A["u0"] + u + 1)
                        if A["u0"] + u >= 2:
                            pe.wait_ge(pt_copy, A["u0"] + u - 1)
                        e = A["t"][1][:, u % 2, :]
                        for j, (c0, c1, _) in enumerate(prob_tiles(A)):
                            mm = pe.transpose(tp[u % 2][:, j * P:j * P + P], e[:, c0:c1], ident[:, :])
                        mm.then_inc(pt_mm, 1)
                    if s >= 2:
                        u = s - 2
                        pe.wait_ge(pt_copy, A["u0"] + u + 1)
                        if A["u0"] + u >= 2:
                            pe.wait_ge(o_lo, A["u0"] + u - 1)
                        pt = A["t"][2][:, u % 2, :]
                        v = values(u)
                        o = ps[u % 2]
                        if A["causal"]:
                            pe.matmul(o[:, 0:S], v(0), pt[:, 0:S], start=True, stop=False, skip_group_check=True)
                            mm = pe.matmul(o[:, P:S], v(1), pt[:, S:S + P], start=False, stop=True, skip_group_check=True)
                        else:
                            pe.matmul(o[:, 0:S], v(0), pt[:, 0:S], start=True, stop=False, skip_group_check=True)
                            mm = pe.matmul(o[:, 0:S], v(1), pt[:, S:2 * S], start=False, stop=True, skip_group_check=True)
                        mm.then_inc(o_mm, 1)

            pe.wait_ge(small_in, 64)
            pe.matmul(ps[0][0:N_SELF, 0:384], tab[:, :], onehot[:, :], start=True, stop=True).then_inc(b_mm, 1)
            norm(hs)
            normed(0)
            with pe.Fori(0, 2) as j:
                n.enter(j, 16)
                bl.enter(j, 2)
                for _ in range(2):
                    features(xh, xl)
                n.leave(2)
                bl.leave(2)
            pe.wait_ge(gates_in, 32)
            pe.wait_ge(conv_done, 2)
            pe.wait_ge(b_f, 1)
            for t in range(RNN_T):
                if t >= 2:
                    pe.wait_ge(gate_read, t - 1)
                pe.matmul(ps[t % 2][:, 0:S], w_rec[:, t, :], rxc[:, t, :], start=True, stop=True, skip_group_check=True)
                pe.matmul(ps[t % 2][:, S:2 * S], w_ing[:, t, :], rxc[:, t, :], start=True, stop=True,
                          skip_group_check=True).then_inc(gate_mm, 1)
            with pe.Fori(0, 2) as j:
                n.enter(j, 16)
                bl.enter(j, 2)
                for _ in range(2):
                    features(xh, xl)
                n.leave(2)
                bl.leave(2)
            pe.wait_ge(f_split, 1)
            for k in range(KT):
                mm = three(tp[0][:, 0:S], f_hi[:, k * 8:k * 8 + P], f_lo[:, k * 8:k * 8 + P], xh[:, k, :], xl[:, k, :],
                           k == 0, k == KT - 1, True)
            mm.then_inc(f_done, 1)
            pe.wait_ge(gate_read, RNN_T)
            for g in range(8):
                pe.wait_ge(sq_ready, g // 2 + 1)
                if g >= 2:
                    pe.wait_ge(ms_root, g - 1)
                pe.matmul(ps[g % 2][:, :], mean[:, :], sq1[:, 2 * g:2 * g + 2, :].rearrange("p a b -> p (a b)"),
                          start=True, stop=True).then_inc(ms_mm, 1)
            for _ in range(2):
                tokens(current)
            pe.wait_ge(qk_ready, 8)
            pe.wait_ge(c_ready, 1)
            pe.wait_ge(late_in, 48)

            def minus_c(u, o, w):
                return pe.matmul(o, negsel[:, u, :], c_cum[:, 0:w], start=False, stop=True, skip_group_check=True)

            for b in range(2):
                pe.wait_ge(acc_free[b], bl.n // 2)
            attend(0, lambda u, c: (qk1[:, u, :], qk1[:, HEADS1 + u, :]),
                   lambda u: lambda kt: v1[:, kt, u * P:u * P + P], minus_c)
            pe.wait_ge(o_lo, HEADS1)
            pe.wait_ge(rnn_lo, 1)
            with pe.Fori(0, 2) as j:
                n.enter(j, 16)
                bl.enter(j, 2)
                for _ in range(2):
                    tokens(current)
                n.leave(2)
                bl.leave(2)
            norm(hs)
            normed(1)
            pe.wait_ge(rt_split, 1)
            for k in range(KT):
                w = slice(k * N_ROUTER, k * N_ROUTER + P)
                mm = three(ps[0][:, 0:S], rt_hi[:, w], rt_lo[:, w], xh[:, k, :], xl[:, k, :], k == 0, k == KT - 1, True)
            mm.then_inc(rt_mm, 1)
            pe.wait_ge(rt_copy, 1)
            for t in range(TT):
                mm = pe.transpose(ps[1][:, t * P:t * P + P], lgT[:, t * P:t * P + P], ident[:, :])
            mm.then_inc(rt_tp, 1)
            downs = Count()

            def down(par):
                pe.wait_ge(hid_lo, downs.at(1))
                downs.n += 1
                for _ in range(4):
                    tokens(lambda k: (hid_h[:, par, k * S:(k + 1) * S], hid_l[:, par, k * S:(k + 1) * S]), 1)

            features(xh, xl)
            with pe.Fori(0, N_EXPERTS // 2 - 1) as i:
                n.enter(i, 24)
                bl.enter(i, 10)
                downs.enter(i, 2)
                for par in range(2):
                    features(xh, xl)
                    down(par)
                for c in (n, bl, downs):
                    c.leave(N_EXPERTS // 2 - 1)
            features(xh, xl)
            down(0)
            down(1)
            pe.wait_ge(pT_ready, 1)
            for _ in range(4):
                tokens(lambda k: (pT_h[:, k, :], pT_l[:, k, :]), 1)
            norm(hs)
            normed(2)
            with pe.Fori(0, 2) as j:
                n.enter(j, 16)
                bl.enter(j, 2)
                for _ in range(2):
                    tokens(current)
                n.leave(2)
                bl.leave(2)
            norm(hs)
            normed(3)
            with pe.Fori(0, 4) as j:
                n.enter(j, 16)
                bl.enter(j, 2)
                for _ in range(2):
                    features(xh, xl)
                n.leave(4)
                bl.leave(4)
            pe.wait_ge(b_in, 32)
            for g in range(8):
                if g >= 2:
                    pe.wait_ge(b_copy, g - 1)
                else:
                    pe.wait_ge(rt_read, 1)
                pe.matmul(ps[g % 2][:, :], flip[:, :], hank[:, 2 * g:2 * g + 2, :].rearrange("p a b -> p (a b)"),
                          start=True, stop=True).then_inc(b_flip, 1)
            with pe.Fori(0, 2) as j:
                n.enter(j, 16)
                bl.enter(j, 2)
                for _ in range(2):
                    tokens(current)
                n.leave(2)
                bl.leave(2)
            pe.wait_ge(b_copy, 8)
            for b in range(2):
                pe.wait_ge(acc_free[b], bl.n // 2)
            attend(1, operands2, lambda u: lambda kt: v2[:, kt, V_TILE[u] * P:V_TILE[u] * P + P])
            for g in range(N_DIFF // 2):
                pe.wait_ge(o_sq, N_DIFF)
                pe.wait_ge(o_lo, HEADS1 + N_SELF)
                if g >= 2:
                    pe.wait_ge(ms_root, 8 + g - 1)
                pe.matmul(ps[g % 2][:, :], mean[:, :], qk2[:, N_DIFF + 2 * g:N_DIFF + 2 * g + 2, :].rearrange("p a b -> p (a b)"),
                          start=True, stop=True).then_inc(ms_mm, 1)
            pe.wait_ge(rnn_lo, 2)
            for _ in range(2):
                tokens(current)
            norm(mem)
            for _ in range(2):
                tokens(current)
            normed(4)
            features(memh, meml)
            tokens(lambda k: (memh[:, k, :], meml[:, k, :]))
            norm(hs_c)
            normed(5)
            features(xh, xl)
            for b in range(2):
                pe.wait_ge(acc_free[b], (bl.n + 1 - b) // 2)
            attend(2, lambda u, c: (qc[:, u, :], km[:, u, :]), lambda u: lambda kt: vm[:, kt, u * P:u * P + P])
            pe.wait_ge(o_lo, HEADS1 + N_SELF + N_MEM_HEADS)
            for _ in range(4):
                tokens(current, 2)
            norm(hs)
            normed(6)
            with pe.Fori(0, FF_T // 4) as j:
                n.enter(j, 16)
                bl.enter(j, 2)
                for _ in range(2):
                    features(xh, xl)
                n.leave(FF_T // 4)
                bl.leave(FF_T // 4)
            pe.wait_ge(a_lo, FF_T // 2)

            def ff(k):
                if k < FA:
                    return ah[:, k, :], al[:, k, :]
                return xh[:, k - FA, :], xl[:, k - FA, :]

            for _ in range(4):
                tokens(ff, FF_T // 2)
            assert n.n == N_CHUNKS

        @block.scalar
        def _(act):
            n = Count()
            bl = Count()
            steps = Count()
            norms = Count()
            hv = Count()

            def split(k):
                m = n.n + k
                if n.i is None and m >= N_CHUNKS:
                    return
                act.wait_ge(raw_in[m % RING], n.at(k, RING, 32) + 32)
                if n.i is not None or m >= RING:
                    act.wait_ge(chunk_used, n.at(k + 1 - RING))
                act.activation(whi[:, m % RING, :], raw[:, m % RING, :], ACT.Copy).then_inc(hi_ready, 1)

            def consume(k):
                for _ in range(k):
                    split(AHEAD)
                    n.n += 1

            def own(ins):
                ins.then_inc(act_step, 1)
                steps.n += 1

            def h_done():
                act.wait_ge(acc_free[0], (bl.n + 1) // 2)
                act.wait_ge(acc_free[1], bl.n // 2)

            def norm_rows(src, dst, junk):
                k = norms.n
                act.activation(junk, src[:, 0, :], ACT.Square, accum_out=ss[:, 0:1]).then_inc(n_ss, 1)
                act.wait_ge(n_inv, k + 1)
                act.activation(rstd[:, :], inv[:, :], ACT.Sqrt).then_inc(n_rstd, 1)
                act.wait_ge(n_rstd, k + 1)
                act.activation(dst[:, 0, :], src[:, 0, :], ACT.Copy, scale=rstd[:, 0:1]).then_inc(n_hs0, 1)

            def norm_parts(hi):
                k = norms.n
                norms.n += 1
                for g in range(KT // 2):
                    act.wait_ge(n_tp, 8 * k + g + 1)
                    for j in range(2):
                        kt = 2 * g + j
                        o = act.activation(hi[:, kt, :], tp[g % 2][:, j * S:(j + 1) * S], ACT.Copy,
                                           scale=col(V_GAIN + k * KT + kt))
                    o.then_inc(n_hi, 1)

            def attend(a, outputs):
                A = AT[a]
                comps, N = A["comps"], A["units"]
                first = [sum(comps[:u]) for u in range(N)]
                sneg, e, pt = A["t"]
                for s in range(N + 3):
                    if s < N:
                        for c in range(comps[s]):
                            m = A["m0"] + first[s] + c
                            act.wait_ge(s_max, m + 1)
                            if c == 0 and s >= 2:
                                act.wait_ge(pt_mm, A["u0"] + s - 1)
                            dst = e[:, s % 2, :] if c == 0 else sneg[:, m % 2, :]
                            for t, (c0, c1, _) in enumerate(spans(A)):
                                o = act.activation(dst[:, c0:c1], sneg[:, m % 2, c0:c1], ACT.Exp,
                                                   bias=stat[:, m % 2, t:t + 1], scale=-1.0,
                                                   accum_out=stat[:, m % 2, 2 + t:3 + t])
                            o.then_inc(s_exp, 1)
                    if 1 <= s <= N:
                        u = s - 1
                        w = len(prob_tiles(A)) * P
                        act.wait_ge(pt_mm, A["u0"] + u + 1)
                        if u >= 2:
                            act.wait_ge(o_mm, A["u0"] + u - 1)
                        act.activation(pt[:, u % 2, 0:w], tp[u % 2][:, 0:w], ACT.Copy).then_inc(pt_copy, 1)
                    if 2 <= s <= N + 1:
                        outputs(s - 2)

            act.wait_ge(vec_in, 16)
            act.wait_ge(x_in, 32)
            norm_rows(h, hs, hs[:, 0, :])
            for k in range(AHEAD):
                split(k)
            act.wait_ge(lam_y, 1)
            act.activation(lru_t[:, 1, :], lru_t[:, 0, :], ACT.Exp, scale=-1.0).then_inc(lam_e, 1)
            act.wait_ge(lam_dot, 2)
            act.activation(lam[:, 2:4], lam[:, 0:2], ACT.Exp).then_inc(lam_e, 1)
            norm_parts(xh)
            act.wait_ge(late_in, 48)
            act.activation(f_hi[:, :], f_raw[:, :], ACT.Copy).then_inc(f_z, 1)
            consume(16)
            bl.n += 2
            for b in range(2):
                consume(8)
                act.wait_ge(chunk_used, n.n)
                act.activation(gel[:, 4 * b:4 * b + 4, :].rearrange("p a b -> p (a b)"), acc[bl.n % 2][:, :],
                               ACT.Gelu_apprx_tanh).then_inc(acc_free[bl.n % 2], 1)
                bl.n += 1
            for t in range(RNN_T):
                act.wait_ge(gate_mm, t + 1)
                act.activation(r_t[:, t, :], ps[t % 2][:, 0:S], ACT.Sigmoid, bias=col(V_BREC + t))
                act.activation(i_t[:, t, :], ps[t % 2][:, S:2 * S], ACT.Sigmoid, bias=col(V_BIN + t)).then_inc(gate_read, 1)
            act.wait_ge(b_out, 16)
            for b in range(4):
                two_t = slice(2 * b, 2 * b + 2)
                consume(4)
                act.wait_ge(la_ready, b + 1)
                act.activation(a_t[:, two_t, :], r_t[:, two_t, :], ACT.Exp, scale=-1.0)
                act.activation(r_t[:, two_t, :], r_t[:, two_t, :], ACT.Tanh).then_inc(a_ready, 1)
                consume(4)
                act.wait_ge(lru_q, b + 1)
                act.activation(r_t[:, two_t, :], r_t[:, two_t, :], ACT.Sqrt).then_inc(lru_root, 1)
                act.wait_ge(acc_free[bl.n % 2], bl.n // 2 + 1)
                act.activation(sq1[:, 4 * b:4 * b + 4, :], qk1[:, 4 * b:4 * b + 4, :], ACT.Square).then_inc(sq_ready, 1)
                bl.n += 1
            act.wait_ge(f_done, 1)
            act.wait_ge(rnn_ready, 4)
            act.activation(z_f[:, :], tp[0][0:8, 0:S], ACT.Identity, bias=vec[0:8, V_BF:V_BF + 1]).then_inc(f_z, 1)
            act.wait_ge(f_abs, 1)
            act.activation(z_y[:, :], z_n[:, :], ACT.Exp, scale=-1.0).then_inc(f_y, 1)
            for g in range(8):
                act.wait_ge(ms_mm, g + 1)
                if g >= 2:
                    act.wait_ge(qk_ready, g - 1)
                act.activation(rst1[:, g % 2, :], ps[g % 2][:, :], ACT.Sqrt, bias=eps[:, 0:1]).then_inc(ms_root, 1)
            consume(16)
            bl.n += 2
            act.wait_ge(rnn_ready, 4)
            act.wait_ge(chunk_used, n.n)
            act.activation(xh[:, HEADS1:KT, :], gel[:, :, :], ACT.Copy).then_inc(rnn_hi, 1)

            def out1(u):
                act.wait_ge(o_mm, u + 1)
                act.activation(xh[:, u, :], ps[u % 2][:, 0:S], ACT.Copy).then_inc(o_hi, 1)

            attend(0, out1)
            with act.Fori(0, 4) as j:
                n.enter(j, 8)
                consume(8)
                n.leave(4)
            bl.n += 4
            act.wait_ge(rt_in, 16)
            act.wait_ge(rt_pad, 1)
            h_done()
            norm_rows(h, hs, hs[:, 0, :])
            act.activation(rt_hi[:, :], rt_raw[:, :], ACT.Copy).then_inc(rt_e, 1)
            norm_parts(xh)
            act.wait_ge(rt_mm, 1)
            act.activation(lgT[:, :], ps[0][:, 0:S], ACT.Copy).then_inc(rt_copy, 1)
            act.wait_ge(rt_read, 2)
            act.activation(g_e[:, :, :], g_sh[:, :, :], ACT.Exp).then_inc(rt_e, 1)
            act.wait_ge(rt_read, 3)
            act.activation(r_s[:, 7, :], r_s[:, 6, :], ACT.Exp).then_inc(rt_e, 1)

            def hidden(par):
                consume(8)
                act.wait_ge(chunk_used, n.at())
                if hv.i is not None or hv.n >= 2:
                    act.wait_ge(hid_ready, hv.at(-1))
                act.activation(sg[:, par, :], acc[bl.n % 2][:, 0:512], ACT.Silu).then_inc(silu_ready, 1)
                bl.n += 1
                act.wait_ge(hid_ready, hv.at(1))
                act.activation(hid_h[:, par, :], hid[:, par, :], ACT.Copy).then_inc(hid_hi, 1)
                hv.n += 1

            def down():
                consume(4)
                bl.n += 4

            hidden(0)
            with act.Fori(0, N_EXPERTS // 2 - 1) as i:
                n.enter(i, 24)
                bl.enter(i, 10)
                hv.enter(i, 2)
                for par in (1, 0):
                    hidden(par)
                    down()
                for c in (n, bl, hv):
                    c.leave(N_EXPERTS // 2 - 1)
            hidden(1)
            down()
            down()
            act.wait_ge(p_in, 48)
            act.activation(pT_h[:, :, :], pT[:, :, :], ACT.Copy).then_inc(rt_e, 1)
            h_done()
            norm_rows(h, hs, hs[:, 0, :])
            for b in range(4):
                act.wait_ge(chunk_used, n.n + 1)
                act.activation(upb[:, :, b * 512:(b + 1) * 512], acc[bl.n % 2][:, :].rearrange("p (t n) -> p t n", t=TT),
                               ACT.Copy).then_inc(acc_free[bl.n % 2], 1)
                bl.n += 1
                consume(1)
            norm_parts(xh)
            gt = Count()
            with act.Fori(0, 2) as j:
                n.enter(j, 16)
                bl.enter(j, 2)
                gt.enter(j, 2)
                for b in range(2):
                    consume(8)
                    act.wait_ge(chunk_used, n.at())
                    act.wait_ge(acc_free[b], bl.at(0, 2))
                    act.activation(gate[:, b, :], acc[bl.n % 2][:, :], ACT.Sigmoid).then_inc(gate_ready, 1)
                    bl.n += 1
                    gt.n += 1
                for c in (n, bl, gt):
                    c.leave(2)
            h_done()
            norm_rows(h, hs, hs[:, 0, :])
            norm_parts(xh)
            with act.Fori(0, 8) as j:
                n.enter(j, 8)
                consume(8)
                n.leave(8)
            for g in range(8):
                act.wait_ge(b_flip, g + 1)
                act.activation(bias[:, 2 * g:2 * g + 2, :].rearrange("p a b -> p (a b)"), ps[g % 2][:, :],
                               ACT.Copy).then_inc(b_copy, 1)
            with act.Fori(0, 4) as j:
                n.enter(j, 8)
                consume(8)
                n.leave(4)
            bl.n += 12

            def out2(u):
                act.wait_ge(o_mm, HEADS1 + u + 1)
                if u < N_DIFF:
                    act.wait_ge(o_lo, HEADS1 + u + 1)
                    act.activation(qk2[:, N_DIFF + u, :], qk2[:, u, :], ACT.Square).then_inc(o_sq, 1)
                else:
                    act.activation(xh[:, u, :], ps[u % 2][:, 0:S], ACT.Copy).then_inc(o_hi, 1)

            attend(1, out2)
            for g in range(N_DIFF // 2):
                act.wait_ge(ms_mm, 8 + g + 1)
                if g >= 2:
                    act.wait_ge(qk_ready, 8 + g - 1)
                act.activation(rst2[:, g % 2, :], ps[g % 2][:, :], ACT.Sqrt, bias=eps[:, 0:1]).then_inc(ms_root, 1)
            act.wait_ge(qk_ready, 8 + N_DIFF // 2)
            act.activation(xh[:, 0:N_DIFF, :], qk2[:, 0:N_DIFF, :], ACT.Copy).then_inc(rnn_hi, 1)
            act.wait_ge(mem_in, 32)
            act.wait_ge(rnn_lo, 2)
            norm_rows(mem, mem, junk_a[:, :])
            consume(16)
            bl.n += 2
            norm_parts(memh)
            consume(16)
            bl.n += 2
            h_done()
            norm_rows(h, hs_c, hs_c[:, 0, :])
            consume(16)
            bl.n += 2
            norm_parts(xh)
            consume(8)
            bl.n += 1

            def out3(u):
                act.wait_ge(o_mm, HEADS1 + N_SELF + u + 1)
                act.activation(xh[:, u, :], ps[u % 2][:, 0:S], ACT.Copy).then_inc(o_hi, 1)

            attend(2, out3)
            consume(8)
            bl.n += 4
            h_done()
            norm_rows(h, hs, hs[:, 0, :])
            norm_parts(xh)
            ff = Count()

            def hidden2(dst):
                consume(8)
                act.wait_ge(chunk_used, n.at())
                if ff.i is not None or ff.n:
                    act.wait_ge(cv_ready, ff.at())
                act.activation(gpad[:, :, 2:2 + S], acc[bl.n % 2][:, 0:512].rearrange("p (a b) -> p a b", a=2),
                               ACT.Copy).then_inc(g_ready, 1)
                act.wait_ge(cv_ready, ff.at(1))
                act.activation(cv[:, :, :], cv[:, :, :], ACT.Silu).then_inc(sil2, 1)
                act.wait_ge(af_ready, ff.at(1))
                act.activation(dst, af[:, :, :], ACT.Copy).then_inc(a_hi, 1)
                bl.n += 1
                ff.n += 1

            with act.Fori(0, FF_T // 4 - 1) as j:
                n.enter(j, 16)
                bl.enter(j, 2)
                ff.enter(j, 2)
                for b in range(2):
                    hidden2(ah[:, bass.ds(j * 4 + 2 * b, 2), :])
                for c in (n, bl, ff):
                    c.leave(FF_T // 4 - 1)
            hidden2(ah[:, FA - 2:FA, :])
            hidden2(xh[:, 0:2, :])
            for b in range(4):
                consume(FF_T // 2)
                bl.n += 1
            assert n.n == N_CHUNKS
            h_done()
            act.activation(hs[:, 0, :], h[:, 0, :], ACT.Square, accum_out=ss[:, 0:1]).then_inc(n_ss, 1)
            act.wait_ge(n_inv, 8)
            act.activation(rstd[:, :], inv[:, :], ACT.Sqrt).then_inc(n_rstd, 1)

        @block.vector
        def _(dve):
            n = Count()
            bl = Count()
            steps = Count()
            norms = Count()
            hv = Count()

            def split(k):
                m = n.n + k
                if n.i is None and m >= N_CHUNKS:
                    return
                dve.wait_ge(hi_ready, n.at(k + 1))
                dve.tensor_tensor(wlo[:, m % RING, :], raw[:, m % RING, :], whi[:, m % RING, :],
                                  ALU.subtract).then_inc(lo_ready, 1)

            def consume(k):
                for _ in range(k):
                    split(AHEAD)
                    n.n += 1

            def own(ins):
                ins.then_inc(dve_step, 1)
                steps.n += 1

            def mine():
                dve.wait_ge(dve_step, steps.at())

            def h_done():
                dve.wait_ge(acc_free[0], (bl.n + 1) // 2)
                dve.wait_ge(acc_free[1], bl.n // 2)

            def mean_inv(k):
                dve.wait_ge(n_ss, k + 1)
                own(dve.tensor_scalar(inv[:, :], ss[:, :], 1.0 / D, EPS, ALU.mult, ALU.add))
                mine()
                dve.reciprocal(inv[:, :], inv[:, :]).then_inc(n_inv, 1)

            def norm_rows(src, dst, junk):
                k = norms.n
                own(dve.tensor_tensor_reduce(junk, src[:, 1, :], src[:, 1, :], 1.0, 0.0, ALU.mult, ALU.add, ss[:, 1:2]))
                mine()
                mean_inv(k)
                dve.wait_ge(n_rstd, k + 1)
                dve.tensor_scalar(dst[:, 1, :], src[:, 1, :], rstd[:, 1:2], None, ALU.mult).then_inc(n_hs1, 1)

            def norm_parts(hi, lo):
                k = norms.n
                norms.n += 1
                for g in range(KT // 2):
                    dve.wait_ge(n_hi, 8 * k + g + 1)
                    for j in range(2):
                        kt = 2 * g + j
                        o = dve.scalar_tensor_tensor(lo[:, kt, :], tp[g % 2][:, j * S:(j + 1) * S],
                                                     col(V_GAIN + k * KT + kt), hi[:, kt, :], ALU.mult, ALU.subtract)
                    o.then_inc(n_lo, 1)

            def add_block(cols):
                b = bl.n % 2
                dve.wait_ge(acc_free[1 - b], bl.at(1, 2))
                hh = h[:, :, cols]
                dve.tensor_tensor(hh, acc[b][:, :].rearrange("p (t n) -> p t n", t=TT), hh, ALU.add).then_inc(acc_free[b], 1)
                bl.n += 1

            def log1p(y, z, q, s, r):
                own(dve.tensor_scalar(z, y, 2.0, None, ALU.add))
                mine()
                own(dve.reciprocal(z, z))
                mine()
                own(dve.tensor_tensor(z, y, z, ALU.mult))
                mine()
                own(dve.tensor_tensor(q, z, z, ALU.mult))
                mine()
                own(dve.tensor_scalar(s, q, 1.0 / 17, None, ALU.mult))
                for d in (15, 13, 11, 9, 7, 5, 3):
                    mine()
                    own(dve.scalar_tensor_tensor(s, s, 1.0 / d, q, ALU.add, ALU.mult))
                mine()
                own(dve.scalar_tensor_tensor(s, s, 1.0, z, ALU.add, ALU.mult))
                mine()
                own(dve.tensor_scalar(r, s, 2.0, None, ALU.mult))
                mine()

            def attend(a, bias_of, scale_of, outputs, mix=None):
                A = AT[a]
                comps, N = A["comps"], A["units"]
                first = [sum(comps[:u]) for u in range(N)]
                sneg, e, pt = A["t"]
                for s in range(N + 3):
                    if s < N:
                        for c in range(comps[s]):
                            m = A["m0"] + first[s] + c
                            dve.wait_ge(s_mm, m + 1)
                            if m >= A["m0"] + 2:
                                dve.wait_ge(s_exp, m - 1)
                                mine()
                            if s and comps[s - 1] == 2:
                                dve.wait_ge(p_ready, A["u0"] + s)
                            for t, (c0, c1, b0) in enumerate(spans(A)):
                                o = dve.tensor_tensor_reduce(sneg[:, m % 2, c0:c1], score[m % 4][:, c0:c1],
                                                             bias_of(s)[:, b0:b0 + c1 - c0], -scale_of(s), 3e38,
                                                             ALU.add, ALU.min, stat[:, m % 2, t:t + 1])
                            o.then_inc(s_max, 1)
                        if comps[s] == 2:
                            finish(A, s, first[s], e, sneg)
                    if 1 <= s <= N and comps[s - 1] == 1:
                        finish(A, s - 1, first[s - 1], e, sneg)
                    if 2 <= s <= N + 1:
                        outputs(s - 2)

            def finish(A, u, f, e, sneg):
                two_c = A["comps"][u] == 2
                m = A["m0"] + f
                dve.wait_ge(s_exp, m + (2 if two_c else 1))
                for c in range(2 if two_c else 1):
                    own(dve.reciprocal(rsum[:, (m + c) % 2, :], stat[:, (m + c) % 2, 2:4]))
                mine()
                if two_c:
                    own(dve.tensor_scalar(rsum[:, (m + 1) % 2, :], rsum[:, (m + 1) % 2, :], lam[:, 5:6], None, ALU.mult))
                for t, (c0, c1, _) in enumerate(spans(A)):
                    d = e[:, u % 2, c0:c1]
                    o = dve.tensor_scalar(d, d, rsum[:, m % 2, t:t + 1], None, ALU.mult)
                    if two_c:
                        own(o)
                if two_c:
                    mine()
                    for t, (c0, c1, _) in enumerate(spans(A)):
                        d = e[:, u % 2, c0:c1]
                        o = dve.scalar_tensor_tensor(d, sneg[:, (m + 1) % 2, c0:c1], rsum[:, (m + 1) % 2, t:t + 1], d,
                                                     ALU.mult, ALU.add)
                o.then_inc(p_ready, 1)

            own(dve.memset(eps[:, :], EPS))
            own(dve.memset(mean[:, :], 1.0 / P))
            own(dve.memset(c_cum[:, :], 0.0))
            own(dve.memset(rxp[:, :, 0:4], 0.0))
            dve.memset(f_raw[:, KT * 8:], 0.0).then_inc(consts, 1)
            dve.wait_ge(lam_in, 16)
            for j in range(2):
                dve.tensor_tensor_reduce(lamj[:, j, :], lamv[:, 2 * j, :], lamv[:, 2 * j + 1, :], 1.0, 0.0, ALU.mult, ALU.add,
                                         lam[:, j:j + 1]).then_inc(lam_dot, 1)
            dve.wait_ge(vec_in, 16)
            own(dve.tensor_scalar(lru_t[:, 0, :], col(V_LAM, RNN_T), -1.0, None, ALU.mult))
            mine()
            dve.tensor_tensor(lru_t[:, 0, :], lru_t[:, 0, :], col(V_LAM, RNN_T), ALU.max).then_inc(lam_y, 1)
            dve.tensor_scalar(qg[:, 0:1], col(V_QN), HEAD_SCALE, None, ALU.mult)
            own(dve.tensor_scalar(qg[:, 1:2], col(V_SUB), 1.0 - LAM_INIT, None, ALU.mult))
            dve.wait_ge(b_mm, 1)
            dve.wait_ge(small_in, 64)
            dve.scalar_tensor_tensor(frev[:, :], ps[0][0:N_SELF, 0:384], iscale[:, 0:1], addend[:, :],
                                     ALU.mult, ALU.add).then_inc(b_f, 1)
            dve.wait_ge(x_in, 32)
            norm_rows(h, hs, hs[:, 1, :])
            for k in range(AHEAD):
                split(k)
            norm_parts(xh, xl)
            dve.wait_ge(lam_e, 2)
            log1p(lru_t[:, 1, :], lru_t[:, 2, :], lru_t[:, 3, :], lru_t[:, 4, :], lru_t[:, 5, :])
            own(dve.tensor_scalar(lru_t[:, 0, :], col(V_LAM, RNN_T), -1.0, 0.0, ALU.mult, ALU.max))
            mine()
            own(dve.tensor_tensor(lru_t[:, 0, :], lru_t[:, 0, :], lru_t[:, 5, :], ALU.add))
            mine()
            own(dve.tensor_scalar(sp8[:, :], lru_t[:, 0, :], LRU_C, None, ALU.mult))
            own(dve.tensor_tensor(lam[:, 4:5], lam[:, 2:3], lam[:, 3:4], ALU.subtract))
            mine()
            own(dve.tensor_scalar(lam[:, 5:6], lam[:, 4:5], LAM_INIT, -1.0, ALU.add, ALU.mult))
            dve.wait_ge(f_z, 1)
            dve.tensor_tensor(f_lo[:, :], f_raw[:, :], f_hi[:, :], ALU.subtract).then_inc(f_split, 1)
            for b in range(2):
                consume(8)
                dve.wait_ge(chunk_used, n.n)
                four = range(4 * b, 4 * b + 4)
                dve.tensor_copy(rxp[:, 4 * b:4 * b + 4, 4:4 + S],
                                acc[bl.n % 2][:, :].rearrange("p (a b) -> p a b", a=4)).then_inc(acc_free[bl.n % 2], 1)
                bl.n += 1
                dve.wait_ge(acc_free[b], 1)
                for t in four:
                    own(dve.tensor_scalar(rxc[:, t, :], rxp[:, t, 4:4 + S], col(V_CONV + 3 * RNN_T + t),
                                          col(V_CONV + 4 * RNN_T + t), ALU.mult, ALU.add))
                for tap in (2, 1, 0):
                    mine()
                    for t in four:
                        o = dve.scalar_tensor_tensor(rxc[:, t, :], rxp[:, t, tap + 1:tap + 1 + S],
                                                     col(V_CONV + tap * RNN_T + t), rxc[:, t, :], ALU.mult, ALU.add)
                        if tap:
                            own(o)
                o.then_inc(conv_done, 1)
            consume(16)
            bl.n += 2
            for b in range(4):
                two_t = slice(2 * b, 2 * b + 2)
                consume(2)
                dve.wait_ge(gate_read, RNN_T)
                mine()
                for t in (2 * b, 2 * b + 1):
                    o = dve.tensor_scalar(r_t[:, t, :], r_t[:, t, :], sp8[:, t:t + 1], None, ALU.mult)
                o.then_inc(la_ready, 1)
                consume(2)
                dve.wait_ge(a_ready, b + 1)
                own(dve.tensor_tensor(i_t[:, two_t, :], i_t[:, two_t, :], rxc[:, two_t, :], ALU.mult))
                d = den[:, b % 2, :].rearrange("p (a b) -> p a b", a=2)
                own(dve.tensor_scalar(d, r_t[:, two_t, :], 1.0, None, ALU.add))
                mine()
                own(dve.reciprocal(d, d))
                mine()
                dve.scalar_tensor_tensor(r_t[:, two_t, :], r_t[:, two_t, :], 2.0, d, ALU.mult, ALU.mult).then_inc(lru_q, 1)
                consume(4)
                dve.wait_ge(chunk_used, n.n)
                dve.tensor_copy(qk1[:, 4 * b:4 * b + 4, :].rearrange("p a b -> p (a b)"), acc[bl.n % 2][:, :])\
                   .then_inc(acc_free[bl.n % 2], 1)
                bl.n += 1
                dve.wait_ge(lru_root, b + 1)
                own(dve.tensor_tensor(i_t[:, two_t, :], i_t[:, two_t, :], r_t[:, two_t, :], ALU.mult))
                mine()
                for t in (2 * b, 2 * b + 1):
                    own(dve.tensor_tensor_scan(rxc[:, t, :], a_t[:, t, :], i_t[:, t, :], 0.0, ALU.mult, ALU.add))
                mine()
                dve.tensor_tensor(gel[:, two_t, :], gel[:, two_t, :], rxc[:, two_t, :], ALU.mult).then_inc(rnn_ready, 1)
            dve.wait_ge(f_z, 2)
            own(dve.tensor_scalar(z_n[:, :], z_f[:, :], -1.0, None, ALU.mult))
            mine()
            dve.tensor_tensor(z_n[:, :], z_n[:, :], z_f[:, :], ALU.max).then_inc(f_abs, 1)
            dve.wait_ge(f_y, 1)
            own(dve.memset(z_1[:, :], 1.0))
            log1p(z_y[:, :], z_z[:, :], z_q[:, :], z_s[:, :], z_n[:, :])
            own(dve.scalar_tensor_tensor(z_f[:, :], z_f[:, :], 0.0, z_n[:, :], ALU.min, ALU.subtract))
            mine()
            dve.tensor_tensor_scan(c_cum[0:8, :], z_1[:, :], z_f[:, :], 0.0, ALU.mult, ALU.add).then_inc(c_ready, 1)
            for g in range(8):
                dve.wait_ge(ms_root, g + 1)
                own(dve.reciprocal(rst1[:, g % 2, :], rst1[:, g % 2, :]))
                mine()
                two_h = qk1[:, 2 * g:2 * g + 2, :].rearrange("p a b -> p (a b)")
                dve.scalar_tensor_tensor(two_h, two_h, qg[:, 0:1] if g < 4 else col(V_KN), rst1[:, g % 2, :],
                                         ALU.mult, ALU.mult).then_inc(qk_ready, 1)
            for b in range(2):
                consume(8)
                dve.wait_ge(chunk_used, n.n)
                dve.tensor_copy(v1[:, :, b * 512:(b + 1) * 512], acc[bl.n % 2][:, :].rearrange("p (t n) -> p t n", t=TT))\
                   .then_inc(acc_free[bl.n % 2], 1)
                bl.n += 1
            dve.wait_ge(rnn_hi, 1)
            dve.tensor_tensor(xl[:, HEADS1:KT, :], gel[:, :, :], xh[:, HEADS1:KT, :], ALU.subtract).then_inc(rnn_lo, 1)

            def out1(u):
                dve.wait_ge(o_hi, u + 1)
                dve.tensor_tensor(xl[:, u, :], ps[u % 2][:, 0:S], xh[:, u, :], ALU.subtract).then_inc(o_lo, 1)

            dve.wait_ge(late_in, 48)
            attend(0, lambda u: causal, lambda u: 1.0, out1)
            with dve.Fori(0, 2) as j:
                n.enter(j, 16)
                bl.enter(j, 2)
                for b in range(2):
                    consume(8)
                    dve.wait_ge(chunk_used, n.at())
                    add_block(bass.ds(j * 1024 + b * 512, 512))
                n.leave(2)
                bl.leave(2)
            h_done()
            norm_rows(h, hs, hs[:, 1, :])
            dve.wait_ge(rt_e, 1)
            dve.tensor_tensor(rt_lo[:, :], rt_raw[:, :], rt_hi[:, :], ALU.subtract).then_inc(rt_split, 1)
            norm_parts(xh, xl)
            dve.wait_ge(rt_tp, 1)
            dve.wait_ge(p_in, 48)
            lg_ps = ps[1][:, 0:S].rearrange("p (t n) -> p t n", t=TT)[:, :, 0:N_ROUTER]
            dve.tensor_copy(lg[:, :, :], lg_ps).then_inc(rt_read, 1)
            dve.wait_ge(rt_read, 1)

            def per(k, like):
                return r_s[:, k, :].unsqueeze(2).to_broadcast(like)

            def first_max(dst, k, x, keys, order, count):
                own(dve.tensor_reduce(r_s[:, k, :], x, AX_X, ALU.max))
                mine()
                own(dve.tensor_tensor(keys, x, per(k, [P, TT, count]), ALU.is_equal))
                mine()
                own(dve.tensor_tensor(keys, keys, order, ALU.mult))
                mine()
                own(dve.tensor_reduce(r_s[:, k + 1, :], keys, AX_X, ALU.max))
                mine()
                own(dve.tensor_tensor(dst, keys, per(k + 1, [P, TT, count]), ALU.is_equal))
                mine()

            gl = lg[:, :, 0:N_GROUPS]
            first_max(g_oh[:, :, :], 0, gl, g_key[:, :, :], desc4[:, :, :], N_GROUPS)
            dve.tensor_tensor(g_sh[:, :, :], gl, per(0, [P, TT, N_GROUPS]), ALU.subtract).then_inc(rt_read, 1)
            own(dve.tensor_scalar(g_key[:, :, :], g_oh[:, :, :], -NEG, NEG, ALU.mult, ALU.add))
            mine()
            for t in range(TT):
                e3 = lambda x: x[:, t, :].rearrange("p (g e) -> p g e", g=N_GROUPS)
                wide = lambda x: x[:, t, :].unsqueeze(2).to_broadcast([P, N_GROUPS, PER_GROUP])
                own(dve.tensor_tensor(e3(em), lg[:, t, N_GROUPS:N_ROUTER].rearrange("p (g e) -> p g e", g=N_GROUPS),
                                      wide(g_oh), ALU.mult))
                mine()
                own(dve.tensor_tensor(e3(em), e3(em), wide(g_key), ALU.add))
            mine()
            first_max(oh1[:, :, :], 2, em[:, :, :], key[:, :, :], desc[:, :, :], N_EXPERTS)
            own(dve.scalar_tensor_tensor(em[:, :, :], oh1[:, :, :], -3e38, em[:, :, :], ALU.mult, ALU.add))
            mine()
            first_max(oh2[:, :, :], 4, em[:, :, :], key[:, :, :], desc[:, :, :], N_EXPERTS)
            dve.tensor_tensor(r_s[:, 6, :], r_s[:, 4, :], r_s[:, 2, :], ALU.subtract).then_inc(rt_read, 1)
            dve.wait_ge(rt_e, 3)
            own(dve.tensor_reduce(r_s[:, 8, :], g_e[:, :, :], AX_X, ALU.add))
            own(dve.tensor_scalar(r_s[:, 9, :], r_s[:, 7, :], 1.0, None, ALU.add))
            mine()
            own(dve.tensor_tensor(r_s[:, 9, :], r_s[:, 9, :], r_s[:, 8, :], ALU.mult))
            mine()
            own(dve.reciprocal(r_s[:, 10, :], r_s[:, 9, :]))
            mine()
            own(dve.tensor_tensor(r_s[:, 11, :], r_s[:, 10, :], r_s[:, 7, :], ALU.mult))
            mine()
            own(dve.tensor_tensor(comb[:, :, :], oh1[:, :, :], per(10, [P, TT, N_EXPERTS]), ALU.mult))
            own(dve.tensor_tensor(key[:, :, :], oh2[:, :, :], per(11, [P, TT, N_EXPERTS]), ALU.mult))
            mine()
            own(dve.tensor_tensor(comb[:, :, :], comb[:, :, :], key[:, :, :], ALU.add))
            mine()

            def hidden(par):
                consume(8)
                dve.wait_ge(silu_ready, hv.at(1))
                dve.tensor_tensor(hid[:, par, :], sg[:, par, :], acc[bl.n % 2][:, 512:1024], ALU.mult).then_inc(hid_ready, 1)
                dve.wait_ge(hid_hi, hv.at(1))
                dve.tensor_tensor(hid_l[:, par, :], hid[:, par, :], hid_h[:, par, :], ALU.subtract).then_inc(hid_lo, 1)
                dve.sem_inc(acc_free[bl.n % 2], 1)
                bl.n += 1
                hv.n += 1

            def down(e):
                for c in range(4):
                    dve.wait_ge(chunk_used, n.at(1))
                    b = bl.n % 2
                    dve.wait_ge(acc_free[1 - b], bl.at(1, 2))
                    for t in range(TT):
                        hh = h[:, t, c * 512:c * 512 + 512]
                        w = comb[:, t, e:e + 1] if isinstance(e, int) else comb[:, t, bass.ds(e, 1)]
                        o = dve.scalar_tensor_tensor(hh, acc[b][:, t * 512:(t + 1) * 512], w, hh, ALU.mult, ALU.add)
                    o.then_inc(acc_free[b], 1)
                    bl.n += 1
                    consume(1)

            hidden(0)
            with dve.Fori(0, N_EXPERTS // 2 - 1) as i:
                n.enter(i, 24)
                bl.enter(i, 10)
                hv.enter(i, 2)
                hidden(1)
                down(i * 2)
                hidden(0)
                down(i * 2 + 1)
                for c in (n, bl, hv):
                    c.leave(N_EXPERTS // 2 - 1)
            hidden(1)
            down(N_EXPERTS - 2)
            down(N_EXPERTS - 1)
            dve.wait_ge(rt_e, 4)
            dve.tensor_tensor(pT_l[:, :, :], pT[:, :, :], pT_h[:, :, :], ALU.subtract).then_inc(pT_ready, 1)
            h_done()
            norm_rows(h, hs, hs[:, 1, :])
            consume(4)
            bl.n += 4
            norm_parts(xh, xl)
            h_done()
            gt = Count()
            with dve.Fori(0, 2) as j:
                n.enter(j, 16)
                bl.enter(j, 2)
                gt.enter(j, 2)
                for b in range(2):
                    consume(8)
                    dve.wait_ge(gate_ready, gt.at(1))
                    gt.n += 1
                    cols = bass.ds(j * 1024 + b * 512, 512)
                    g3 = gate[:, b, :].rearrange("p (t n) -> p t n", t=TT)
                    dve.tensor_tensor(g3, g3, upb[:, :, cols], ALU.mult).then_inc(ple_prod, 1)
                    dve.wait_ge(ple_prod, gt.at())
                    hh = h[:, :, cols]
                    dve.tensor_tensor(hh, hh, g3, ALU.add).then_inc(acc_free[bl.n % 2], 1)
                    bl.n += 1
                for c in (n, bl, gt):
                    c.leave(2)
            assert (bl.n + 1) // 2 == PLE_END[0] and bl.n // 2 == PLE_END[1], bl.n
            h_done()
            norm_rows(h, hs, hs[:, 1, :])
            norm_parts(xh, xl)
            with dve.Fori(0, 4) as j:
                n.enter(j, 16)
                bl.enter(j, 2)
                for b in range(2):
                    consume(8)
                    dve.wait_ge(chunk_used, n.at())
                    dve.tensor_copy(qk2[:, bass.ds(j * 8 + 4 * b, 4), :], acc[bl.n % 2][:, :].rearrange("p (a b) -> p a b", a=4))\
                       .then_inc(acc_free[bl.n % 2], 1)
                    bl.n += 1
                n.leave(4)
                bl.leave(4)
            with dve.Fori(0, 2) as j:
                n.enter(j, 16)
                bl.enter(j, 2)
                for b in range(2):
                    consume(8)
                    dve.wait_ge(chunk_used, n.at())
                    dve.tensor_copy(v2[:, :, bass.ds(j * 1024 + b * 512, 512)],
                                    acc[bl.n % 2][:, :].rearrange("p (t n) -> p t n", t=TT)).then_inc(acc_free[bl.n % 2], 1)
                    bl.n += 1
                n.leave(2)
                bl.leave(2)

            def out2(u):
                if u < N_DIFF:
                    dve.wait_ge(o_mm, HEADS1 + u + 1)
                    dve.tensor_copy(qk2[:, u, :], ps[u % 2][:, 0:S]).then_inc(o_lo, 1)
                else:
                    dve.wait_ge(o_hi, HEADS1 + u - N_DIFF + 1)
                    dve.tensor_tensor(xl[:, u, :], ps[u % 2][:, 0:S], xh[:, u, :], ALU.subtract).then_inc(o_lo, 1)

            dve.wait_ge(b_copy, 8)
            attend(1, lambda u: bias[:, u, :], lambda u: DIFF_SCALE if u < N_DIFF else HEAD_SCALE, out2)
            for g in range(N_DIFF // 2):
                dve.wait_ge(ms_root, 8 + g + 1)
                own(dve.reciprocal(rst2[:, g % 2, :], rst2[:, g % 2, :]))
                mine()
                two_h = qk2[:, 2 * g:2 * g + 2, :].rearrange("p a b -> p (a b)")
                dve.scalar_tensor_tensor(two_h, two_h, qg[:, 1:2], rst2[:, g % 2, :], ALU.mult, ALU.mult).then_inc(qk_ready, 1)
            dve.wait_ge(rnn_hi, 2)
            dve.tensor_tensor(xl[:, 0:N_DIFF, :], qk2[:, 0:N_DIFF, :], xh[:, 0:N_DIFF, :], ALU.subtract).then_inc(rnn_lo, 1)
            dve.wait_ge(mem_in, 32)
            norm_rows(mem, mem, junk_v[:, :])

            def add_two(j):
                for b in range(2):
                    consume(8)
                    dve.wait_ge(chunk_used, n.n)
                    add_block(slice(j * 1024 + b * 512, j * 1024 + b * 512 + 512))

            add_two(0)
            norm_parts(memh, meml)
            add_two(1)
            h_done()
            norm_rows(h, hs_c, hs_c[:, 1, :])
            consume(8)
            dve.wait_ge(chunk_used, n.n)
            dve.tensor_copy(km[:, :, :].rearrange("p a b -> p (a b)"), acc[bl.n % 2][:, :]).then_inc(acc_free[bl.n % 2], 1)
            bl.n += 1
            consume(8)
            dve.wait_ge(chunk_used, n.n)
            dve.tensor_copy(vm[:, :, :], acc[bl.n % 2][:, :].rearrange("p (t n) -> p t n", t=TT)).then_inc(acc_free[bl.n % 2], 1)
            bl.n += 1
            norm_parts(xh, xl)
            own(dve.memset(zero[:, :], 0.0))
            mine()
            consume(8)
            dve.wait_ge(chunk_used, n.n)
            dve.tensor_copy(qc[:, :, :].rearrange("p a b -> p (a b)"), acc[bl.n % 2][:, :]).then_inc(acc_free[bl.n % 2], 1)
            bl.n += 1

            def out3(u):
                dve.wait_ge(o_hi, HEADS1 + N_SELF - N_DIFF + u + 1)
                dve.tensor_tensor(xl[:, u, :], ps[u % 2][:, 0:S], xh[:, u, :], ALU.subtract).then_inc(o_lo, 1)

            attend(2, lambda u: zero, lambda u: HEAD_SCALE, out3)
            for b in range(4):
                consume(2)
                dve.wait_ge(chunk_used, n.n)
                add_block(slice(b * 512, b * 512 + 512))
            h_done()
            norm_rows(h, hs, hs[:, 1, :])
            norm_parts(xh, xl)
            own(dve.memset(gpad[:, :, 0:2], 0.0))
            mine()
            ff = Count()
            cs = Count()

            def hidden2(t0, hi, lo):
                consume(8)
                dve.wait_ge(g_ready, ff.at(1))

                def tap(k, t):
                    c = V_CONV2 + k * FF_T
                    if isinstance(t0, int):
                        return vec[:, c + t0 + t:c + t0 + t + 1]
                    return vec[:, bass.ds(t0 + (c + t), 1)]

                if ff.i is not None or ff.n:
                    dve.wait_ge(af_ready, ff.at())
                for t in range(2):
                    dve.tensor_scalar(cv[:, t, :], gpad[:, t, 2:2 + S], tap(2, t), tap(3, t), ALU.mult, ALU.add).then_inc(conv2, 1)
                    cs.n += 1
                for k in (1, 0):
                    dve.wait_ge(conv2, cs.at())
                    for t in range(2):
                        o = dve.scalar_tensor_tensor(cv[:, t, :], gpad[:, t, k:k + S], tap(k, t), cv[:, t, :], ALU.mult, ALU.add)
                        if k:
                            o.then_inc(conv2, 1)
                            cs.n += 1
                o.then_inc(cv_ready, 1)
                dve.wait_ge(sil2, ff.at(1))
                if ff.i is not None or ff.n:
                    dve.wait_ge(a_hi, ff.at())
                    dve.wait_ge(a_lo, ff.at())
                dve.tensor_tensor(af[:, :, :], cv[:, :, :], acc[bl.n % 2][:, 512:1024].rearrange("p (a b) -> p a b", a=2),
                                  ALU.mult).then_inc(af_ready, 1)
                dve.wait_ge(a_hi, ff.at(1))
                dve.tensor_tensor(lo, af[:, :, :], hi, ALU.subtract).then_inc(a_lo, 1)
                dve.sem_inc(acc_free[bl.n % 2], 1)
                bl.n += 1
                ff.n += 1

            with dve.Fori(0, FF_T // 4 - 1) as j:
                for c, k in ((n, 16), (bl, 2), (ff, 2), (cs, 8)):
                    c.enter(j, k)
                for b in range(2):
                    t4 = bass.ds(j * 4 + 2 * b, 2)
                    hidden2(j * 4 + 2 * b, ah[:, t4, :], al[:, t4, :])
                for c in (n, bl, ff, cs):
                    c.leave(FF_T // 4 - 1)
            hidden2(FA - 2, ah[:, FA - 2:FA, :], al[:, FA - 2:FA, :])
            hidden2(FA, xh[:, 0:2, :], xl[:, 0:2, :])
            for b in range(4):
                consume(FF_T // 2)
                dve.wait_ge(chunk_used, n.n)
                add_block(slice(b * 512, b * 512 + 512))
            h_done()
            own(dve.tensor_tensor_reduce(hs[:, 1, :], h[:, 1, :], h[:, 1, :], 1.0, 0.0, ALU.mult, ALU.add, ss[:, 1:2]))
            mine()
            mean_inv(7)
            dve.wait_ge(n_rstd, 8)
            dve.wait_ge(gf_in, 16)
            for t in range(TT):
                dve.scalar_tensor_tensor(h[:, t, :], h[:, t, :], rstd[:, t:t + 1], gfin[:, :], ALU.mult, ALU.mult)\
                   .then_inc(fin_ready, 1)


LAM_INIT = 0.8 - 0.6 * math.exp(-0.3 * 0)
_BLOCKS = 10 + 4 + 5 * N_EXPERTS + 4 + 4
PLE_END = ((_BLOCKS + 1) // 2, _BLOCKS // 2)


def _bucket(d):
    if d < 16:
        return max(d, 0)
    return min(16 + int(math.log(d / 16) / math.log(2048 / 16) * 16), 31)


def _constants():
    c = {}
    c["ident"] = np.eye(P, dtype=np.float32)
    c["flip"] = np.ascontiguousarray(np.eye(P, dtype=np.float32)[::-1])
    q, j = np.arange(P)[:, None], np.arange(S)[None, :]
    c["causal"] = np.where(j - P > q, np.float32(NEG), np.float32(0)).astype(np.float32)
    neg = np.zeros((P, HEADS1, P), np.float32)
    for u in range(HEADS1):
        neg[u, u, :] = -1.0
    c["negsel"] = neg
    dist = 255 - np.arange(384)
    onehot = np.zeros((32, 384), np.float32)
    for m, d in enumerate(dist):
        onehot[_bucket(int(d)), m] = 1.0
    c["onehot"] = onehot
    scale = np.array([DIFF_SCALE] * N_DIFF + [HEAD_SCALE] * (N_MOBA + N_DIL), np.float64)
    c["iscale"] = (1.0 / scale).astype(np.float32)[:, None]
    addend = np.zeros((N_SELF, 384), np.float64)
    branches = (dist <= 128).astype(int) + (dist % 4 == 0) + (dist % 16 == 0)
    addend[N_DIFF + N_MOBA:] = np.where(branches > 0, np.log(np.maximum(branches, 1)), NEG) / HEAD_SCALE
    addend[:, dist < 0] = NEG
    c["addend"] = np.maximum(addend, NEG).astype(np.float32)
    c["desc"] = np.broadcast_to(np.arange(N_EXPERTS, 0, -1, dtype=np.float32), (P, TT, N_EXPERTS))
    c["desc4"] = np.broadcast_to(np.arange(N_GROUPS, 0, -1, dtype=np.float32), (P, TT, N_GROUPS))
    return c


_WHOLE = ["x", "w_in", "w_rec_gate", "w_in_gate", "w_out", "w_expert_gate", "w_expert_up", "w_expert_down", "w_ple_gate",
          "w_ple_up", "mem_2", "w_in_2", "w_out_2", "diff_lambda_2", "rel_bias_table_2", "w_cq_2", "w_ckv_2", "w_co_2",
          "w_up_2", "w_down_2", "g_final_2"]


def kernel(**inputs):
    import numpy as _np
    import concourse.bacc as _bacc
    from concourse import mybir as _mybir
    from concourse.bass_utils import run_bass_kernel_spmd as _run

    a = {k: _np.asarray(v) for k, v in inputs.items()}
    arrays = {name: _np.ascontiguousarray(a[name]) for name in _WHOLE}

    def tiles(x):
        return x.reshape(-1, P).T

    forget = _np.zeros((P, 1), _np.float32)
    forget[:HEADS1, 0] = a["b_forget"][0]
    arrays["vec"] = _np.concatenate(
        [tiles(a[k]) for k in ("mix_norm", "ffn_norm", "ple_norm", "g_mix_2", "g_mem_2", "g_cross_2", "g_ffn_2",
                               "conv_w", "conv_b", "b_rec_gate", "b_in_gate", "lru_lambda", "q_norm", "k_norm",
                               "diff_subln_2")] + [forget] + [tiles(a["conv_w_2"]), tiles(a["conv_b_2"])], axis=1)

    def rows(x):
        return x.reshape(KT, P, -1).transpose(1, 0, 2).reshape(P, -1)

    arrays["w_f"] = rows(a["w_in"][0][:, COL_F:COL_F + HEADS1])
    arrays["w_router"] = rows(_np.concatenate([a["w_router_group"][0], a["w_router_expert"][0]], axis=1))
    arrays["pT"] = a["p"][0, 0].T.reshape(2, P, S).transpose(1, 0, 2)
    arrays.update(_constants())
    arrays = {k: _np.ascontiguousarray(v) for k, v in arrays.items()}

    nc = _bacc.Bacc("TRN2", target_bir_lowering=False, num_devices=1)
    aps = {k: nc.dram_tensor(f"in_{k}", v.shape, _mybir.dt.from_np(v.dtype), kind="ExternalInput").ap()
           for k, v in arrays.items()}
    out = nc.dram_tensor("out_0", (1, S, D), _mybir.dt.from_np(_np.dtype("float32")), kind="ExternalOutput").ap()
    program(nc, aps, out)
    r = _run(nc, [{f"in_{k}": v for k, v in arrays.items()}], core_ids=[0])
    return r.results[0]["out_0"]
```

```python
import math
from contextlib import ExitStack

import numpy as np
import concourse.bass as bass
from concourse import mybir

F32 = mybir.dt.float32
F32R = mybir.dt.float32r
BF16 = mybir.dt.bfloat16
I32 = mybir.dt.int32
ALU = mybir.AluOpType
ACT = mybir.ActivationFunctionType
AX_X = mybir.AxisListType.X

P = 128
S = 256
TT = S // P
D = 2048
KT = D // P
HEADS1 = 8
RNN_T = 8
N_GROUPS, PER_GROUP = 4, 8
N_EXPERTS = N_GROUPS * PER_GROUP
D_EXPERT = 256
D_PLE = 256
N_DIFF, N_MOBA, N_DIL = 6, 4, 6
N_SELF = N_DIFF + N_MOBA + N_DIL
N_MEM_HEADS = 4
D_FF = 5632
FF_T = D_FF // P
EPS = 1e-6
NEG = -1e30
LRU_C = 8.0
COL_F = 3072
COL_RX = 3080
N_ROUTER = N_GROUPS + N_EXPERTS
SLOTS = 64
PAIRS = N_EXPERTS // 2
OV_PE, OV_ACT, OV_DVE = 10, 1, 9
OV_X = KT // 2
MAX_OVER = 7

CHUNK = 1024
RING = 8
AHEAD = 4
N_CHUNKS = 2 * (40 + 16 + 6 * N_EXPERTS + 2 + 16 + 48 + 16 + 8 + 4 + 4 + 88 + 44)

V_GAIN = 0
V_CONV = 7 * KT
V_BREC, V_BIN, V_LAM = V_CONV + 5 * RNN_T, V_CONV + 6 * RNN_T, V_CONV + 7 * RNN_T
V_QN = V_CONV + 8 * RNN_T
V_KN, V_SUB, V_BF = V_QN + 1, V_QN + 2, V_QN + 3
V_CONV2 = V_QN + 4
N_VEC = V_CONV2 + 4 * FF_T

DIFF_SCALE = 64 ** -0.5
HEAD_SCALE = 128 ** -0.5


class Count:

    def __init__(self):
        self.n, self.i, self.per = 0, None, 0

    def enter(self, i, per, start=0):
        self.i, self.per, self.first, self.start = i, per, self.n, start

    def leave(self, turns):
        assert self.n - self.first == self.per, (self.n - self.first, self.per)
        self.n, self.i = self.first + turns * self.per, None

    def at(self, k=0, div=1, mul=1):
        v = (self.n + k) // div * mul
        if self.i is None:
            return v
        assert self.per % div == 0
        turn = self.per // div * mul
        return self.i * turn + (v - self.start * turn)


def program(nc, I, out):
    ctx = ExitStack()
    with ctx:
        def sb(name, shape, dt=F32):
            return ctx.enter_context(nc.sbuf_tensor(name, shape, dt))

        def sem(name):
            return ctx.enter_context(nc.semaphore(name))

        whi = sb("whi", [P, RING, CHUNK], F32R)
        h = sb("h", [P, TT, D])
        xh = sb("xh", [P, KT, S], F32R)
        xl = sb("xl", [P, KT, S], F32R)
        vec = sb("vec", [P, N_VEC])
        ident = sb("ident", [P, P])
        mean = sb("mean", [P, P])
        eps = sb("eps", [P, 1])
        lam = sb("lam", [P, 8])
        ss = sb("ss", [P, TT])
        rms = sb("rms", [P, TT])
        warm = sb("warm", [P, 8])
        rstd = sb("rstd", [P, TT])
        sp8 = sb("sp8", [P, RNN_T])
        lru_t = sb("lru_t", [P, 6, RNN_T])
        qg = sb("qg", [P, 2])
        stat = sb("stat", [P, 2, 4])
        rsum = sb("rsum", [P, 2, 2])

        base = (nc.sbuf_base + 31) // 32 * 32
        size = (nc.sbuf_usable_end - base) // 32 * 32 - 64

        def at(name, kb, shape, dt=F32):
            off = int(kb * 1024)
            assert off + (2 if dt == BF16 else 4) * int(np.prod(shape[1:])) <= size, (name, off, shape, size)
            return nc.alloc_sbuf_tensor_at(name, shape, dt, offset=base + off)

        raw = at("raw", 0, [P, RING, CHUNK])
        wlo = at("wlo", 0, [P, RING, CHUNK], F32R)
        ring_size = RING * CHUNK * 4
        base, size = base + ring_size, size - ring_size

        hs = at("hs", 0, [P, TT, D])
        diag = at("diag", 91.5, [P, TT, P])
        qk1 = at("qk1", 0, [P, 16, S])
        sq1 = at("sq1", 16, [P, 16, S])
        v1 = at("v1", 16, [P, TT, 1024])
        rxp = at("rxp", 32, [P, RNN_T, 4 + S])
        a_t = at("a_t", 32, [P, RNN_T, S])
        rxc = at("rxc", 41, [P, RNN_T, S])
        gel = at("gel", 49, [P, RNN_T, S])
        r_t = at("r_t", 57, [P, RNN_T, S])
        i_t = at("i_t", 65, [P, RNN_T, S])
        w_rec = at("w_rec", 73, [P, RNN_T, P])
        w_ing = at("w_ing", 77, [P, RNN_T, P])
        negsel = at("negsel", 81, [P, HEADS1, P])
        causal = at("causal", 85, [P, S])
        c_cum = at("c_cum", 86, [P, S])
        f_raw = at("f_raw", 87, [P, KT * 8 + 120])
        f_hi = at("f_hi", 88, [P, KT * 8 + 120], F32R)
        f_lo = at("f_lo", 89, [P, KT * 8 + 120], F32R)
        rst1 = at("rst1", 65, [P, 2, 512])
        den = at("den", 76, [P, 2, 512])
        z_f = at("z_f", 69, [8, S])
        z_n = at("z_n", 70, [8, S])
        z_y = at("z_y", 71, [8, S])
        z_z = at("z_z", 72, [8, S])
        z_q = at("z_q", 57, [8, S])
        z_s = at("z_s", 58, [8, S])
        z_1 = at("z_1", 59, [8, S])
        t1 = [at("sneg1", 57, [P, 2, 512]), at("e1", 61, [P, 2, 512]), at("pt1", 65, [P, 2, 512])]
        rt_raw = at("rt_raw", 73, [P, KT * N_ROUTER + 92])
        rt_hi = at("rt_hi", 76, [P, KT * N_ROUTER + 92], F32R)
        rt_lo = at("rt_lo", 79, [P, KT * N_ROUTER + 92], F32R)
        lgT = at("lgT", 16, [P, S])
        lg = at("lg", 17, [P, TT, N_ROUTER])
        comb = at("comb", 18, [P, TT, N_EXPERTS])
        oh1 = at("oh1", 18.5, [P, TT, N_EXPERTS])
        oh2 = at("oh2", 19, [P, TT, N_EXPERTS])
        em = at("em", 19.5, [P, TT, N_EXPERTS])
        key = at("key", 20, [P, TT, N_EXPERTS])
        desc = at("desc", 20.5, [P, TT, N_EXPERTS])
        desc4 = at("desc4", 21, [P, TT, N_GROUPS])
        g_sh = at("g_sh", 21.25, [P, TT, N_GROUPS])
        g_e = at("g_e", 21.5, [P, TT, N_GROUPS])
        g_oh = at("g_oh", 21.75, [P, TT, N_GROUPS])
        g_key = at("g_key", 22, [P, TT, N_GROUPS])
        r_s = at("r_s", 22.25, [P, 12, TT])
        xs = at("xs", 33, [P, TT, D])
        xb = at("xb", 49, [P, 3, TT, D], BF16)
        g_row = at("g_row", 82, [P, D])
        ident_b = at("ident_b", 90, [P, P], BF16)
        ones_b = at("ones_b", 90.25, [P, P], BF16)
        tri_b = at("tri_b", 90.5, [P, P], BF16)
        tri = at("tri", 23, [P, P])
        iota = at("iota", 90.75, [P, SLOTS])
        G = at("G", 23, [P, TT, N_EXPERTS * SLOTS], BF16)
        GT = at("GT", 31, [P, S], F32R)
        taken = at("taken", 22.625, [P, TT, N_EXPERTS], BF16)
        pos = at("pos", 91, [P, TT, N_EXPERTS])
        combo = at("combo", 91.25, [P, TT, N_EXPERTS])
        c3 = at("c3", 19, [P, 3, TT, N_EXPERTS], BF16)
        c_rest = at("c_rest", 20, [P, TT, N_EXPERTS])
        w_slot = at("w_slot", 20.5, [P, PAIRS])
        w_now = at("w_now", 22.75, [P, 1])
        over = at("over", 21, [P, 4, N_EXPERTS])
        over_eq = at("over_eq", 33, [P, MAX_OVER + 1, N_EXPERTS])
        over_f = at("over_f", 21.5, [P, MAX_OVER + 2])
        over_i = at("over_i", 21.75, [P, MAX_OVER + 2], I32)
        yh = at("yh", 0, [P, D], F32R)
        yl = at("yl", 8, [P, D], F32R)
        sg = at("sg", 33, [P, 2, 256])
        hid = at("hid", 35, [P, 2, 256])
        hid_h = at("hid_h", 37, [P, 2, 256], F32R)
        hid_l = at("hid_l", 39, [P, 2, 256], F32R)
        xT = at("xT", 0, [P, KT, S])
        ov_w = at("ov_w", 49, [P, KT, 256])
        upb = at("upb", 73, [P, TT, D])
        pT = at("pT", 24, [P, 2, S])
        pT_h = at("pT_h", 26, [P, 2, S], F32R)
        pT_l = at("pT_l", 28, [P, 2, S], F32R)
        gate = at("gate", 65, [P, 2, 1024])
        qk2 = at("qk2", 0, [P, 32, S])
        v2 = at("v2", 32, [P, TT, N_SELF * P])
        bias = at("bias", 48, [P, N_SELF, S])
        hank = at("hank", 64, [P, N_SELF, S])
        flip = at("flip", 88, [P, P])
        mem = at("mem", 64, [P, TT, D])
        t2 = [at("sneg2", 80, [P, 2, 512]), at("e2", 84, [P, 2, 512]), at("pt2", 88, [P, 2, 512])]
        junk_a = at("junk_a", 80, [P, D])
        junk_v = at("junk_v", 48, [P, D])
        rst2 = at("rst2", 80, [P, 2, 512])
        tab = at("tab", 16, [32, N_SELF])
        onehot = at("onehot", 17, [32, 384])
        addend = at("addend", 19, [N_SELF, 384])
        iscale = at("iscale", 21, [N_SELF, 1])
        frev = at("frev", 22, [N_SELF, 384])
        lamv = at("lamv", 24, [P, 4, 64])
        lamj = at("lamj", 25, [P, 2, 64])
        memh = at("memh", 0, [P, KT, S], F32R)
        meml = at("meml", 16, [P, KT, S], F32R)
        km = at("km", 32, [P, N_MEM_HEADS, S])
        vm = at("vm", 36, [P, TT, 512])
        qc = at("qc", 40, [P, N_MEM_HEADS, S])
        zero = at("zero", 44, [P, S])
        junk_c = at("junk_c", 48, [P, TT, D])
        FA = FF_T - 2
        ah = at("ah", 0, [P, FA, S], F32R)
        al = at("al", FA, [P, FA, S], F32R)
        gpad = at("gpad", 2 * FA, [P, 2, 2 + S])
        cv = at("cv", 2 * FA + 2.0625, [P, 2, S])
        af = at("af", 2 * FA + 4.0625, [P, 2, S])
        gfin = at("gfin", 2 * FA, [P, D])

        acc = [ctx.enter_context(nc.psum_tensor(f"acc{b}", [P, 1024], F32)) for b in range(2)]
        tp = [ctx.enter_context(nc.psum_tensor(f"tp{b}", [P, 512], F32)) for b in range(2)]
        ps = [ctx.enter_context(nc.psum_tensor(f"ps{b}", [P, 512], F32)) for b in range(2)]
        score = [acc[b][:, k * 512:(k + 1) * 512] for b in range(2) for k in range(2)]

        frev_d = nc.dram_tensor("frev_d", (N_SELF, 384), F32, kind="Internal").ap()

        raw_in = [sem(f"raw_in{r}") for r in range(RING)]
        hi_ready, lo_ready = sem("hi_ready"), sem("lo_ready")
        chunk_used = sem("chunk_used")
        acc_free = [sem(f"acc_free{b}") for b in range(2)]
        act_step, dve_step = sem("act_step"), sem("dve_step")
        x_in, vec_in, ident_in = sem("x_in"), sem("vec_in"), sem("ident_in")
        small_in, lam_in, gates_in, late_in = sem("small_in"), sem("lam_in"), sem("gates_in"), sem("late_in")
        consts = sem("consts")
        n_ss0, n_ss1, n_rms = sem("n_ss0"), sem("n_ss1"), sem("n_rms")
        n_inv, n_diag, n_rows = sem("n_inv"), sem("n_diag"), sem("n_rows")
        n_tp, n_hi, n_lo = sem("n_tp"), sem("n_hi"), sem("n_lo")
        lam_y, lam_dot, lam_e = sem("lam_y"), sem("lam_dot"), sem("lam_e")
        f_split, f_done, f_z, f_y, f_abs, c_ready = (sem(n) for n in
                                                     ("f_split", "f_done", "f_z", "f_y", "f_abs", "c_ready"))
        conv_done, gate_mm, gate_read = sem("conv_done"), sem("gate_mm"), sem("gate_read")
        la_ready, a_ready, lru_q, lru_root, gel_ready = (sem(n) for n in
                                                         ("la_ready", "a_ready", "lru_q", "lru_root", "gel_ready"))
        sq_ready, ms_mm, ms_root, qk_ready = sem("sq_ready"), sem("ms_mm"), sem("ms_root"), sem("qk_ready")
        rnn_ready, rnn_hi, rnn_lo = sem("rnn_ready"), sem("rnn_hi"), sem("rnn_lo")
        s_mm, s_max, s_exp, p_ready = sem("s_mm"), sem("s_max"), sem("s_exp"), sem("p_ready")
        pt_mm, pt_copy, o_mm, o_hi, o_lo = sem("pt_mm"), sem("pt_copy"), sem("o_mm"), sem("o_hi"), sem("o_lo")
        o_sq = sem("o_sq")
        rt_in, rt_split, rt_mm, rt_copy, rt_tp, rt_read, rt_e = (sem(n) for n in
                                                                 ("rt_in", "rt_split", "rt_mm", "rt_copy", "rt_tp", "rt_read", "rt_e"))
        silu_ready, hid_ready, hid_lo = sem("silu_ready"), sem("hid_ready"), sem("hid_lo")
        moe_in, xs_ready, xa_ready, xr_ready, xb_ready, xc_ready = (sem(n) for n in (
            "moe_in", "xs_ready", "xa_ready", "xr_ready", "xb_ready", "xc_ready"))
        taken_ready, rank_mm, slots_ready = sem("taken_ready"), sem("rank_mm"), sem("slots_ready")
        t_done, t_hi, t_read = sem("t_done"), sem("t_hi"), sem("t_read")
        w_ready, y_hi, y_ready = sem("w_ready"), sem("y_hi"), sem("y_ready")
        ov_list, ov_in, ov_pe, ov_act, ov_dve = (sem(n) for n in ("ov_list", "ov_in", "ov_pe", "ov_act", "ov_dve"))
        p_in, pT_ready, gate_ready = sem("p_in"), sem("pT_ready"), sem("gate_ready")
        b_mm, b_f, b_out, b_in, b_flip, b_copy = (sem(n) for n in ("b_mm", "b_f", "b_out", "b_in", "b_flip", "b_copy"))
        mem_in, km_ready, vm_ready, qc_ready = sem("mem_in"), sem("km_ready"), sem("vm_ready"), sem("qc_ready")
        g_ready, cv_ready, sil2, af_ready, a_hi, a_lo = (sem(n) for n in
                                                         ("g_ready", "cv_ready", "sil2", "af_ready", "a_hi", "a_lo"))
        rt_pad = sem("rt_pad")
        ple_prod, conv2 = sem("ple_prod"), sem("conv2")
        gf_in, fin_ready, out_done = sem("gf_in"), sem("fin_ready"), sem("out_done")

        block = ctx.enter_context(nc.Block())

        def col(c, n=1):
            return vec[:, c:c + n]

        def rows4(w):
            return w.rearrange("(ko p) n -> p ko n", p=P)

        @block.sync
        def _(sp):
            n = Count()

            def load(pieces):
                r = n.n % RING
                if n.n >= RING:
                    sp.wait_ge(chunk_used, n.at(1 - RING))
                for dst, src in pieces(r):
                    sp.dma_start(dst, src).then_inc(raw_in[r], 16)
                n.n += 1

            def two_tiles(r):
                return raw[:, r, :].rearrange("p (k n) -> p k n", k=2)

            def k2(w, kt, cols):
                return lambda r: [(two_tiles(r)[:, j:j + 1, :], w[:, one(kt, j), cols]) for j in range(2)]

            def two(wa, ca, wb, cb, kt):
                k = slice(kt, kt + 2) if isinstance(kt, int) else bass.ds(kt, 2)
                return lambda r: [(two_tiles(r)[:, :, 0:256], wa[:, k, ca]), (two_tiles(r)[:, :, 256:512], wb[:, k, cb])]

            def one(kt, j):
                return slice(kt + j, kt + j + 1) if isinstance(kt, int) else bass.ds(kt + j, 1)

            for t in range(TT):
                sp.dma_start(h[:, t, :], I["x"][0, t * P:(t + 1) * P, :]).then_inc(x_in, 16)
            w_in = rows4(I["w_in"][0])
            for c in range(RING):
                load(k2(w_in, 2 * c, slice(COL_RX, COL_RX + 512)))
            for c0, first in ((COL_RX, 1), (0, 0)):
                with sp.Fori(first, 4) as j:
                    n.enter(j, 8, first)
                    for c in range(8):
                        load(k2(w_in, 2 * c, bass.ds(j * 512 + c0, 512)))
                    n.leave(4 - first)
            for c0 in (2048, 2560):
                for c in range(8):
                    load(k2(w_in, 2 * c, slice(c0, c0 + 512)))
            w_out = rows4(I["w_out"][0])
            with sp.Fori(0, 4) as j:
                n.enter(j, 8)
                for c in range(8):
                    load(k2(w_out, 2 * c, bass.ds(j * 512, 512)))
                n.leave(4)
            w_pu = rows4(I["w_ple_up"][0])
            for c in range(D // 512):
                load(k2(w_pu, 0, slice(c * 512, c * 512 + 512)))
            wg = I["w_expert_gate"][0].rearrange("e (ko p) n -> p (e ko) n", p=P)
            wu = I["w_expert_up"][0].rearrange("e (ko p) n -> p (e ko) n", p=P)
            wd = I["w_expert_down"][0].rearrange("e (ko p) n -> p (e ko) n", p=P)

            def gate_up(e):
                for c in range(8):
                    load(two(wg, slice(0, 256), wu, slice(0, 256), e * KT + 2 * c))

            def down(e):
                for c in range(4):
                    load(k2(wd, e * 2, slice(c * 512, c * 512 + 512)))

            with sp.Fori(0, PAIRS) as i:
                n.enter(i, 24)
                gate_up(i * 2)
                gate_up(i * 2 + 1)
                down(i * 2)
                down(i * 2 + 1)
                n.leave(PAIRS)
            w_pg = rows4(I["w_ple_gate"][0])
            for c in range(8):
                load(k2(w_pg, 2 * c, slice(0, 512)))
            sp.wait_ge(ov_list, 1)
            count = sp.value_load(over_i[0:1, 0:1], min_val=0, max_val=MAX_OVER)
            with sp.If(count > 0):
                with sp.Fori(0, count) as i:
                    ex = sp.value_load(over_i[0:1, bass.ds(i + 1, 1)], min_val=0, max_val=N_EXPERTS - 1)
                    sp.wait_ge(ov_pe, i * OV_PE + OV_X)
                    sp.dma_start(ov_w[:, :, :], wg[:, bass.ds(ex * KT, KT), :]).then_inc(ov_in, 16)
                    sp.wait_ge(ov_pe, i * OV_PE + (OV_X + 1))
                    sp.dma_start(ov_w[:, :, :], wu[:, bass.ds(ex * KT, KT), :]).then_inc(ov_in, 16)
                    sp.wait_ge(ov_pe, i * OV_PE + (OV_X + 2))
                    sp.dma_start(ov_w.rearrange("p a b -> p (a b)").rearrange("p (k n) -> p k n", k=2),
                                 wd[:, bass.ds(ex * 2, 2), :]).then_inc(ov_in, 16)
            with sp.Fori(1, 4) as j:
                n.enter(j, 8, 1)
                for c in range(8):
                    load(k2(w_pg, 2 * c, bass.ds(j * 512, 512)))
                n.leave(3)
            w_in2 = rows4(I["w_in_2"][0])
            for c0, blocks in ((0, 3), (2304, 2), (3840, 3)):
                with sp.Fori(0, blocks) as j:
                    n.enter(j, 8)
                    for c in range(8):
                        load(k2(w_in2, 2 * c, bass.ds(j * 512 + c0, 512)))
                    n.leave(blocks)
            for ca, cb in ((1536, 1792), (2048, 5376), (3328, 3584), (5632, 5888)):
                for c in range(8):
                    load(two(w_in2, slice(ca, ca + 256), w_in2, slice(cb, cb + 256), 2 * c))
            w_out2 = rows4(I["w_out_2"][0])
            for j in range(4):
                for c in range(8):
                    load(k2(w_out2, (2 * c + N_DIFF) % KT, slice(j * 512, j * 512 + 512)))
            w_ckv = rows4(I["w_ckv_2"][0])
            with sp.Fori(0, 2) as j:
                n.enter(j, 8)
                for c in range(8):
                    load(k2(w_ckv, 2 * c, bass.ds(j * 512, 512)))
                n.leave(2)
            w_cq = rows4(I["w_cq_2"][0])
            for c in range(8):
                load(k2(w_cq, 2 * c, slice(0, 512)))
            w_co = rows4(I["w_co_2"][0])
            for j in range(4):
                for c in range(2):
                    load(k2(w_co, 2 * c, slice(j * 512, j * 512 + 512)))
            w_up = rows4(I["w_up_2"][0])
            with sp.Fori(0, FF_T // 2) as j:
                n.enter(j, 8)
                for c in range(8):
                    load(two(w_up, bass.ds(j * 256, 256), w_up, bass.ds(j * 256 + D_FF, 256), 2 * c))
                n.leave(FF_T // 2)
            w_dn = rows4(I["w_down_2"][0])
            for j in range(4):
                for c in range(FF_T // 2):
                    load(k2(w_dn, 2 * c, slice(j * 512, j * 512 + 512)))
            assert n.n == N_CHUNKS
            for t in range(TT):
                sp.wait_ge(fin_ready, t + 1)
                sp.dma_start(out[0, t * P:(t + 1) * P, :], h[:, t, :]).then_inc(out_done, 16)
            sp.wait_ge(out_done, 32)

        @block.gpsimd
        def _(pool):
            pool.dma_start(vec[:, :], I["vec"]).then_inc(vec_in, 16)
            pool.dma_start(ident[:, :], I["ident"]).then_inc(ident_in, 16)
            pool.dma_start(lamv[:, :, :], I["diff_lambda_2"].broadcast_to((P, 4, 64))).then_inc(lam_in, 16)
            pool.dma_start(tab[:, :], I["rel_bias_table_2"]).then_inc(small_in, 16)
            pool.dma_start(onehot[:, :], I["onehot"]).then_inc(small_in, 16)
            pool.dma_start(addend[:, :], I["addend"]).then_inc(small_in, 16)
            pool.dma_start(iscale[:, :], I["iscale"]).then_inc(small_in, 16)
            pool.dma_start(w_rec[:, :, :], I["w_rec_gate"][0].rearrange("n i j -> i n j")).then_inc(gates_in, 16)
            pool.dma_start(w_ing[:, :, :], I["w_in_gate"][0].rearrange("n i j -> i n j")).then_inc(gates_in, 16)
            pool.wait_ge(consts, 1)
            pool.dma_start(f_raw[:, 0:KT * 8], I["w_f"]).then_inc(late_in, 16)
            pool.dma_start(negsel[:, :, :], I["negsel"]).then_inc(late_in, 16)
            pool.dma_start(causal[:, :], I["causal"]).then_inc(late_in, 16)
            pool.wait_ge(b_f, 1)
            pool.dma_start(frev_d, frev[:, :]).then_inc(b_out, 16)
            pool.wait_ge(gate_mm, RNN_T)
            pool.memset(rt_raw[:, KT * N_ROUTER:], 0.0).then_inc(rt_pad, 1)
            pool.dma_start(rt_raw[:, 0:KT * N_ROUTER], I["w_router"]).then_inc(rt_in, 16)
            pool.wait_ge(o_lo, HEADS1)
            pool.wait_ge(rnn_lo, 1)
            pool.dma_start(pT[:, :, :], I["pT"]).then_inc(p_in, 16)
            pool.dma_start(desc[:, :, :], I["desc"]).then_inc(moe_in, 16)
            pool.dma_start(desc4[:, :, :], I["desc4"]).then_inc(moe_in, 16)
            pool.dma_start(tri[:, :], I["tri"]).then_inc(moe_in, 16)
            pool.dma_start(iota[:, :], I["iota"]).then_inc(moe_in, 16)
            pool.dma_start(g_row[:, :], I["ffn_norm"].broadcast_to((P, D))).then_inc(moe_in, 16)
            pool.wait_ge(moe_in, 80)
            for t in range(TT):
                pool.wait_ge(n_rows, t + 1)
                pool.tensor_tensor(xs[:, t, :], hs[:, t, :], g_row[:, :], ALU.mult).then_inc(xs_ready, 1)
            for t in range(TT):
                pool.wait_ge(xb_ready, t + 1)
                pool.tensor_tensor(xb[:, 2, t, :], xs[:, t, :], xb[:, 1, t, :], ALU.subtract).then_inc(xc_ready, 1)
            pool.wait_ge(b_out, 16)
            pool.wait_ge(acc_free[0], PLE_END[0])
            pool.wait_ge(acc_free[1], PLE_END[1])
            diagonals = bass.AP(tensor=frev_d.tensor, offset=0, ap=[[1, P], [384, N_SELF], [1, S]])
            pool.dma_start(hank[:, :, :], diagonals).then_inc(b_in, 16)
            pool.dma_start(flip[:, :], I["flip"]).then_inc(b_in, 16)
            pool.wait_ge(b_copy, 8)
            for t in range(TT):
                pool.dma_start(mem[:, t, :], I["mem_2"][0, t * P:(t + 1) * P, :]).then_inc(mem_in, 16)
            pool.wait_ge(af_ready, FF_T // 2)
            pool.wait_ge(a_lo, FF_T // 2)
            pool.wait_ge(a_hi, FF_T // 2)
            pool.dma_start(gfin[:, :], I["g_final_2"].rearrange("(a n) -> a n", a=1).broadcast_to((P, D))).then_inc(gf_in, 16)

        V_TILE = [0, 1, 2, 3, 4, 5] + [8, 9, 10, 11] + [6, 7, 12, 13, 14, 15]
        comps2 = [2] * N_DIFF + [1] * (N_MOBA + N_DIL)
        M1 = HEADS1
        M2 = sum(comps2)

        def operands2(u, c):
            if u < N_DIFF:
                part = slice(64 * c, 64 * c + 64)
                return qk2[part, u, :], qk2[part, N_DIFF + u, :]
            if u < N_DIFF + N_MOBA:
                return qk2[:, 12 + u - N_DIFF, :], qk2[:, 16 + u - N_DIFF, :]
            v = u - N_DIFF - N_MOBA
            return qk2[:, 20 + v, :], qk2[:, 26 + v, :]

        AT = [dict(units=HEADS1, comps=[1] * HEADS1, causal=True, m0=0, u0=0, t=t1),
              dict(units=N_SELF, comps=comps2, causal=True, m0=M1, u0=HEADS1, t=t2),
              dict(units=N_MEM_HEADS, comps=[1] * N_MEM_HEADS, causal=False, m0=M1 + M2, u0=HEADS1 + N_SELF, t=t2)]

        def spans(at_):
            if at_["causal"]:
                return [(0, P, P), (P, P + S, 0)]
            return [(0, S, 0), (S, 2 * S, 0)]

        def prob_tiles(A):
            if A["causal"]:
                return [(0, P, 0), (P, 2 * P, 0), (2 * P, 3 * P, 0)]
            return [(0, P, 0), (S, S + P, 0), (P, S, 0), (S + P, 2 * S, 0)]

        GU, DN = 8, 4

        def steps_after(c, first, last):
            steps = []
            if 2 <= c < 10 and not first:
                steps.append(("scatter", c - 2))
            if c == 4 and first:
                steps.append(("weights", 0))
            if c in (11, 17):
                steps.append(("transpose", 0 if c == 11 else 1))
            if c in (15, 16, 18, 19) and not last:
                steps.append(("gather", (15, 16, 18, 19).index(c)))
            return steps

        def pair_rows(q):
            return slice(q * SLOTS, (q + 1) * SLOTS)

        def pair_cols(g):
            return slice(g * P, g * P + P) if isinstance(g, int) else bass.ds(g * P, P)

        xg_h, xg_l = (w.rearrange("p k s -> p (k s)")[:, 0:KT * P] for w in (xh, xl))
        USES = 4 + 7 + 14 * (PAIRS - 2) + 10 + 8

        @block.tensor
        def _(pe):
            n, bl = Count(), Count()
            norms = Count()

            def three(o, wh, wl, ah_, al_, first, last, weights_stationary):
                pairs = ((wh, ah_), (wh, al_), (wl, ah_))
                if not weights_stationary:
                    pairs = ((wh, ah_), (wl, ah_), (wh, al_))
                for j, (w, a) in enumerate(pairs):
                    lhsT, rhs = (w, a) if weights_stationary else (a, w)
                    mm = pe.matmul(o, lhsT, rhs, start=first and j == 0, stop=last and j == 2, skip_group_check=True)
                return mm

            def take():
                b = bl.n % 2
                if bl.i is not None or bl.n >= 2:
                    pe.wait_ge(acc_free[b], bl.at(0, 2))
                bl.n += 1
                return acc[b]

            def chunk():
                pe.wait_ge(lo_ready, n.at(1))
                s = n.n % RING
                n.n += 1
                return tuple(w[:, s, :].rearrange("p (k n) -> p k n", k=2) for w in (whi, wlo))

            def features(ah_, al_, before=None):
                o = take()
                for c in range(KT // 2):
                    if before:
                        before(c)
                    wh, wl = chunk()
                    for k in range(2):
                        for ct in range(4):
                            w = slice(ct * P, ct * P + P)
                            mm = three(o[:, ct * S:(ct + 1) * S], wh[:, k, w], wl[:, k, w], ah_[:, 2 * c + k, :],
                                       al_[:, 2 * c + k, :], c == 0 and k == 0 and ct % 2 == 0, c == KT // 2 - 1 and k == 1, True)
                    mm.then_inc(chunk_used, 1)

            def tokens(operand, chunks=KT // 2, before=None):
                o = take()
                for c in range(chunks):
                    if before:
                        before(c)
                    wh, wl = chunk()
                    for k in range(2):
                        xh_, xl_ = operand(2 * c + k)
                        for t in range(TT):
                            q = slice(t * P, t * P + P)
                            mm = three(o[:, t * 512:(t + 1) * 512], wh[:, k, :], wl[:, k, :], xh_[:, q], xl_[:, q],
                                       c == 0 and k == 0, c == chunks - 1 and k == 1, False)
                    mm.then_inc(chunk_used, 1)

            def current(k):
                return xh[:, k, :], xl[:, k, :]

            def norm_step(src, k, g):
                if g == 0:
                    pe.wait_ge(n_diag, k + 1)
                if 8 * k + g >= 2:
                    pe.wait_ge(n_lo, 8 * k + g - 1)
                for j in range(2):
                    f = slice((2 * g + j) * P, (2 * g + j + 1) * P)
                    for t in range(TT):
                        mm = pe.matmul(tp[g % 2][:, j * S + t * P:j * S + t * P + P], src[:, t, f], diag[:, t, :],
                                       start=True, stop=True, skip_group_check=True)
                mm.then_inc(n_tp, 1)

            def norm(src):
                for g in range(KT // 2):
                    norm_step(src, norms.n, g)
                norms.n += 1

            def normed(k):
                pe.wait_ge(n_lo, 8 * (k + 1))

            def leading(src):
                k = norms.n
                norms.n += 1

                def before(c):
                    for g in ((0, 1) if c == 0 else (2 * c, 2 * c + 1) if c < 4 else ()):
                        norm_step(src, k, g)
                    pe.wait_ge(n_lo, 8 * k + c + 1)
                return before

            def attend(a, operands, values, scores_extra=None):
                A = AT[a]
                comps, N = A["comps"], A["units"]
                first = [sum(comps[:u]) for u in range(N)]
                for s in range(N + 2):
                    if s < N:
                        for c in range(comps[s]):
                            m = A["m0"] + first[s] + c
                            if m >= 4:
                                pe.wait_ge(s_max, m - 3)
                            q, k = operands(s, c)
                            o = score[m % 4]
                            for t, (c0, c1, _) in enumerate(spans(A)):
                                w = c1 - c0
                                mm = pe.matmul(o[:, c0:c1], q[:, t * P:t * P + P], k[:, 0:w], start=True,
                                               stop=scores_extra is None, skip_group_check=True)
                                if scores_extra:
                                    mm = scores_extra(s, o[:, c0:c1], w)
                            mm.then_inc(s_mm, 1)
                    if 1 <= s <= N:
                        u = s - 1
                        pe.wait_ge(p_ready, A["u0"] + u + 1)
                        if A["u0"] + u >= 2:
                            pe.wait_ge(pt_copy, A["u0"] + u - 1)
                        e = A["t"][1][:, u % 2, :]
                        for j, (c0, c1, _) in enumerate(prob_tiles(A)):
                            mm = pe.transpose(tp[u % 2][:, j * P:j * P + P], e[:, c0:c1], ident[:, :])
                        mm.then_inc(pt_mm, 1)
                    if s >= 2:
                        u = s - 2
                        pe.wait_ge(pt_copy, A["u0"] + u + 1)
                        if A["u0"] + u >= 2:
                            pe.wait_ge(o_lo, A["u0"] + u - 1)
                        pt = A["t"][2][:, u % 2, :]
                        v = values(u)
                        o = ps[u % 2]
                        if A["causal"]:
                            pe.matmul(o[:, 0:S], v(0), pt[:, 0:S], start=True, stop=False, skip_group_check=True)
                            mm = pe.matmul(o[:, P:S], v(1), pt[:, S:S + P], start=False, stop=True, skip_group_check=True)
                        else:
                            pe.matmul(o[:, 0:S], v(0), pt[:, 0:S], start=True, stop=False, skip_group_check=True)
                            mm = pe.matmul(o[:, 0:S], v(1), pt[:, S:2 * S], start=False, stop=True, skip_group_check=True)
                        mm.then_inc(o_mm, 1)

            pe.wait_ge(ident_in, 16)
            features(xh, xl, leading(h))
            pe.wait_ge(small_in, 64)
            pe.matmul(ps[0][0:N_SELF, 0:384], tab[:, :], onehot[:, :], start=True, stop=True).then_inc(b_mm, 1)
            features(xh, xl)
            with pe.Fori(1, 2) as j:
                n.enter(j, 16, 1)
                bl.enter(j, 2, 1)
                for _ in range(2):
                    features(xh, xl)
                n.leave(1)
                bl.leave(1)
            pe.wait_ge(gates_in, 32)
            pe.wait_ge(conv_done, 2)
            pe.wait_ge(b_f, 1)
            for t in range(RNN_T):
                if t >= 2:
                    pe.wait_ge(gate_read, t - 1)
                pe.matmul(ps[t % 2][:, 0:S], w_rec[:, t, :], rxc[:, t, :], start=True, stop=True, skip_group_check=True)
                pe.matmul(ps[t % 2][:, S:2 * S], w_ing[:, t, :], rxc[:, t, :], start=True, stop=True,
                          skip_group_check=True).then_inc(gate_mm, 1)
            with pe.Fori(0, 2) as j:
                n.enter(j, 16)
                bl.enter(j, 2)
                for _ in range(2):
                    features(xh, xl)
                n.leave(2)
                bl.leave(2)
            pe.wait_ge(f_split, 1)
            for k in range(KT):
                mm = three(tp[0][:, 0:S], f_hi[:, k * 8:k * 8 + P], f_lo[:, k * 8:k * 8 + P], xh[:, k, :], xl[:, k, :],
                           k == 0, k == KT - 1, True)
            mm.then_inc(f_done, 1)
            pe.wait_ge(gate_read, RNN_T)

            def qk_mean(g):
                pe.wait_ge(sq_ready, g // 2 + 1)
                if g >= 2:
                    pe.wait_ge(ms_root, g - 1)
                pe.matmul(ps[g % 2][:, :], mean[:, :], sq1[:, 2 * g:2 * g + 2, :].rearrange("p a b -> p (a b)"),
                          start=True, stop=True).then_inc(ms_mm, 1)

            tokens(current, before=qk_mean)
            tokens(current)
            pe.wait_ge(qk_ready, 8)
            pe.wait_ge(c_ready, 1)
            pe.wait_ge(late_in, 48)

            def minus_c(u, o, w):
                return pe.matmul(o, negsel[:, u, :], c_cum[:, 0:w], start=False, stop=True, skip_group_check=True)

            for b in range(2):
                pe.wait_ge(acc_free[b], bl.n // 2)
            attend(0, lambda u, c: (qk1[:, u, :], qk1[:, HEADS1 + u, :]),
                   lambda u: lambda kt: v1[:, kt, u * P:u * P + P], minus_c)
            pe.wait_ge(o_lo, HEADS1)
            pe.wait_ge(rnn_lo, 1)
            with pe.Fori(0, 2) as j:
                n.enter(j, 16)
                bl.enter(j, 2)
                for _ in range(2):
                    tokens(current)
                n.leave(2)
                bl.leave(2)
            before = leading(h)
            pe.wait_ge(rt_split, 1)
            for k in range(KT):
                if k % 2 == 0:
                    before(k // 2)
                w = slice(k * N_ROUTER, k * N_ROUTER + P)
                mm = three(ps[0][:, 0:S], rt_hi[:, w], rt_lo[:, w], xh[:, k, :], xl[:, k, :], k == 0, k == KT - 1, True)
            mm.then_inc(rt_mm, 1)
            pe.wait_ge(rt_copy, 1)
            for t in range(TT):
                mm = pe.transpose(ps[1][:, t * P:t * P + P], lgT[:, t * P:t * P + P], ident[:, :])
            mm.then_inc(rt_tp, 1)
            pe.wait_ge(pT_ready, 1)
            for _ in range(4):
                tokens(lambda k: (pT_h[:, k, :], pT_l[:, k, :]), 1)
            pe.wait_ge(taken_ready, 1)
            pe.matmul(ps[0][:, 0:32], tri_b[:, :], taken[:, 0, :], start=True, stop=True, skip_group_check=True)
            pe.matmul(ps[0][:, 32:64], ones_b[:, :], taken[:, 0, :], start=True, stop=False, skip_group_check=True)
            pe.matmul(ps[0][:, 32:64], tri_b[:, :], taken[:, 1, :], start=False, stop=True, skip_group_check=True)
            pe.matmul(ps[0][:, 64:96], ones_b[:, :], taken[:, 0, :], start=True, stop=False, skip_group_check=True)
            pe.matmul(ps[0][:, 64:96], ones_b[:, :], taken[:, 1, :], start=False, stop=True,
                      skip_group_check=True).then_inc(rank_mm, 1)
            tu, hv = Count(), Count()

            def use():
                if tu.i is not None or tu.n >= 2:
                    pe.wait_ge(t_read, tu.at(-1))
                tu.n += 1
                return tp[(tu.n - 1) % 2]

            def gather(g, k):
                o = use()
                for j in range(4):
                    f = slice((4 * k + j) * P, (4 * k + j + 1) * P)
                    for m in range(3 * TT):
                        mm = pe.matmul(o[:, j * P:(j + 1) * P], xb[:, m // TT, m % TT, f], G[:, m % TT, pair_cols(g)],
                                       start=m == 0, stop=m == 3 * TT - 1, skip_group_check=True)
                mm.then_inc(t_done, 1)

            def scatter(k):
                pe.wait_ge(y_ready, hv.at(k // 4 - 1))
                o = use()
                q = slice(k % 2 * P, k % 2 * P + P)
                cs = slice(k // 2 * 512, k // 2 * 512 + 512)
                pe.matmul(o[:, :], GT[:, q], yh[:, cs], start=True, stop=False, skip_group_check=True)
                pe.matmul(o[:, :], GT[:, q], yl[:, cs], start=False, stop=True, skip_group_check=True).then_inc(t_done, 1)

            def transpose(g, q):
                pe.wait_ge(hid_ready, hv.at(q + 1))
                o = use()
                for k in range(2):
                    mm = pe.transpose(o[:, k * P:(k + 1) * P], hid[:, q, k * P:(k + 1) * P], ident[:, :])
                if q == 0:
                    for t in range(TT):
                        mm = pe.matmul(o[:, S + t * P:S + (t + 1) * P], G[:, t, pair_cols(g)], ident_b[:, :], start=True,
                                       stop=True, skip_group_check=True)
                mm.then_inc(t_done, 1)

            def weights():
                o = use()
                for g in range(PAIRS):
                    for m in range(3 * TT):
                        mm = pe.matmul(o[:, 2 * g:2 * g + 2], G[:, m % TT, pair_cols(g)], c3[:, m // TT, m % TT, 2 * g:2 * g + 2],
                                       start=m == 0, stop=m == 3 * TT - 1, skip_group_check=True)
                mm.then_inc(t_done, 1)

            def pair(g, first=False, last=False):
                for c in range(2 * GU + 2 * DN):
                    if c < 2 * GU:
                        q, kc = c // GU, c % GU
                        if c == 0:
                            pe.wait_ge(t_read, tu.at())
                        if kc == 0 and not first:
                            pe.wait_ge(hid_ready, hv.at(q - 1))
                        wh, wl = chunk()
                        for k in range(2):
                            f = slice((2 * kc + k) * P, (2 * kc + k + 1) * P)
                            mm = three(ps[q][:, :], wh[:, k, :], wl[:, k, :], xg_h[:, f], xg_l[:, f], kc == 0 and k == 0,
                                       kc == GU - 1 and k == 1, False)
                    else:
                        q, b = (c - 2 * GU) // DN, (c - 2 * GU) % DN
                        if b == 0:
                            pe.wait_ge(hid_lo, hv.at(q + 1))
                        if q == 0 and b % 2 == 0:
                            if first:
                                pe.wait_ge(acc_free[b // 2], bl.n // 2)
                            else:
                                pe.wait_ge(y_ready, hv.at(b // 2 - 1))
                        wh, wl = chunk()
                        o = acc[b // 2][:, b % 2 * 512:b % 2 * 512 + 512]
                        for k in range(2):
                            f = slice(k * P, (k + 1) * P)
                            mm = three(o, wh[:, k, :], wl[:, k, :], hid_h[:, q, f], hid_l[:, q, f], q == 0 and k == 0,
                                       q == 1 and k == 1, False)
                    mm.then_inc(chunk_used, 1)
                    for step, k in steps_after(c, first, last):
                        if step == "scatter":
                            scatter(k)
                        elif step == "gather":
                            gather(g + 1, k)
                        elif step == "transpose":
                            transpose(g, k)
                        else:
                            weights()
                hv.n += 2

            pe.wait_ge(slots_ready, 1)
            pe.wait_ge(xc_ready, TT)
            for k in range(4):
                gather(0, k)
            pair(0, first=True)
            with pe.Fori(1, PAIRS - 1) as i:
                n.enter(i, 24, 1)
                tu.enter(i, 14, 1)
                hv.enter(i, 2, 1)
                pair(i)
                for c in (n, tu, hv):
                    c.leave(PAIRS - 2)
            pair(PAIRS - 1, last=True)
            for k in range(8):
                scatter(k)
            assert tu.n == USES
            pe.wait_ge(y_ready, 2 * PAIRS)
            pe.wait_ge(t_read, USES)
            pe.wait_ge(ov_list, 1)
            count = pe.value_load(over_i[0:1, 0:1], min_val=0, max_val=MAX_OVER)
            with pe.If(count > 0):
                for k in range(KT // 2):
                    if k >= 2:
                        pe.wait_ge(ov_act, k - 1)
                    for j in range(2):
                        f = slice((2 * k + j) * P, (2 * k + j + 1) * P)
                        for t in range(TT):
                            for m in range(3):
                                mm = pe.matmul(tp[k % 2][:, j * S + t * P:j * S + (t + 1) * P], xb[:, m, t, f], ident_b[:, :],
                                               start=m == 0, stop=m == 2, skip_group_check=True)
                    mm.then_inc(ov_pe, 1)
                pe.wait_ge(ov_act, KT // 2)
                with pe.Fori(0, count) as i:
                    for m in range(2):
                        pe.wait_ge(ov_in, i * 48 + (16 * m + 16))
                        for ht in range(2):
                            for k in range(KT):
                                mm = pe.matmul(ps[m][:, ht * S:(ht + 1) * S], ov_w[:, k, ht * P:(ht + 1) * P], xT[:, k, :],
                                               start=k == 0, stop=k == KT - 1, skip_group_check=True)
                        mm.then_inc(ov_pe, 1)
                    pe.wait_ge(ov_in, i * 48 + 48)
                    pe.wait_ge(ov_dve, i * OV_DVE + 1)
                    w2 = ov_w.rearrange("p a b -> p (a b)")
                    hid_t = hid.rearrange("p a b -> p (a b)")
                    for k in range(8):
                        if k >= 2:
                            pe.wait_ge(ov_dve, i * OV_DVE + k)
                        for m in range(2):
                            mm = pe.matmul(acc[0][:, k % 2 * 512:k % 2 * 512 + 512],
                                           hid_t[:, m * S + k % 2 * P:m * S + k % 2 * P + P],
                                           w2[:, m * D + k // 2 * 512:m * D + k // 2 * 512 + 512], start=m == 0, stop=m == 1,
                                           skip_group_check=True)
                        mm.then_inc(ov_pe, 1)
                    pe.wait_ge(ov_dve, i * OV_DVE + OV_DVE)
            tokens(current, before=leading(h))
            tokens(current)
            with pe.Fori(1, 2) as j:
                n.enter(j, 16, 1)
                bl.enter(j, 2, 1)
                for _ in range(2):
                    tokens(current)
                n.leave(1)
                bl.leave(1)
            features(xh, xl, leading(h))
            features(xh, xl)
            with pe.Fori(1, 4) as j:
                n.enter(j, 16, 1)
                bl.enter(j, 2, 1)
                for _ in range(2):
                    features(xh, xl)
                n.leave(3)
                bl.leave(3)
            pe.wait_ge(b_in, 32)
            for g in range(8):
                if g >= 2:
                    pe.wait_ge(b_copy, g - 1)
                else:
                    pe.wait_ge(rt_read, 1)
                pe.matmul(ps[g % 2][:, :], flip[:, :], hank[:, 2 * g:2 * g + 2, :].rearrange("p a b -> p (a b)"),
                          start=True, stop=True).then_inc(b_flip, 1)
            with pe.Fori(0, 2) as j:
                n.enter(j, 16)
                bl.enter(j, 2)
                for _ in range(2):
                    tokens(current)
                n.leave(2)
                bl.leave(2)
            pe.wait_ge(b_copy, 8)
            for b in range(2):
                pe.wait_ge(acc_free[b], bl.n // 2)
            attend(1, operands2, lambda u: lambda kt: v2[:, kt, V_TILE[u] * P:V_TILE[u] * P + P])
            pe.wait_ge(o_sq, N_DIFF)
            pe.wait_ge(o_lo, HEADS1 + N_SELF)

            def diff_mean(c):
                if c < N_DIFF // 2:
                    if c >= 2:
                        pe.wait_ge(ms_root, 8 + c - 1)
                    pe.matmul(ps[c % 2][:, :], mean[:, :], qk2[:, N_DIFF + 2 * c:N_DIFF + 2 * c + 2, :].rearrange("p a b -> p (a b)"),
                              start=True, stop=True).then_inc(ms_mm, 1)
                if 2 * c == KT - N_DIFF:
                    pe.wait_ge(rnn_lo, 2)

            def mixed(k):
                return current((k + N_DIFF) % KT)

            tokens(mixed, before=diff_mean)
            tokens(mixed)
            norm(mem)
            for _ in range(2):
                tokens(mixed)
            normed(4)
            features(memh, meml)
            tokens(lambda k: (memh[:, k, :], meml[:, k, :]))
            features(xh, xl, leading(h))
            for b in range(2):
                pe.wait_ge(acc_free[b], (bl.n + 1 - b) // 2)
            attend(2, lambda u, c: (qc[:, u, :], km[:, u, :]), lambda u: lambda kt: vm[:, kt, u * P:u * P + P])
            pe.wait_ge(o_lo, HEADS1 + N_SELF + N_MEM_HEADS)
            for _ in range(4):
                tokens(current, 2)
            features(xh, xl, leading(h))
            features(xh, xl)
            with pe.Fori(1, FF_T // 4) as j:
                n.enter(j, 16, 1)
                bl.enter(j, 2, 1)
                for _ in range(2):
                    features(xh, xl)
                n.leave(FF_T // 4 - 1)
                bl.leave(FF_T // 4 - 1)
            pe.wait_ge(a_lo, FF_T // 2)

            def ff(k):
                if k < FA:
                    return ah[:, k, :], al[:, k, :]
                return xh[:, k - FA, :], xl[:, k - FA, :]

            for _ in range(4):
                tokens(ff, FF_T // 2)
            assert n.n == N_CHUNKS

        @block.scalar
        def _(act):
            n = Count()
            bl = Count()
            steps = Count()
            norms = Count()
            hv = Count()

            def split(k):
                m = n.n + k
                if n.i is None and m >= N_CHUNKS:
                    return
                act.wait_ge(raw_in[m % RING], n.at(k, RING, 32) + 32)
                if n.i is not None or m >= RING:
                    act.wait_ge(chunk_used, n.at(k + 1 - RING))
                act.activation(whi[:, m % RING, :], raw[:, m % RING, :], ACT.Copy).then_inc(hi_ready, 1)

            def consume(k):
                for _ in range(k):
                    split(AHEAD)
                    n.n += 1

            def own(ins):
                ins.then_inc(act_step, 1)
                steps.n += 1

            def h_done():
                act.wait_ge(acc_free[0], (bl.n + 1) // 2)
                act.wait_ge(acc_free[1], bl.n // 2)

            def norm_rows(src, junk, ready):
                k = norms.n
                act.activation(warm[:, k:k + 1], eps[:, 0:1], ACT.Sqrt)
                ready()
                act.activation(junk, src[:, 0, :], ACT.Square, accum_out=ss[:, 0:1]).then_inc(n_ss0, 1)
                act.wait_ge(n_ss1, k + 1)
                act.wait_ge(n_ss0, k + 1)
                act.activation(rms[:, :], ss[:, :], ACT.Sqrt, bias=eps[:, 0:1], scale=1.0 / D).then_inc(n_rms, 1)

            def norm_parts(hi):
                k = norms.n
                norms.n += 1
                for g in range(KT // 2):
                    act.wait_ge(n_tp, 8 * k + g + 1)
                    for j in range(2):
                        kt = 2 * g + j
                        o = act.activation(hi[:, kt, :], tp[g % 2][:, j * S:(j + 1) * S], ACT.Copy,
                                           scale=col(V_GAIN + k * KT + kt))
                    o.then_inc(n_hi, 1)

            def attend(a, outputs):
                A = AT[a]
                comps, N = A["comps"], A["units"]
                first = [sum(comps[:u]) for u in range(N)]
                sneg, e, pt = A["t"]
                for s in range(N + 3):
                    if s < N:
                        for c in range(comps[s]):
                            m = A["m0"] + first[s] + c
                            act.wait_ge(s_max, m + 1)
                            if c == 0 and s >= 2:
                                act.wait_ge(pt_mm, A["u0"] + s - 1)
                            dst = e[:, s % 2, :] if c == 0 else sneg[:, m % 2, :]
                            for t, (c0, c1, _) in enumerate(spans(A)):
                                o = act.activation(dst[:, c0:c1], sneg[:, m % 2, c0:c1], ACT.Exp,
                                                   bias=stat[:, m % 2, t:t + 1], scale=-1.0,
                                                   accum_out=stat[:, m % 2, 2 + t:3 + t])
                            o.then_inc(s_exp, 1)
                    if 1 <= s <= N:
                        u = s - 1
                        w = len(prob_tiles(A)) * P
                        act.wait_ge(pt_mm, A["u0"] + u + 1)
                        if u >= 2:
                            act.wait_ge(o_mm, A["u0"] + u - 1)
                        act.activation(pt[:, u % 2, 0:w], tp[u % 2][:, 0:w], ACT.Copy).then_inc(pt_copy, 1)
                    if 2 <= s <= N + 1:
                        outputs(s - 2)

            act.wait_ge(vec_in, 16)
            act.wait_ge(consts, 1)
            norm_rows(h, hs[:, 0, :], lambda: act.wait_ge(x_in, 32))
            for k in range(AHEAD):
                split(k)
            norm_parts(xh)
            consume(6)
            act.wait_ge(lam_y, 1)
            act.activation(lru_t[:, 1, :], lru_t[:, 0, :], ACT.Exp, scale=-1.0).then_inc(lam_e, 1)
            act.wait_ge(lam_dot, 2)
            act.activation(lam[:, 2:4], lam[:, 0:2], ACT.Exp).then_inc(lam_e, 1)
            act.wait_ge(late_in, 48)
            act.activation(f_hi[:, :], f_raw[:, :], ACT.Copy).then_inc(f_z, 1)
            consume(10)
            bl.n += 2
            for b in range(2):
                consume(8)
                act.wait_ge(chunk_used, n.n)
                act.activation(gel[:, 4 * b:4 * b + 4, :].rearrange("p a b -> p (a b)"), acc[bl.n % 2][:, :],
                               ACT.Gelu_apprx_tanh).then_inc(acc_free[bl.n % 2], 1)
                bl.n += 1
            for t in range(RNN_T):
                act.wait_ge(gate_mm, t + 1)
                act.activation(r_t[:, t, :], ps[t % 2][:, 0:S], ACT.Sigmoid, bias=col(V_BREC + t))
                act.activation(i_t[:, t, :], ps[t % 2][:, S:2 * S], ACT.Sigmoid, bias=col(V_BIN + t)).then_inc(gate_read, 1)
            act.wait_ge(b_out, 16)
            for b in range(4):
                two_t = slice(2 * b, 2 * b + 2)
                consume(4)
                act.wait_ge(la_ready, b + 1)
                act.activation(a_t[:, two_t, :], r_t[:, two_t, :], ACT.Exp, scale=-1.0)
                act.activation(r_t[:, two_t, :], r_t[:, two_t, :], ACT.Tanh).then_inc(a_ready, 1)
                consume(4)
                act.wait_ge(lru_q, b + 1)
                act.activation(r_t[:, two_t, :], r_t[:, two_t, :], ACT.Sqrt).then_inc(lru_root, 1)
                act.wait_ge(acc_free[bl.n % 2], bl.n // 2 + 1)
                act.activation(sq1[:, 4 * b:4 * b + 4, :], qk1[:, 4 * b:4 * b + 4, :], ACT.Square).then_inc(sq_ready, 1)
                bl.n += 1
            act.wait_ge(f_done, 1)
            act.wait_ge(rnn_ready, 4)
            act.activation(z_f[:, :], tp[0][0:8, 0:S], ACT.Identity, bias=vec[0:8, V_BF:V_BF + 1]).then_inc(f_z, 1)
            act.wait_ge(f_abs, 1)
            act.activation(z_y[:, :], z_n[:, :], ACT.Exp, scale=-1.0).then_inc(f_y, 1)
            for g in range(8):
                consume(1)
                act.wait_ge(ms_mm, g + 1)
                if g >= 2:
                    act.wait_ge(qk_ready, g - 1)
                act.activation(rst1[:, g % 2, :], ps[g % 2][:, :], ACT.Sqrt, bias=eps[:, 0:1]).then_inc(ms_root, 1)
            consume(8)
            bl.n += 2
            act.wait_ge(rnn_ready, 4)
            act.wait_ge(chunk_used, n.n)
            act.activation(xh[:, HEADS1:KT, :], gel[:, :, :], ACT.Copy).then_inc(rnn_hi, 1)

            def out1(u):
                act.wait_ge(o_mm, u + 1)
                act.activation(xh[:, u, :], ps[u % 2][:, 0:S], ACT.Copy).then_inc(o_hi, 1)

            attend(0, out1)
            with act.Fori(0, 4) as j:
                n.enter(j, 8)
                consume(8)
                n.leave(4)
            bl.n += 4
            act.wait_ge(rt_in, 16)
            act.wait_ge(rt_pad, 1)
            norm_rows(h, hs[:, 0, :], h_done)
            act.activation(rt_hi[:, :], rt_raw[:, :], ACT.Copy).then_inc(rt_e, 1)
            act.wait_ge(p_in, 16)
            act.activation(pT_h[:, :, :], pT[:, :, :], ACT.Copy).then_inc(rt_e, 1)
            norm_parts(xh)
            for t in range(TT):
                act.wait_ge(xs_ready, t + 1)
                act.activation(xb[:, 0, t, :], xs[:, t, :], ACT.Copy).then_inc(xa_ready, 1)
            act.wait_ge(rt_mm, 1)
            act.activation(lgT[:, :], ps[0][:, 0:S], ACT.Copy).then_inc(rt_copy, 1)
            for t in range(TT):
                act.wait_ge(xr_ready, t + 1)
                act.activation(xb[:, 1, t, :], xs[:, t, :], ACT.Copy).then_inc(xb_ready, 1)
            def embedded(b):
                act.wait_ge(chunk_used, n.n + 1)
                act.activation(upb[:, :, b * 512:(b + 1) * 512], acc[bl.n % 2][:, :].rearrange("p (t n) -> p t n", t=TT),
                               ACT.Copy).then_inc(acc_free[bl.n % 2], 1)
                bl.n += 1
                consume(1)

            embedded(0)
            embedded(1)
            act.wait_ge(rt_read, 2)
            act.activation(g_e[:, :, :], g_sh[:, :, :], ACT.Exp).then_inc(rt_e, 1)
            act.wait_ge(rt_read, 3)
            act.activation(r_s[:, 7, :], r_s[:, 6, :], ACT.Exp).then_inc(rt_e, 1)
            embedded(2)
            embedded(3)

            tu, th, hv = Count(), Count(), Count()

            def read_high(dst):
                act.wait_ge(t_done, tu.at(1))
                act.activation(dst, tp[tu.n % 2][:, 0:dst.shape[-1]], ACT.Copy).then_inc(t_hi, 1)
                tu.n += 1
                th.n += 1

            def gathered(k):
                read_high(xg_h[:, k * 512:k * 512 + 512])

            def pair(g, first=False, last=False):
                for c in range(2 * GU + 2 * DN):
                    consume(1)
                    if c in (GU - 1, 2 * GU - 1):
                        q = c // GU
                        act.wait_ge(chunk_used, n.at())
                        if not first:
                            act.wait_ge(hid_ready, hv.at(q - 1))
                        r = pair_rows(q)
                        act.activation(sg[r, q, :], ps[q][r, 0:256], ACT.Silu).then_inc(silu_ready, 1)
                    for step, k in steps_after(c, first, last):
                        if step == "gather":
                            gathered(k)
                        elif step == "transpose":
                            read_high(hid_h[:, k, :])
                        else:
                            tu.n += 1
                            if step == "weights":
                                act.wait_ge(t_read, tu.at())
                    if c in (2 * GU + DN + 1, 2 * GU + 2 * DN - 1):
                        b = (c - 2 * GU - DN) // 2
                        act.wait_ge(w_ready, hv.at(2, 2))
                        act.wait_ge(chunk_used, n.at())
                        act.activation(yh[:, b * 1024:(b + 1) * 1024], acc[b][:, :], ACT.Copy, scale=w_now[:, :]).then_inc(y_hi, 1)
                hv.n += 2

            for k in range(4):
                gathered(k)
            pair(0, first=True)
            with act.Fori(1, PAIRS - 1) as i:
                for c, k in ((n, 24), (tu, 14), (th, 6), (hv, 2)):
                    c.enter(i, k, 1)
                pair(i)
                for c in (n, tu, th, hv):
                    c.leave(PAIRS - 2)
            pair(PAIRS - 1, last=True)
            act.wait_ge(t_read, USES)
            act.wait_ge(ov_list, 1)
            count = act.value_load(over_i[0:1, 0:1], min_val=0, max_val=MAX_OVER)
            with act.If(count > 0):
                for k in range(KT // 2):
                    act.wait_ge(ov_pe, k + 1)
                    act.activation(xT[:, 2 * k:2 * k + 2, :].rearrange("p a b -> p (a b)"), tp[k % 2][:, :],
                                   ACT.Copy).then_inc(ov_act, 1)
                with act.Fori(0, count) as i:
                    act.wait_ge(ov_pe, i * OV_PE + (OV_X + 1))
                    act.activation(sg.rearrange("p a b -> p (a b)"), ps[0][:, :], ACT.Silu).then_inc(ov_act, 1)
                    act.wait_ge(ov_dve, i * OV_DVE + OV_DVE)
            norm_rows(h, hs[:, 0, :], h_done)
            norm_parts(xh)
            gt = Count()
            with act.Fori(0, 2) as j:
                n.enter(j, 16)
                bl.enter(j, 2)
                gt.enter(j, 2)
                for b in range(2):
                    consume(8)
                    act.wait_ge(chunk_used, n.at())
                    act.wait_ge(acc_free[b], bl.at(0, 2))
                    act.activation(gate[:, b, :], acc[bl.n % 2][:, :], ACT.Sigmoid).then_inc(gate_ready, 1)
                    bl.n += 1
                    gt.n += 1
                for c in (n, bl, gt):
                    c.leave(2)
            norm_rows(h, hs[:, 0, :], h_done)
            norm_parts(xh)
            with act.Fori(0, 8) as j:
                n.enter(j, 8)
                consume(8)
                n.leave(8)
            for g in range(8):
                act.wait_ge(b_flip, g + 1)
                act.activation(bias[:, 2 * g:2 * g + 2, :].rearrange("p a b -> p (a b)"), ps[g % 2][:, :],
                               ACT.Copy).then_inc(b_copy, 1)
            with act.Fori(0, 4) as j:
                n.enter(j, 8)
                consume(8)
                n.leave(4)
            bl.n += 12

            def out2(u):
                act.wait_ge(o_mm, HEADS1 + u + 1)
                if u < N_DIFF:
                    act.wait_ge(o_lo, HEADS1 + u + 1)
                    act.activation(qk2[:, N_DIFF + u, :], qk2[:, u, :], ACT.Square).then_inc(o_sq, 1)
                else:
                    act.activation(xh[:, u, :], ps[u % 2][:, 0:S], ACT.Copy).then_inc(o_hi, 1)

            attend(1, out2)
            for g in range(N_DIFF // 2):
                act.wait_ge(ms_mm, 8 + g + 1)
                if g >= 2:
                    act.wait_ge(qk_ready, 8 + g - 1)
                act.activation(rst2[:, g % 2, :], ps[g % 2][:, :], ACT.Sqrt, bias=eps[:, 0:1]).then_inc(ms_root, 1)
            act.wait_ge(qk_ready, 8 + N_DIFF // 2)
            act.activation(xh[:, 0:N_DIFF, :], qk2[:, 0:N_DIFF, :], ACT.Copy).then_inc(rnn_hi, 1)
            consume(8)

            def memory():
                act.wait_ge(mem_in, 32)
                act.wait_ge(rnn_lo, 2)

            norm_rows(mem, junk_a[:, :], memory)
            consume(8)
            bl.n += 2
            norm_parts(memh)
            consume(16)
            bl.n += 2
            norm_rows(h, junk_c[:, 0, :], h_done)
            consume(16)
            bl.n += 2
            norm_parts(xh)
            consume(8)
            bl.n += 1

            def out3(u):
                act.wait_ge(o_mm, HEADS1 + N_SELF + u + 1)
                act.activation(xh[:, u, :], ps[u % 2][:, 0:S], ACT.Copy).then_inc(o_hi, 1)

            attend(2, out3)
            consume(8)
            bl.n += 4
            norm_rows(h, hs[:, 0, :], h_done)
            norm_parts(xh)
            ff = Count()

            def hidden2(dst):
                consume(8)
                act.wait_ge(chunk_used, n.at())
                if ff.i is not None or ff.n:
                    act.wait_ge(cv_ready, ff.at())
                act.activation(gpad[:, :, 2:2 + S], acc[bl.n % 2][:, 0:512].rearrange("p (a b) -> p a b", a=2),
                               ACT.Copy).then_inc(g_ready, 1)
                act.wait_ge(cv_ready, ff.at(1))
                act.activation(cv[:, :, :], cv[:, :, :], ACT.Silu).then_inc(sil2, 1)
                act.wait_ge(af_ready, ff.at(1))
                act.activation(dst, af[:, :, :], ACT.Copy).then_inc(a_hi, 1)
                bl.n += 1
                ff.n += 1

            for t in (0, 2):
                hidden2(ah[:, t:t + 2, :])
            with act.Fori(1, FF_T // 4 - 1) as j:
                n.enter(j, 16, 1)
                bl.enter(j, 2, 1)
                ff.enter(j, 2, 1)
                for b in range(2):
                    hidden2(ah[:, bass.ds(j * 4 + 2 * b, 2), :])
                for c in (n, bl, ff):
                    c.leave(FF_T // 4 - 2)
            hidden2(ah[:, FA - 2:FA, :])
            hidden2(xh[:, 0:2, :])
            for b in range(4):
                consume(FF_T // 2)
                bl.n += 1
            assert n.n == N_CHUNKS
            norm_rows(h, hs[:, 0, :], h_done)

        @block.vector
        def _(dve):
            n = Count()
            bl = Count()
            steps = Count()
            norms = Count()
            hv = Count()

            def split(k):
                m = n.n + k
                if n.i is None and m >= N_CHUNKS:
                    return
                dve.wait_ge(hi_ready, n.at(k + 1))
                dve.tensor_tensor(wlo[:, m % RING, :], raw[:, m % RING, :], whi[:, m % RING, :],
                                  ALU.subtract).then_inc(lo_ready, 1)

            def consume(k):
                for _ in range(k):
                    split(AHEAD)
                    n.n += 1

            def own(ins):
                ins.then_inc(dve_step, 1)
                steps.n += 1

            def mine():
                dve.wait_ge(dve_step, steps.at())

            def h_done():
                dve.wait_ge(acc_free[0], (bl.n + 1) // 2)
                dve.wait_ge(acc_free[1], bl.n // 2)

            def norm_rows(src, junk, last=False):
                k = norms.n
                dve.tensor_tensor_reduce(junk, src[:, 1, :], src[:, 1, :], 1.0, 0.0, ALU.mult, ALU.add,
                                         ss[:, 1:2]).then_inc(n_ss1, 1)
                dve.wait_ge(n_rms, k + 1)
                dve.reciprocal(rstd[:, :], rms[:, :]).then_inc(n_inv, 1)
                if not last:
                    dve.wait_ge(n_inv, k + 1)
                    own(dve.tensor_scalar(diag[:, 0, :], ident[:, :], rstd[:, 0:1], None, ALU.mult))
                    own(dve.tensor_scalar(diag[:, 1, :], ident[:, :], rstd[:, 1:2], None, ALU.mult))
                    mine()
                    dve.sem_inc(n_diag, 1)

            def norm_parts(hi, lo):
                k = norms.n
                norms.n += 1
                for g in range(KT // 2):
                    dve.wait_ge(n_hi, 8 * k + g + 1)
                    for j in range(2):
                        kt = 2 * g + j
                        o = dve.scalar_tensor_tensor(lo[:, kt, :], tp[g % 2][:, j * S:(j + 1) * S],
                                                     col(V_GAIN + k * KT + kt), hi[:, kt, :], ALU.mult, ALU.subtract)
                    o.then_inc(n_lo, 1)

            def add_block(cols):
                b = bl.n % 2
                dve.wait_ge(acc_free[1 - b], bl.at(1, 2))
                hh = h[:, :, cols]
                dve.tensor_tensor(hh, acc[b][:, :].rearrange("p (t n) -> p t n", t=TT), hh, ALU.add).then_inc(acc_free[b], 1)
                bl.n += 1

            def log1p(y, z, q, s, r):
                own(dve.tensor_scalar(z, y, 2.0, None, ALU.add))
                mine()
                own(dve.reciprocal(z, z))
                mine()
                own(dve.tensor_tensor(z, y, z, ALU.mult))
                mine()
                own(dve.tensor_tensor(q, z, z, ALU.mult))
                mine()
                own(dve.tensor_scalar(s, q, 1.0 / 17, None, ALU.mult))
                for d in (15, 13, 11, 9, 7, 5, 3):
                    mine()
                    own(dve.scalar_tensor_tensor(s, s, 1.0 / d, q, ALU.add, ALU.mult))
                mine()
                own(dve.scalar_tensor_tensor(s, s, 1.0, z, ALU.add, ALU.mult))
                mine()
                own(dve.tensor_scalar(r, s, 2.0, None, ALU.mult))
                mine()

            def attend(a, bias_of, scale_of, outputs, mix=None):
                A = AT[a]
                comps, N = A["comps"], A["units"]
                first = [sum(comps[:u]) for u in range(N)]
                sneg, e, pt = A["t"]
                for s in range(N + 3):
                    if s < N:
                        for c in range(comps[s]):
                            m = A["m0"] + first[s] + c
                            dve.wait_ge(s_mm, m + 1)
                            if m >= A["m0"] + 2:
                                dve.wait_ge(s_exp, m - 1)
                                mine()
                            if s and comps[s - 1] == 2:
                                dve.wait_ge(p_ready, A["u0"] + s)
                            for t, (c0, c1, b0) in enumerate(spans(A)):
                                o = dve.tensor_tensor_reduce(sneg[:, m % 2, c0:c1], score[m % 4][:, c0:c1],
                                                             bias_of(s)[:, b0:b0 + c1 - c0], -scale_of(s), 3e38,
                                                             ALU.add, ALU.min, stat[:, m % 2, t:t + 1])
                            o.then_inc(s_max, 1)
                        if comps[s] == 2:
                            finish(A, s, first[s], e, sneg)
                    if 1 <= s <= N and comps[s - 1] == 1:
                        finish(A, s - 1, first[s - 1], e, sneg)
                    if 2 <= s <= N + 1:
                        outputs(s - 2)

            def finish(A, u, f, e, sneg):
                two_c = A["comps"][u] == 2
                m = A["m0"] + f
                dve.wait_ge(s_exp, m + (2 if two_c else 1))
                for c in range(2 if two_c else 1):
                    own(dve.reciprocal(rsum[:, (m + c) % 2, :], stat[:, (m + c) % 2, 2:4]))
                mine()
                if two_c:
                    own(dve.tensor_scalar(rsum[:, (m + 1) % 2, :], rsum[:, (m + 1) % 2, :], lam[:, 5:6], None, ALU.mult))
                for t, (c0, c1, _) in enumerate(spans(A)):
                    d = e[:, u % 2, c0:c1]
                    o = dve.tensor_scalar(d, d, rsum[:, m % 2, t:t + 1], None, ALU.mult)
                    if two_c:
                        own(o)
                if two_c:
                    mine()
                    for t, (c0, c1, _) in enumerate(spans(A)):
                        d = e[:, u % 2, c0:c1]
                        o = dve.scalar_tensor_tensor(d, sneg[:, (m + 1) % 2, c0:c1], rsum[:, (m + 1) % 2, t:t + 1], d,
                                                     ALU.mult, ALU.add)
                o.then_inc(p_ready, 1)

            own(dve.memset(eps[:, :], EPS))
            own(dve.memset(mean[:, :], 1.0 / P))
            own(dve.memset(ones_b[:, :], 1.0))
            own(dve.memset(c_cum[:, :], 0.0))
            own(dve.memset(rxp[:, :, 0:4], 0.0))
            dve.memset(f_raw[:, KT * 8:], 0.0).then_inc(consts, 1)
            dve.wait_ge(x_in, 32)
            dve.wait_ge(ident_in, 16)
            norm_rows(h, hs[:, 1, :])
            for k in range(AHEAD):
                split(k)
            norm_parts(xh, xl)
            consume(6)
            dve.wait_ge(lam_in, 16)
            for j in range(2):
                dve.tensor_tensor_reduce(lamj[:, j, :], lamv[:, 2 * j, :], lamv[:, 2 * j + 1, :], 1.0, 0.0, ALU.mult, ALU.add,
                                         lam[:, j:j + 1]).then_inc(lam_dot, 1)
            dve.wait_ge(vec_in, 16)
            own(dve.tensor_scalar(lru_t[:, 0, :], col(V_LAM, RNN_T), -1.0, None, ALU.mult))
            mine()
            dve.tensor_tensor(lru_t[:, 0, :], lru_t[:, 0, :], col(V_LAM, RNN_T), ALU.max).then_inc(lam_y, 1)
            dve.tensor_scalar(qg[:, 0:1], col(V_QN), HEAD_SCALE, None, ALU.mult)
            own(dve.tensor_scalar(qg[:, 1:2], col(V_SUB), 1.0 - LAM_INIT, None, ALU.mult))
            dve.wait_ge(b_mm, 1)
            dve.wait_ge(small_in, 64)
            dve.scalar_tensor_tensor(frev[:, :], ps[0][0:N_SELF, 0:384], iscale[:, 0:1], addend[:, :],
                                     ALU.mult, ALU.add).then_inc(b_f, 1)
            dve.wait_ge(lam_e, 2)
            log1p(lru_t[:, 1, :], lru_t[:, 2, :], lru_t[:, 3, :], lru_t[:, 4, :], lru_t[:, 5, :])
            own(dve.tensor_scalar(lru_t[:, 0, :], col(V_LAM, RNN_T), -1.0, 0.0, ALU.mult, ALU.max))
            mine()
            own(dve.tensor_tensor(lru_t[:, 0, :], lru_t[:, 0, :], lru_t[:, 5, :], ALU.add))
            mine()
            own(dve.tensor_scalar(sp8[:, :], lru_t[:, 0, :], LRU_C, None, ALU.mult))
            own(dve.tensor_tensor(lam[:, 4:5], lam[:, 2:3], lam[:, 3:4], ALU.subtract))
            mine()
            own(dve.tensor_scalar(lam[:, 5:6], lam[:, 4:5], LAM_INIT, -1.0, ALU.add, ALU.mult))
            dve.wait_ge(f_z, 1)
            dve.tensor_tensor(f_lo[:, :], f_raw[:, :], f_hi[:, :], ALU.subtract).then_inc(f_split, 1)
            consume(2)
            for b in range(2):
                if b:
                    consume(8)
                dve.wait_ge(chunk_used, n.n)
                four = range(4 * b, 4 * b + 4)
                dve.tensor_copy(rxp[:, 4 * b:4 * b + 4, 4:4 + S],
                                acc[bl.n % 2][:, :].rearrange("p (a b) -> p a b", a=4)).then_inc(acc_free[bl.n % 2], 1)
                bl.n += 1
                dve.wait_ge(acc_free[b], 1)
                for t in four:
                    own(dve.tensor_scalar(rxc[:, t, :], rxp[:, t, 4:4 + S], col(V_CONV + 3 * RNN_T + t),
                                          col(V_CONV + 4 * RNN_T + t), ALU.mult, ALU.add))
                for tap in (2, 1, 0):
                    mine()
                    for t in four:
                        o = dve.scalar_tensor_tensor(rxc[:, t, :], rxp[:, t, tap + 1:tap + 1 + S],
                                                     col(V_CONV + tap * RNN_T + t), rxc[:, t, :], ALU.mult, ALU.add)
                        if tap:
                            own(o)
                o.then_inc(conv_done, 1)
            consume(16)
            bl.n += 2
            for b in range(4):
                two_t = slice(2 * b, 2 * b + 2)
                consume(2)
                dve.wait_ge(gate_read, RNN_T)
                mine()
                for t in (2 * b, 2 * b + 1):
                    o = dve.tensor_scalar(r_t[:, t, :], r_t[:, t, :], sp8[:, t:t + 1], None, ALU.mult)
                o.then_inc(la_ready, 1)
                consume(2)
                dve.wait_ge(a_ready, b + 1)
                own(dve.tensor_tensor(i_t[:, two_t, :], i_t[:, two_t, :], rxc[:, two_t, :], ALU.mult))
                d = den[:, b % 2, :].rearrange("p (a b) -> p a b", a=2)
                own(dve.tensor_scalar(d, r_t[:, two_t, :], 1.0, None, ALU.add))
                mine()
                own(dve.reciprocal(d, d))
                mine()
                dve.scalar_tensor_tensor(r_t[:, two_t, :], r_t[:, two_t, :], 2.0, d, ALU.mult, ALU.mult).then_inc(lru_q, 1)
                consume(4)
                dve.wait_ge(chunk_used, n.n)
                dve.tensor_copy(qk1[:, 4 * b:4 * b + 4, :].rearrange("p a b -> p (a b)"), acc[bl.n % 2][:, :])\
                   .then_inc(acc_free[bl.n % 2], 1)
                bl.n += 1
                dve.wait_ge(lru_root, b + 1)
                own(dve.tensor_tensor(i_t[:, two_t, :], i_t[:, two_t, :], r_t[:, two_t, :], ALU.mult))
                mine()
                for t in (2 * b, 2 * b + 1):
                    own(dve.tensor_tensor_scan(rxc[:, t, :], a_t[:, t, :], i_t[:, t, :], 0.0, ALU.mult, ALU.add))
                mine()
                dve.tensor_tensor(gel[:, two_t, :], gel[:, two_t, :], rxc[:, two_t, :], ALU.mult).then_inc(rnn_ready, 1)
            dve.wait_ge(f_z, 2)
            own(dve.tensor_scalar(z_n[:, :], z_f[:, :], -1.0, None, ALU.mult))
            mine()
            dve.tensor_tensor(z_n[:, :], z_n[:, :], z_f[:, :], ALU.max).then_inc(f_abs, 1)
            dve.wait_ge(f_y, 1)
            own(dve.memset(z_1[:, :], 1.0))
            log1p(z_y[:, :], z_z[:, :], z_q[:, :], z_s[:, :], z_n[:, :])
            own(dve.scalar_tensor_tensor(z_f[:, :], z_f[:, :], 0.0, z_n[:, :], ALU.min, ALU.subtract))
            mine()
            dve.tensor_tensor_scan(c_cum[0:8, :], z_1[:, :], z_f[:, :], 0.0, ALU.mult, ALU.add).then_inc(c_ready, 1)
            for g in range(8):
                consume(1)
                dve.wait_ge(ms_root, g + 1)
                own(dve.reciprocal(rst1[:, g % 2, :], rst1[:, g % 2, :]))
                mine()
                two_h = qk1[:, 2 * g:2 * g + 2, :].rearrange("p a b -> p (a b)")
                dve.scalar_tensor_tensor(two_h, two_h, qg[:, 0:1] if g < 4 else col(V_KN), rst1[:, g % 2, :],
                                         ALU.mult, ALU.mult).then_inc(qk_ready, 1)
            for b in range(2):
                if b:
                    consume(8)
                dve.wait_ge(chunk_used, n.n)
                dve.tensor_copy(v1[:, :, b * 512:(b + 1) * 512], acc[bl.n % 2][:, :].rearrange("p (t n) -> p t n", t=TT))\
                   .then_inc(acc_free[bl.n % 2], 1)
                bl.n += 1
            dve.wait_ge(rnn_hi, 1)
            dve.tensor_tensor(xl[:, HEADS1:KT, :], gel[:, :, :], xh[:, HEADS1:KT, :], ALU.subtract).then_inc(rnn_lo, 1)

            def out1(u):
                dve.wait_ge(o_hi, u + 1)
                dve.tensor_tensor(xl[:, u, :], ps[u % 2][:, 0:S], xh[:, u, :], ALU.subtract).then_inc(o_lo, 1)

            dve.wait_ge(late_in, 48)
            attend(0, lambda u: causal, lambda u: 1.0, out1)
            with dve.Fori(0, 2) as j:
                n.enter(j, 16)
                bl.enter(j, 2)
                for b in range(2):
                    consume(8)
                    dve.wait_ge(chunk_used, n.at())
                    add_block(bass.ds(j * 1024 + b * 512, 512))
                n.leave(2)
                bl.leave(2)
            h_done()
            norm_rows(h, hs[:, 1, :])
            for t in range(TT):
                dve.tensor_scalar(hs[:, t, :], h[:, t, :], rstd[:, t:t + 1], None, ALU.mult).then_inc(n_rows, 1)
            dve.wait_ge(rt_e, 1)
            dve.tensor_tensor(rt_lo[:, :], rt_raw[:, :], rt_hi[:, :], ALU.subtract).then_inc(rt_split, 1)
            dve.wait_ge(rt_e, 2)
            dve.tensor_tensor(pT_l[:, :, :], pT[:, :, :], pT_h[:, :, :], ALU.subtract).then_inc(pT_ready, 1)
            norm_parts(xh, xl)
            dve.wait_ge(moe_in, 80)
            own(dve.tensor_copy(ident_b[:, :], ident[:, :]))
            own(dve.tensor_copy(tri_b[:, :], tri[:, :]))
            for t in range(TT):
                dve.wait_ge(xa_ready, t + 1)
                dve.tensor_tensor(xs[:, t, :], xs[:, t, :], xb[:, 0, t, :], ALU.subtract).then_inc(xr_ready, 1)
            dve.wait_ge(rt_tp, 1)
            lg_ps = ps[1][:, 0:S].rearrange("p (t n) -> p t n", t=TT)[:, :, 0:N_ROUTER]
            dve.tensor_copy(lg[:, :, :], lg_ps).then_inc(rt_read, 1)
            dve.wait_ge(rt_read, 1)

            def per(k, like):
                return r_s[:, k, :].unsqueeze(2).to_broadcast(like)

            def first_max(dst, k, x, keys, order, count):
                own(dve.tensor_reduce(r_s[:, k, :], x, AX_X, ALU.max))
                mine()
                own(dve.tensor_tensor(keys, x, per(k, [P, TT, count]), ALU.is_equal))
                mine()
                own(dve.tensor_tensor(keys, keys, order, ALU.mult))
                mine()
                own(dve.tensor_reduce(r_s[:, k + 1, :], keys, AX_X, ALU.max))
                mine()
                own(dve.tensor_tensor(dst, keys, per(k + 1, [P, TT, count]), ALU.is_equal))
                mine()

            gl = lg[:, :, 0:N_GROUPS]
            first_max(g_oh[:, :, :], 0, gl, g_key[:, :, :], desc4[:, :, :], N_GROUPS)
            dve.tensor_tensor(g_sh[:, :, :], gl, per(0, [P, TT, N_GROUPS]), ALU.subtract).then_inc(rt_read, 1)
            own(dve.tensor_scalar(g_key[:, :, :], g_oh[:, :, :], -NEG, NEG, ALU.mult, ALU.add))
            mine()
            for t in range(TT):
                e3 = lambda x: x[:, t, :].rearrange("p (g e) -> p g e", g=N_GROUPS)
                wide = lambda x: x[:, t, :].unsqueeze(2).to_broadcast([P, N_GROUPS, PER_GROUP])
                own(dve.tensor_tensor(e3(em), lg[:, t, N_GROUPS:N_ROUTER].rearrange("p (g e) -> p g e", g=N_GROUPS),
                                      wide(g_oh), ALU.mult))
                mine()
                own(dve.tensor_tensor(e3(em), e3(em), wide(g_key), ALU.add))
            mine()
            first_max(oh1[:, :, :], 2, em[:, :, :], key[:, :, :], desc[:, :, :], N_EXPERTS)
            own(dve.scalar_tensor_tensor(em[:, :, :], oh1[:, :, :], -3e38, em[:, :, :], ALU.mult, ALU.add))
            mine()
            first_max(oh2[:, :, :], 4, em[:, :, :], key[:, :, :], desc[:, :, :], N_EXPERTS)
            dve.tensor_tensor(r_s[:, 6, :], r_s[:, 4, :], r_s[:, 2, :], ALU.subtract).then_inc(rt_read, 1)
            own(dve.tensor_tensor(taken[:, :, :], oh1[:, :, :], oh2[:, :, :], ALU.add))
            mine()
            dve.sem_inc(taken_ready, 1)
            dve.wait_ge(rt_e, 4)
            own(dve.tensor_reduce(r_s[:, 8, :], g_e[:, :, :], AX_X, ALU.add))
            own(dve.tensor_scalar(r_s[:, 9, :], r_s[:, 7, :], 1.0, None, ALU.add))
            mine()
            own(dve.tensor_tensor(r_s[:, 9, :], r_s[:, 9, :], r_s[:, 8, :], ALU.mult))
            mine()
            own(dve.reciprocal(r_s[:, 10, :], r_s[:, 9, :]))
            mine()
            own(dve.tensor_tensor(r_s[:, 11, :], r_s[:, 10, :], r_s[:, 7, :], ALU.mult))
            mine()
            own(dve.tensor_tensor(comb[:, :, :], oh1[:, :, :], per(10, [P, TT, N_EXPERTS]), ALU.mult))
            own(dve.tensor_tensor(key[:, :, :], oh2[:, :, :], per(11, [P, TT, N_EXPERTS]), ALU.mult))
            mine()
            own(dve.tensor_tensor(comb[:, :, :], comb[:, :, :], key[:, :, :], ALU.add))
            mine()

            consume(4)
            dve.wait_ge(chunk_used, n.n)
            bl.n += 4
            dve.wait_ge(rank_mm, 1)
            rank = ps[0][:, 0:64].rearrange("p (t e) -> p t e", t=TT)
            own(dve.scalar_tensor_tensor(pos[:, :, :], rank, 1.0, taken[:, :, :], ALU.add, ALU.mult))
            own(dve.tensor_scalar(combo[:, :, :], rank, float(SLOTS), None, ALU.is_ge))
            own(dve.tensor_copy(over[:, 0, :], ps[0][:, 64:96]))
            mine()
            own(dve.tensor_scalar(pos[:, :, :], pos[:, :, :], -1.0, None, ALU.add))
            own(dve.tensor_tensor(combo[:, :, :], combo[:, :, :], comb[:, :, :], ALU.mult))
            own(dve.tensor_copy(c3[:, 0, :, :], comb[:, :, :]))
            mine()
            for t in range(TT):
                own(dve.tensor_tensor(G[:, t, :].rearrange("p (e s) -> p e s", e=N_EXPERTS),
                                      pos[:, t, :].unsqueeze(2).to_broadcast([P, N_EXPERTS, SLOTS]),
                                      iota[:, :].unsqueeze(1).to_broadcast([P, N_EXPERTS, SLOTS]), ALU.is_equal))
            own(dve.tensor_tensor(c_rest[:, :, :], comb[:, :, :], c3[:, 0, :, :], ALU.subtract))
            mine()
            own(dve.tensor_copy(c3[:, 1, :, :], c_rest[:, :, :]))
            mine()
            own(dve.tensor_tensor(c3[:, 2, :, :], c_rest[:, :, :], c3[:, 1, :, :], ALU.subtract))
            dve.wait_ge(xc_ready, TT)
            own(dve.memset(hid[:, :, :], 0.0))
            mine()
            dve.sem_inc(slots_ready, 1)
            own(dve.tensor_scalar(over[:, 1, :], over[:, 0, :], float(SLOTS), None, ALU.is_gt))
            own(dve.memset(over[:, 3, :], 1.0))
            mine()
            own(dve.tensor_tensor_scan(over[:, 2, :], over[:, 3, :], over[:, 1, :], 0.0, ALU.mult, ALU.add))
            mine()
            own(dve.tensor_tensor(over[:, 3, :], over[:, 2, :], over[:, 1, :], ALU.mult))
            own(dve.tensor_copy(over_f[:, 0:1], over[:, 2, N_EXPERTS - 1:N_EXPERTS]))
            mine()
            own(dve.tensor_scalar(over[:, 3, :], over[:, 3, :], -1.0, None, ALU.add))
            mine()
            wide = [P, MAX_OVER + 1, N_EXPERTS]
            own(dve.tensor_tensor(over_eq[:, :, :], over[:, 3, :].unsqueeze(1).to_broadcast(wide),
                                  iota[:, 0:MAX_OVER + 1].unsqueeze(2).to_broadcast(wide), ALU.is_equal))
            mine()
            own(dve.tensor_tensor(over_eq[:, :, :], over_eq[:, :, :], iota[:, 0:N_EXPERTS].unsqueeze(1).to_broadcast(wide), ALU.mult))
            mine()
            own(dve.tensor_reduce(over_f[:, 1:MAX_OVER + 2], over_eq[:, :, :], AX_X, ALU.add))
            mine()
            dve.tensor_copy(over_i[:, :], over_f[:, :]).then_inc(ov_list, 1)

            tu, th, hv = Count(), Count(), Count()

            def read_low(dst, hi):
                dve.wait_ge(t_hi, th.at(1))
                o = dve.tensor_tensor(dst, tp[tu.n % 2][:, 0:dst.shape[-1]], hi, ALU.subtract)
                tu.n += 1
                th.n += 1
                return o

            def gathered(k):
                cs = slice(k * 512, k * 512 + 512)
                read_low(xg_l[:, cs], xg_h[:, cs]).then_inc(t_read, 1)

            def scattered(k):
                dve.wait_ge(t_done, tu.at(1))
                hh = h[:, k % 2, k // 2 * 512:k // 2 * 512 + 512]
                dve.tensor_tensor(hh, tp[tu.n % 2][:, :], hh, ALU.add).then_inc(t_read, 1)
                tu.n += 1

            def transposed(q):
                o = read_low(hid_l[:, q, :], hid_h[:, q, :])
                if q == 0:
                    o.then_inc(hid_lo, 1)
                    dve.tensor_copy(GT[:, :], tp[(tu.n - 1) % 2][:, S:2 * S]).then_inc(t_read, 1)
                else:
                    o.then_inc(t_read, 1)
                    dve.wait_ge(t_read, tu.at())
                    dve.sem_inc(hid_lo, 1)

            def slot_weights():
                dve.wait_ge(t_done, tu.at(1))
                o = tp[tu.n % 2][:, 0:2 * PAIRS].rearrange("p (g q) -> p g q", q=2)
                tu.n += 1
                for q in range(2):
                    r = pair_rows(q)
                    own(dve.tensor_copy(w_slot[r, :].unsqueeze(2), o[r, :, q:q + 1]))
                mine()
                dve.sem_inc(t_read, 1)

            def pair(g, first=False, last=False):
                for c in range(2 * GU + 2 * DN):
                    consume(1)
                    if c == 2 * GU - 2:
                        w = w_slot[:, g:g + 1] if isinstance(g, int) else w_slot[:, bass.ds(g, 1)]
                        dve.tensor_copy(w_now[:, :], w).then_inc(w_ready, 1)
                    if c in (GU, 2 * GU):
                        q = c // GU - 1
                        r = pair_rows(q)
                        dve.wait_ge(silu_ready, hv.at(q + 1))
                        dve.tensor_tensor(hid[r, q, :], sg[r, q, :], ps[q][r, 256:512], ALU.mult).then_inc(hid_ready, 1)
                    for step, k in steps_after(c, first, last):
                        {"gather": gathered, "scatter": scattered, "transpose": transposed,
                         "weights": lambda _: slot_weights()}[step](k)
                    if c in (2 * GU + DN + 1, 2 * GU + 2 * DN - 1):
                        b = (c - 2 * GU - DN) // 2
                        dve.wait_ge(y_hi, hv.at(b + 1))
                        dve.wait_ge(w_ready, hv.at(2, 2))
                        cs = slice(b * 1024, (b + 1) * 1024)
                        dve.scalar_tensor_tensor(yl[:, cs], acc[b][:, :], w_now[:, :], yh[:, cs], ALU.mult,
                                                 ALU.subtract).then_inc(y_ready, 1)
                hv.n += 2

            for k in range(4):
                gathered(k)
            pair(0, first=True)
            with dve.Fori(1, PAIRS - 1) as i:
                for c, k in ((n, 24), (tu, 14), (th, 6), (hv, 2)):
                    c.enter(i, k, 1)
                pair(i)
                for c in (n, tu, th, hv):
                    c.leave(PAIRS - 2)
            pair(PAIRS - 1, last=True)
            for k in range(8):
                scattered(k)
            dve.wait_ge(t_read, USES)
            dve.wait_ge(ov_list, 1)
            count = dve.value_load(over_i[0:1, 0:1], min_val=0, max_val=MAX_OVER)
            with dve.If(count > 0):
                with dve.Fori(0, count) as i:
                    ex = dve.value_load(over_i[0:1, bass.ds(i + 1, 1)], min_val=0, max_val=N_EXPERTS - 1)
                    dve.wait_ge(ov_pe, i * OV_PE + (OV_X + 2))
                    dve.wait_ge(ov_act, i * OV_ACT + (OV_X + 1))
                    dve.tensor_tensor(hid.rearrange("p a b -> p (a b)"), sg.rearrange("p a b -> p (a b)"), ps[1][:, :],
                                      ALU.mult).then_inc(ov_dve, 1)
                    for k in range(8):
                        dve.wait_ge(ov_pe, i * OV_PE + (OV_X + 3 + k))
                        hh = h[:, k % 2, k // 2 * 512:k // 2 * 512 + 512]
                        dve.scalar_tensor_tensor(hh, acc[0][:, k % 2 * 512:k % 2 * 512 + 512], combo[:, k % 2, bass.ds(ex, 1)], hh,
                                                 ALU.mult, ALU.add).then_inc(ov_dve, 1)
                    dve.wait_ge(ov_dve, i * OV_DVE + OV_DVE)
            h_done()
            norm_rows(h, hs[:, 1, :])
            norm_parts(xh, xl)
            h_done()
            gt = Count()
            with dve.Fori(0, 2) as j:
                n.enter(j, 16)
                bl.enter(j, 2)
                gt.enter(j, 2)
                for b in range(2):
                    consume(8)
                    dve.wait_ge(gate_ready, gt.at(1))
                    gt.n += 1
                    cols = bass.ds(j * 1024 + b * 512, 512)
                    g3 = gate[:, b, :].rearrange("p (t n) -> p t n", t=TT)
                    dve.tensor_tensor(g3, g3, upb[:, :, cols], ALU.mult).then_inc(ple_prod, 1)
                    dve.wait_ge(ple_prod, gt.at())
                    hh = h[:, :, cols]
                    dve.tensor_tensor(hh, hh, g3, ALU.add).then_inc(acc_free[bl.n % 2], 1)
                    bl.n += 1
                for c in (n, bl, gt):
                    c.leave(2)
            assert (bl.n + 1) // 2 == PLE_END[0] and bl.n // 2 == PLE_END[1], bl.n
            h_done()
            norm_rows(h, hs[:, 1, :])
            norm_parts(xh, xl)
            with dve.Fori(0, 4) as j:
                n.enter(j, 16)
                bl.enter(j, 2)
                for b in range(2):
                    consume(8)
                    dve.wait_ge(chunk_used, n.at())
                    dve.tensor_copy(qk2[:, bass.ds(j * 8 + 4 * b, 4), :], acc[bl.n % 2][:, :].rearrange("p (a b) -> p a b", a=4))\
                       .then_inc(acc_free[bl.n % 2], 1)
                    bl.n += 1
                n.leave(4)
                bl.leave(4)
            with dve.Fori(0, 2) as j:
                n.enter(j, 16)
                bl.enter(j, 2)
                for b in range(2):
                    consume(8)
                    dve.wait_ge(chunk_used, n.at())
                    dve.tensor_copy(v2[:, :, bass.ds(j * 1024 + b * 512, 512)],
                                    acc[bl.n % 2][:, :].rearrange("p (t n) -> p t n", t=TT)).then_inc(acc_free[bl.n % 2], 1)
                    bl.n += 1
                n.leave(2)
                bl.leave(2)

            def out2(u):
                if u < N_DIFF:
                    dve.wait_ge(o_mm, HEADS1 + u + 1)
                    dve.tensor_copy(qk2[:, u, :], ps[u % 2][:, 0:S]).then_inc(o_lo, 1)
                else:
                    dve.wait_ge(o_hi, HEADS1 + u - N_DIFF + 1)
                    dve.tensor_tensor(xl[:, u, :], ps[u % 2][:, 0:S], xh[:, u, :], ALU.subtract).then_inc(o_lo, 1)

            dve.wait_ge(b_copy, 8)
            attend(1, lambda u: bias[:, u, :], lambda u: DIFF_SCALE if u < N_DIFF else HEAD_SCALE, out2)
            for g in range(N_DIFF // 2):
                dve.wait_ge(ms_root, 8 + g + 1)
                own(dve.reciprocal(rst2[:, g % 2, :], rst2[:, g % 2, :]))
                mine()
                two_h = qk2[:, 2 * g:2 * g + 2, :].rearrange("p a b -> p (a b)")
                dve.scalar_tensor_tensor(two_h, two_h, qg[:, 1:2], rst2[:, g % 2, :], ALU.mult, ALU.mult).then_inc(qk_ready, 1)
            dve.wait_ge(rnn_hi, 2)
            dve.tensor_tensor(xl[:, 0:N_DIFF, :], qk2[:, 0:N_DIFF, :], xh[:, 0:N_DIFF, :], ALU.subtract).then_inc(rnn_lo, 1)

            def add_one(b):
                consume(8)
                dve.wait_ge(chunk_used, n.n)
                add_block(slice(b * 512, b * 512 + 512))

            add_one(0)
            dve.wait_ge(mem_in, 32)
            norm_rows(mem, junk_v[:, :])
            add_one(1)
            norm_parts(memh, meml)
            add_one(2)
            add_one(3)
            h_done()
            norm_rows(h, junk_c[:, 1, :])
            consume(8)
            dve.wait_ge(chunk_used, n.n)
            dve.tensor_copy(km[:, :, :].rearrange("p a b -> p (a b)"), acc[bl.n % 2][:, :]).then_inc(acc_free[bl.n % 2], 1)
            bl.n += 1
            consume(8)
            dve.wait_ge(chunk_used, n.n)
            dve.tensor_copy(vm[:, :, :], acc[bl.n % 2][:, :].rearrange("p (t n) -> p t n", t=TT)).then_inc(acc_free[bl.n % 2], 1)
            bl.n += 1
            norm_parts(xh, xl)
            own(dve.memset(zero[:, :], 0.0))
            mine()
            consume(8)
            dve.wait_ge(chunk_used, n.n)
            dve.tensor_copy(qc[:, :, :].rearrange("p a b -> p (a b)"), acc[bl.n % 2][:, :]).then_inc(acc_free[bl.n % 2], 1)
            bl.n += 1

            def out3(u):
                dve.wait_ge(o_hi, HEADS1 + N_SELF - N_DIFF + u + 1)
                dve.tensor_tensor(xl[:, u, :], ps[u % 2][:, 0:S], xh[:, u, :], ALU.subtract).then_inc(o_lo, 1)

            attend(2, lambda u: zero, lambda u: HEAD_SCALE, out3)
            for b in range(4):
                consume(2)
                dve.wait_ge(chunk_used, n.n)
                add_block(slice(b * 512, b * 512 + 512))
            h_done()
            norm_rows(h, hs[:, 1, :])
            norm_parts(xh, xl)
            own(dve.memset(gpad[:, :, 0:2], 0.0))
            mine()
            ff = Count()
            cs = Count()

            def hidden2(t0, hi, lo):
                consume(8)
                dve.wait_ge(g_ready, ff.at(1))

                def tap(k, t):
                    c = V_CONV2 + k * FF_T
                    if isinstance(t0, int):
                        return vec[:, c + t0 + t:c + t0 + t + 1]
                    return vec[:, bass.ds(t0 + (c + t), 1)]

                if ff.i is not None or ff.n:
                    dve.wait_ge(af_ready, ff.at())
                for t in range(2):
                    dve.tensor_scalar(cv[:, t, :], gpad[:, t, 2:2 + S], tap(2, t), tap(3, t), ALU.mult, ALU.add).then_inc(conv2, 1)
                    cs.n += 1
                for k in (1, 0):
                    dve.wait_ge(conv2, cs.at())
                    for t in range(2):
                        o = dve.scalar_tensor_tensor(cv[:, t, :], gpad[:, t, k:k + S], tap(k, t), cv[:, t, :], ALU.mult, ALU.add)
                        if k:
                            o.then_inc(conv2, 1)
                            cs.n += 1
                o.then_inc(cv_ready, 1)
                dve.wait_ge(sil2, ff.at(1))
                if ff.i is not None or ff.n:
                    dve.wait_ge(a_hi, ff.at())
                    dve.wait_ge(a_lo, ff.at())
                dve.tensor_tensor(af[:, :, :], cv[:, :, :], acc[bl.n % 2][:, 512:1024].rearrange("p (a b) -> p a b", a=2),
                                  ALU.mult).then_inc(af_ready, 1)
                dve.wait_ge(a_hi, ff.at(1))
                dve.tensor_tensor(lo, af[:, :, :], hi, ALU.subtract).then_inc(a_lo, 1)
                dve.sem_inc(acc_free[bl.n % 2], 1)
                bl.n += 1
                ff.n += 1

            for t in (0, 2):
                hidden2(t, ah[:, t:t + 2, :], al[:, t:t + 2, :])
            with dve.Fori(1, FF_T // 4 - 1) as j:
                for c, k in ((n, 16), (bl, 2), (ff, 2), (cs, 8)):
                    c.enter(j, k, 1)
                for b in range(2):
                    t4 = bass.ds(j * 4 + 2 * b, 2)
                    hidden2(j * 4 + 2 * b, ah[:, t4, :], al[:, t4, :])
                for c in (n, bl, ff, cs):
                    c.leave(FF_T // 4 - 2)
            hidden2(FA - 2, ah[:, FA - 2:FA, :], al[:, FA - 2:FA, :])
            hidden2(FA, xh[:, 0:2, :], xl[:, 0:2, :])
            for b in range(4):
                consume(FF_T // 2)
                dve.wait_ge(chunk_used, n.n)
                add_block(slice(b * 512, b * 512 + 512))
            h_done()
            norm_rows(h, hs[:, 1, :], last=True)
            dve.wait_ge(n_inv, 8)
            dve.wait_ge(gf_in, 16)
            for t in range(TT):
                dve.scalar_tensor_tensor(h[:, t, :], h[:, t, :], rstd[:, t:t + 1], gfin[:, :], ALU.mult, ALU.mult)\
                   .then_inc(fin_ready, 1)


LAM_INIT = 0.8 - 0.6 * math.exp(-0.3 * 0)
_BLOCKS = 10 + 4 + 4 + 4
PLE_END = ((_BLOCKS + 1) // 2, _BLOCKS // 2)


def _bucket(d):
    if d < 16:
        return max(d, 0)
    return min(16 + int(math.log(d / 16) / math.log(2048 / 16) * 16), 31)


def _constants():
    c = {}
    c["ident"] = np.eye(P, dtype=np.float32)
    c["flip"] = np.ascontiguousarray(np.eye(P, dtype=np.float32)[::-1])
    q, j = np.arange(P)[:, None], np.arange(S)[None, :]
    c["causal"] = np.where(j - P > q, np.float32(NEG), np.float32(0)).astype(np.float32)
    neg = np.zeros((P, HEADS1, P), np.float32)
    for u in range(HEADS1):
        neg[u, u, :] = -1.0
    c["negsel"] = neg
    dist = 255 - np.arange(384)
    onehot = np.zeros((32, 384), np.float32)
    for m, d in enumerate(dist):
        onehot[_bucket(int(d)), m] = 1.0
    c["onehot"] = onehot
    scale = np.array([DIFF_SCALE] * N_DIFF + [HEAD_SCALE] * (N_MOBA + N_DIL), np.float64)
    c["iscale"] = (1.0 / scale).astype(np.float32)[:, None]
    addend = np.zeros((N_SELF, 384), np.float64)
    branches = (dist <= 128).astype(int) + (dist % 4 == 0) + (dist % 16 == 0)
    addend[N_DIFF + N_MOBA:] = np.where(branches > 0, np.log(np.maximum(branches, 1)), NEG) / HEAD_SCALE
    addend[:, dist < 0] = NEG
    c["addend"] = np.maximum(addend, NEG).astype(np.float32)
    c["desc"] = np.broadcast_to(np.arange(N_EXPERTS, 0, -1, dtype=np.float32), (P, TT, N_EXPERTS))
    c["desc4"] = np.broadcast_to(np.arange(N_GROUPS, 0, -1, dtype=np.float32), (P, TT, N_GROUPS))
    q, j = np.arange(P)[:, None], np.arange(P)[None, :]
    c["tri"] = (q < j).astype(np.float32)
    c["iota"] = np.broadcast_to(np.arange(SLOTS, dtype=np.float32), (P, SLOTS))
    return c


_WHOLE = ["x", "ffn_norm", "w_in", "w_rec_gate", "w_in_gate", "w_out", "w_expert_gate", "w_expert_up", "w_expert_down", "w_ple_gate",
          "w_ple_up", "mem_2", "w_in_2", "w_out_2", "diff_lambda_2", "rel_bias_table_2", "w_cq_2", "w_ckv_2", "w_co_2",
          "w_up_2", "w_down_2", "g_final_2"]


def kernel(**inputs):
    import numpy as _np
    import concourse.bacc as _bacc
    from concourse import mybir as _mybir
    from concourse.bass_utils import run_bass_kernel_spmd as _run

    a = {k: _np.asarray(v) for k, v in inputs.items()}
    arrays = {name: _np.ascontiguousarray(a[name]) for name in _WHOLE}

    def tiles(x):
        return x.reshape(-1, P).T

    forget = _np.zeros((P, 1), _np.float32)
    forget[:HEADS1, 0] = a["b_forget"][0]
    arrays["vec"] = _np.concatenate(
        [tiles(a[k]) for k in ("mix_norm", "ffn_norm", "ple_norm", "g_mix_2", "g_mem_2", "g_cross_2", "g_ffn_2",
                               "conv_w", "conv_b", "b_rec_gate", "b_in_gate", "lru_lambda", "q_norm", "k_norm",
                               "diff_subln_2")] + [forget] + [tiles(a["conv_w_2"]), tiles(a["conv_b_2"])], axis=1)

    def rows(x):
        return x.reshape(KT, P, -1).transpose(1, 0, 2).reshape(P, -1)

    arrays["w_f"] = rows(a["w_in"][0][:, COL_F:COL_F + HEADS1])
    arrays["w_router"] = rows(_np.concatenate([a["w_router_group"][0], a["w_router_expert"][0]], axis=1))
    arrays["pT"] = a["p"][0, 0].T.reshape(2, P, S).transpose(1, 0, 2)
    arrays.update(_constants())
    arrays = {k: _np.ascontiguousarray(v) for k, v in arrays.items()}

    nc = _bacc.Bacc("TRN2", target_bir_lowering=False, num_devices=1)
    aps = {k: nc.dram_tensor(f"in_{k}", v.shape, _mybir.dt.from_np(v.dtype), kind="ExternalInput").ap()
           for k, v in arrays.items()}
    out = nc.dram_tensor("out_0", (1, S, D), _mybir.dt.from_np(_np.dtype("float32")), kind="ExternalOutput").ap()
    program(nc, aps, out)
    r = _run(nc, [{f"in_{k}": v for k, v in arrays.items()}], core_ids=[0])
    return r.results[0]["out_0"]
```
